# Optimizing a Trainium2 kernel written in Bass

```python
import jax, jax.numpy as jnp
from jax import lax
import numpy as np

D_MODEL = 2048
BATCH = 1
SEQ = 1024
DEPTH = 1

FOX_HEADS = 8
FOX_HEAD_DIM = 128
FOX_WIDTH = FOX_HEADS * FOX_HEAD_DIM
SWA_Q_HEADS = 16
SWA_KV_HEADS = 4
SWA_HEAD_DIM = 64
SWA_GROUP = SWA_Q_HEADS // SWA_KV_HEADS
SWA_WIDTH = SWA_Q_HEADS * SWA_HEAD_DIM
SWA_KV_WIDTH = SWA_KV_HEADS * SWA_HEAD_DIM
WINDOW = 128
Q_BLOCK = 128
LN_EPS = 1e-5
NEG_INF = -1e30
DEEPNORM_ALPHA = (2.0 * DEPTH) ** 0.25
DEEPNORM_BETA = (8.0 * DEPTH) ** -0.25

_SPLIT_SIZES = (FOX_WIDTH, FOX_WIDTH, FOX_WIDTH, FOX_HEADS,
                SWA_WIDTH, SWA_KV_WIDTH, SWA_KV_WIDTH,
                FOX_WIDTH, SWA_WIDTH,
                D_MODEL, D_MODEL)
IN_WIDTH = sum(_SPLIT_SIZES)
SPLIT_IDX = tuple(int(v) for v in np.cumsum(_SPLIT_SIZES)[:-1])

kernel_name = "hybrid_fox_swa_gated_deepnorm_adaln"

def _layer_norm(x):
    xf = x.astype(jnp.float32)
    mu = jnp.mean(xf, axis=-1, keepdims=True)
    var = jnp.mean(jnp.square(xf - mu), axis=-1, keepdims=True)
    return ((xf - mu) * lax.rsqrt(var + LN_EPS)).astype(x.dtype)

def _forgetting_attention(q, k, v, fgate_logit, b_f):
    B, S, H, Dh = q.shape
    log_f = jax.nn.log_sigmoid(fgate_logit.astype(jnp.float32) + b_f.astype(jnp.float32))
    cum = jnp.cumsum(log_f, axis=1)
    cum_k = cum.transpose(0, 2, 1)[:, :, None, :]
    nb = S // Q_BLOCK
    qb = q.reshape(B, nb, Q_BLOCK, H, Dh).transpose(1, 0, 2, 3, 4)
    cqb = cum.reshape(B, nb, Q_BLOCK, H).transpose(1, 0, 2, 3)
    qpos = jnp.arange(S, dtype=jnp.int32).reshape(nb, Q_BLOCK)
    kpos = jnp.arange(S, dtype=jnp.int32)
    scale = Dh ** -0.5

    def block(args):
        qi, ci, pi = args
        s = jnp.einsum('bqhd,bkhd->bhqk', qi, k).astype(jnp.float32) * scale
        s = s + ci.transpose(0, 2, 1)[..., None] - cum_k
        mask = kpos[None, :] <= pi[:, None]
        s = jnp.where(mask[None, None], s, NEG_INF)
        p = jax.nn.softmax(s, axis=-1).astype(v.dtype)
        return jnp.einsum('bhqk,bkhd->bqhd', p, v)

    out = lax.map(block, (qb, cqb, qpos))
    return out.transpose(1, 0, 2, 3, 4).reshape(B, S, H * Dh)

def _sliding_window_attention(q, k, v, sinks):
    B, S, HQ, d = q.shape
    nb = S // WINDOW
    qb = q.reshape(B, nb, WINDOW, SWA_KV_HEADS, SWA_GROUP, d)
    kb = k.reshape(B, nb, WINDOW, SWA_KV_HEADS, d)
    vb = v.reshape(B, nb, WINDOW, SWA_KV_HEADS, d)
    pad = ((0, 0), (1, 0), (0, 0), (0, 0), (0, 0))
    kk = jnp.concatenate([jnp.pad(kb, pad)[:, :-1], kb], axis=2)
    vv = jnp.concatenate([jnp.pad(vb, pad)[:, :-1], vb], axis=2)
    s = jnp.einsum('bnqhgd,bnkhd->bnhgqk', qb, kk).astype(jnp.float32) * (d ** -0.5)
    i = jnp.arange(WINDOW, dtype=jnp.int32)[:, None]
    j = jnp.arange(2 * WINDOW, dtype=jnp.int32)[None, :]
    dist = (i - j + WINDOW)
    n = jnp.arange(nb, dtype=jnp.int32)[:, None, None]
    kpos_abs = n * WINDOW - WINDOW + j[None]
    valid = (dist[None] >= 0) & (dist[None] < WINDOW) & (kpos_abs >= 0)
    slopes = 2.0 ** (-8.0 * (jnp.arange(HQ, dtype=jnp.float32) + 1.0) / HQ)
    slopes = slopes.reshape(SWA_KV_HEADS, SWA_GROUP)
    s = s - slopes[:, :, None, None] * dist.astype(jnp.float32)
    s = jnp.where(valid[None, :, None, None], s, NEG_INF)
    sink = jnp.broadcast_to(sinks.astype(jnp.float32).reshape(SWA_KV_HEADS, SWA_GROUP)[:, :, None, None],
                            s.shape[:-1] + (1,))
    p = jax.nn.softmax(jnp.concatenate([s, sink], axis=-1), axis=-1)[..., :-1].astype(v.dtype)
    out = jnp.einsum('bnhgqk,bnkhd->bnqhgd', p, vv)
    return out.reshape(B, S, HQ * d)

def setup_inputs(seed: int = 0) -> dict:
    key = jax.random.key(seed)
    ks = jax.random.split(key, 13)
    f32 = jnp.float32
    nrm = lambda k, shape, s: jax.random.normal(k, shape, f32) * s
    x = nrm(ks[0], (BATCH, SEQ, D_MODEL), 1.0)
    c = nrm(ks[1], (BATCH, D_MODEL), 1.0)
    w_ada = nrm(ks[2], (DEPTH, D_MODEL, 3 * D_MODEL), 0.5 * D_MODEL ** -0.5)
    b_ada = nrm(ks[3], (DEPTH, 3 * D_MODEL), 0.02)
    w_in = nrm(ks[4], (DEPTH, D_MODEL, IN_WIDTH), D_MODEL ** -0.5)
    b_f = jnp.linspace(2.0, 7.0, FOX_HEADS, dtype=f32)[None, :] + nrm(ks[5], (DEPTH, FOX_HEADS), 0.1)
    attn_sinks = nrm(ks[6], (DEPTH, SWA_Q_HEADS), 1.0)
    w_br_fox = nrm(ks[7], (DEPTH, FOX_WIDTH, D_MODEL), DEEPNORM_BETA * FOX_WIDTH ** -0.5)
    w_br_swa = nrm(ks[8], (DEPTH, SWA_WIDTH, D_MODEL), DEEPNORM_BETA * SWA_WIDTH ** -0.5)
    w_out = nrm(ks[9], (DEPTH, D_MODEL, D_MODEL), DEEPNORM_BETA * D_MODEL ** -0.5)
    ln_g = 1.0 + nrm(ks[10], (DEPTH, D_MODEL), 0.02)
    ln_b = nrm(ks[11], (DEPTH, D_MODEL), 0.02)
    return {"x": x, "c": c, "w_ada": w_ada, "b_ada": b_ada, "w_in": w_in, "b_f": b_f,
            "attn_sinks": attn_sinks, "w_br_fox": w_br_fox, "w_br_swa": w_br_swa,
            "w_out": w_out, "ln_g": ln_g, "ln_b": ln_b}

def reference(x, c, w_ada, b_ada, w_in, b_f, attn_sinks, w_br_fox, w_br_swa, w_out, ln_g, ln_b):
    B, S, D = x.shape
    for l in range(DEPTH):
        ada = c @ w_ada[l] + b_ada[l]
        shift, scale, gate = jnp.split(ada, 3, axis=-1)
        h = _layer_norm(x) * (1.0 + scale[:, None, :]) + shift[:, None, :]
        proj = h @ w_in[l]
        (fq, fk, fv, flog, sq, sk, sv, g_fox, g_swa, m_fox, m_swa) = jnp.split(proj, SPLIT_IDX, axis=-1)
        o_fox = _forgetting_attention(fq.reshape(B, S, FOX_HEADS, FOX_HEAD_DIM),
                                      fk.reshape(B, S, FOX_HEADS, FOX_HEAD_DIM),
                                      fv.reshape(B, S, FOX_HEADS, FOX_HEAD_DIM),
                                      flog, b_f[l])
        o_swa = _sliding_window_attention(sq.reshape(B, S, SWA_Q_HEADS, SWA_HEAD_DIM),
                                          sk.reshape(B, S, SWA_KV_HEADS, SWA_HEAD_DIM),
                                          sv.reshape(B, S, SWA_KV_HEADS, SWA_HEAD_DIM),
                                          attn_sinks[l])
        y_fox = (o_fox * jax.nn.silu(g_fox)) @ w_br_fox[l]
        y_swa = (o_swa * jax.nn.silu(g_swa)) @ w_br_swa[l]
        merged = jax.nn.sigmoid(m_fox) * y_fox + jax.nn.sigmoid(m_swa) * y_swa
        sub = merged @ w_out[l]
        z = DEEPNORM_ALPHA * x + gate[:, None, :] * sub
        x = _layer_norm(z) * ln_g[l] + ln_b[l]
    return x


_drawn_inputs = setup_inputs


def setup_inputs(seed=0):
    import zlib

    import numpy as np

    out = dict(_drawn_inputs(seed))
    spreads = {}
    factors = {'b_ada': 8.0, 'b_f': 29.96, 'attn_sinks': 24.304, 'ln_g': 8.201, 'ln_b': 8.327}
    for name, (base, spread) in spreads.items():
        noise = np.random.default_rng([zlib.crc32(name.encode()), seed]).standard_normal(out[name].shape)
        drawn = base * np.exp(spread * noise) if base else spread * noise
        out[name] = __import__('jax').numpy.asarray(drawn.astype(out[name].dtype))
    for name, factor in factors.items():
        out[name] = (out[name] * factor).astype(out[name].dtype)
    return out
```

```python
from contextlib import ExitStack

import concourse.bass as bass
from concourse import mybir

F32 = mybir.dt.float32
F32R = mybir.dt.float32r
ALU = mybir.AluOpType
ACT = mybir.ActivationFunctionType
AX = mybir.AxisListType
ds = bass.ds

P = 128
D = 2048
SEQ = 1024
HALF = 512
KD = D // P
FOX_HEADS = 8
FOX_WIDTH = 1024
SWA_HEADS = 16
SWA_KV = 4
SWA_D = 64
SWA_WIDTH = 1024
LN_EPS = 1e-5
NEG = -1e30
FAR = 1e34
ALPHA = 2.0 ** 0.25

COL_FLOG = 3 * FOX_WIDTH
COL_REST = COL_FLOG + FOX_HEADS
B_SQ = 1
B_SK = B_SQ + SWA_WIDTH // P
B_SV = B_SK + SWA_KV * SWA_D // P
B_FQ = B_SV + SWA_KV * SWA_D // P
B_FK = B_FQ + FOX_WIDTH // P
B_FV = B_FK + FOX_WIDTH // P
B_G = B_FV + FOX_WIDTH // P
B_M = B_G + (FOX_WIDTH + SWA_WIDTH) // P
BLOCKS = B_M + 2 * D // P
MMS = 48
TAIL = 2 * BLOCKS


class Steps:

    def __init__(self, eng, sem):
        self.eng, self.sem, self.total, self.base, self.n = eng, sem, 0, 0, 0

    def enter(self, before=0):
        self.base, self.n = self.total + before, 0

    def leave(self, steps, times=1, per=None):
        assert self.n == (steps // times if per is None else per), (self.n, steps, times)
        self.total += steps

    def __call__(self, ins):
        self.n += 1
        ins.then_inc(self.sem, 1)
        self.eng.wait_ge(self.sem, self.base + self.n)


def build(nc, x, c, w_ada, b_ada, w_in, b_f, attn_sinks, w_br_fox, w_br_swa, w_out, ln_g, ln_b, out):
    x2 = x.rearrange("a (t p) d -> p (a t) d", p=P)
    out2 = out.rearrange("a (t p) d -> p (a t) d", p=P)
    ada_v = w_ada.rearrange("a (p k) n -> p (a k) n", p=P)
    w_in_v = w_in.rearrange("a (k p) n -> p (a k) n", p=P)
    wbf_v = w_br_fox.rearrange("a (k p) n -> p (a k) n", p=P)
    wbs_v = w_br_swa.rearrange("a (k p) n -> p (a k) n", p=P)
    w_out_v = w_out.rearrange("a (k p) n -> p (a k) n", p=P)

    proj_d = nc.dram_tensor("proj_scratch", (BLOCKS, P, SEQ), F32).ap()
    o_d = nc.dram_tensor("o_scratch", (KD, P, SEQ), F32).ap()
    gate_d = nc.dram_tensor("gate_scratch", (1, D), F32).ap()
    q_heads = proj_d[B_SQ:B_SK].rearrange("b (e d) t -> d (b e) t", d=SWA_D)
    o_heads = o_d[FOX_HEADS:KD].rearrange("b (e d) t -> d (b e) t", d=SWA_D)

    ctx = ExitStack()
    with ctx:
        def sem(name):
            return ctx.enter_context(nc.semaphore(name))

        def psum(name, shape):
            return ctx.enter_context(nc.psum_tensor(name, shape, F32))

        def sb(name, shape, dt=F32, scope=ctx):
            return scope.enter_context(nc.sbuf_tensor(name, shape, dt))

        w_raw = sb("w_raw", [P, 2, 1024])
        w_hi = sb("w_hi", [P, 2, 1024], F32R)
        w_lo = sb("w_lo", [P, 2, 1024], F32R)
        chunk_loaded = [sem("chunk_loaded_0"), sem("chunk_loaded_1")]
        chunk_hi = sem("chunk_hi")
        chunk_lo = sem("chunk_lo")
        chunk_used = sem("chunk_used")
        dve_step = sem("dve_step")
        act_step = sem("act_step")

        def load_chunk(sp, n, slot, source, first=False):
            if not first:
                sp.wait_ge(chunk_lo, n - 1)
            dst = w_raw[:, slot, :].rearrange("p (k n) -> p k n", k=source.shape[1])
            sp.dma_start(dst, source).then_inc(chunk_loaded[slot], 16)

        def split_hi(act, n, slot, loads):
            act.wait_ge(chunk_loaded[slot], 16 * loads)
            if not (isinstance(n, int) and n < 2):
                act.wait_ge(chunk_used, n - 1)
            nc.scalar.copy(w_hi[:, slot, :], w_raw[:, slot, :]).then_inc(chunk_hi, 1)

        def split_lo(dve, n, slot):
            dve.wait_ge(chunk_hi, n + 1)
            nc.vector.tensor_tensor(w_lo[:, slot, :], w_raw[:, slot, :], w_hi[:, slot, :].bitcast(F32),
                                    ALU.subtract).then_inc(chunk_lo, 1)

        main = ExitStack()
        with main:
            psums = ExitStack()
            main.enter_context(psums)

            def pst(name, shape):
                return psums.enter_context(nc.psum_tensor(name, shape, F32))

            projP = pst("projP", [P, 2, HALF])
            sP = pst("sP", [P, 2, HALF])
            tP = pst("tP", [P, 2, HALF])
            oP = pst("oP", [P, HALF])
            adaP = pst("adaP", [P, HALF])

            with ExitStack() as x_scope:
                x_t = sb("x_t", [P, 2, D], F32, x_scope)
            h_hi = sb("h_hi", [P, KD, SEQ], F32R, main)
            lo_scope = ExitStack()
            xnT = sb("xnT", [P, KD, SEQ], F32, lo_scope)
            lo_scope.close()
            h_lo = sb("h_lo", [P, KD, SEQ], F32R, main)
            stage = sb("stage", [P, 2, HALF], F32, main)
            ident = sb("ident", [P, P], F32, main)
            ident_r = sb("ident_r", [P, P], F32R, main)
            mask_r = sb("mask_r", [P, P], F32R, main)
            cum_k = sb("cum_k", [P, SEQ], F32R, main)
            cum_q = sb("cum_q", [P, SEQ], F32R, main)
            head_sel = sb("head_sel", [P, FOX_HEADS], F32, main)
            c_sb = sb("c_sb", [P, KD], F32, main)
            neg_max = sb("neg_max", [P, 4], F32, main)
            row_sum = sb("row_sum", [P, 4], F32, main)
            row_inv = sb("row_inv", [P, 4], F32, main)
            sink_exp = sb("sink_exp", [P, 4], F32, main)

            with ExitStack() as s0:
                ada_raw = sb("ada_raw", [P, 2, KD, 2, P], F32, s0)
                ada_rows = sb("ada_rows", [2 * KD, P], F32, s0)
                ada_b = sb("ada_b", [P, 2, KD], F32, s0)
                ada_s = sb("ada_s", [P, KD, 2], F32, s0)
                bn = sb("bn", [P, 4, 6], F32, s0)
                mv = sb("mv", [P, 2], F32, s0)
                sm = sb("sm", [P, 4], F32, s0)
            with ExitStack() as s1:
                gate_raw = sb("gate_raw", [P, D], F32, s1)
                gate_acc = sb("gate_acc", [P, D], F32, s1)
                fg = [sb(f"fg{i}", [FOX_HEADS, SEQ], F32, s1) for i in range(5)]
                bf_c = sb("bf_c", [FOX_HEADS, 1], F32, s1)
                ones = sb("ones", [P, 1], F32, s1)
            gate_row = gate_raw[0:1, :]
            with ExitStack() as s2:
                sq_raw = sb("sq_raw", [P, 2, 4, P], F32, s2)
                sk_raw = sb("sk_raw", [P, 2, P], F32, s2)
                sv_raw = sb("sv_raw", [P, 2, P], F32, s2)
                sq_hi = sb("sq_hi", [P, 4, P], F32R, s2)
                sq_lo = sb("sq_lo", [P, 4, P], F32R, s2)
                sk_hi = sb("sk_hi", [P, 2, P], F32R, s2)
                sk_lo = sb("sk_lo", [P, 2, P], F32R, s2)
                sv_hi = sb("sv_hi", [P, 2, 2, P], F32R, s2)
                sv_lo = sb("sv_lo", [P, 2, 2, P], F32R, s2)
                s_bias = sb("s_bias", [P, 2, 4, 2, P], F32, s2)
                dist = sb("dist", [P, 2, P], F32, s2)
                no_prev = sb("no_prev", [P, 4], F32, s2)
                sinks = sb("sinks", [P, SWA_HEADS], F32, s2)
                neg_sinks = sb("neg_sinks", [P, SWA_HEADS], F32, s2)
                sp_w = sb("sp_w", [P, 4, 2, P], F32, s2)
                spT_hi = sb("spT_hi", [P, 2, 4 * P], F32R, s2)
                spT_lo = sb("spT_lo", [P, 2, 4 * P], F32R, s2)
                so_st = sb("so_st", [P, 4, P], F32, s2)
            with ExitStack() as s3:
                fq_raw = sb("fq_raw", [P, 2, P], F32, s3)
                fk_raw = sb("fk_raw", [P, SEQ], F32, s3)
                fv_raw = sb("fv_raw", [P, SEQ], F32, s3)
                fq_hi = sb("fq_hi", [P, P], F32R, s3)
                fq_lo = sb("fq_lo", [P, P], F32R, s3)
                fk_hi = sb("fk_hi", [P, SEQ], F32R, s3)
                fk_lo = sb("fk_lo", [P, SEQ], F32R, s3)
                fv_hi = sb("fv_hi", [P, 8, P], F32R, s3)
                fv_lo = sb("fv_lo", [P, 8, P], F32R, s3)
                fcq = sb("fcq", [P, P], F32R, s3)
                fp_w = sb("fp_w", [P, 8, P], F32, s3)
                fpT_hi = sb("fpT_hi", [P, 8, P], F32R, s3)
                fpT_lo = sb("fpT_lo", [P, 8, P], F32R, s3)
                fo_st = sb("fo_st", [P, P], F32, s3)

            x_loaded = [sem("x_loaded_0"), sem("x_loaded_1")]
            x_normed = sem("x_normed")
            x_var = sem("x_var")
            x_std = sem("x_std")
            x_turned = sem("x_turned")
            xt_copied = sem("xt_copied")
            ada_loaded = [sem("ada_loaded_0"), sem("ada_loaded_1")]
            ada_done = sem("ada_done")
            small_loaded = sem("small_loaded")
            mod_ready = sem("mod_ready")
            c_loaded = sem("c_loaded")
            x_stats = sem("x_stats")
            ada_b_turned = sem("ada_b_turned")
            ada_read = sem("ada_read")
            s_scaled = sem("s_scaled")
            h_hi_ready = sem("h_hi_ready")
            h_ready = sem("h_ready")
            consts = sem("consts")
            pool_step = sem("pool_step")
            ident_ready = sem("ident_ready")
            half0_done = sem("half0_done")
            proj_copied = sem("proj_copied")
            proj_stored = [sem("proj_stored_0"), sem("proj_stored_1")]
            gate_loaded = sem("gate_loaded")
            gate_added = sem("gate_added")
            gate_summed = sem("gate_summed")
            gate_ready = sem("gate_ready")
            gate_stored = sem("gate_stored")
            fg_loaded = sem("fg_loaded")
            fg_neg = sem("fg_neg")
            fg_exp = sem("fg_exp")
            cum_done = sem("cum_done")
            cum_hi = sem("cum_hi")
            cum_ready = sem("cum_ready")
            s_loaded = [sem("s_loaded_0"), sem("s_loaded_1")]
            s_hi = sem("s_hi")
            s_prep = sem("s_prep")
            s_vt = sem("s_vt")
            s_vt_hi = sem("s_vt_hi")
            s_v = sem("s_v")
            s_qk = sem("s_qk")
            s_biased = sem("s_biased")
            s_max = sem("s_max")
            s_exp = sem("s_exp")
            s_inv = sem("s_inv")
            s_norm = sem("s_norm")
            s_turned = sem("s_turned")
            s_pt_hi = sem("s_pt_hi")
            s_pt = sem("s_pt")
            s_pv = sem("s_pv")
            s_o = sem("s_o")
            s_stored = sem("s_stored")
            f_q_loaded = [sem("f_q_loaded_0"), sem("f_q_loaded_1")]
            f_kv_loaded = sem("f_kv_loaded")
            f_k_hi = sem("f_k_hi")
            f_k = sem("f_k")
            f_vt = sem("f_vt")
            f_vt_hi = sem("f_vt_hi")
            f_v = sem("f_v")
            f_q_hi = sem("f_q_hi")
            f_q = sem("f_q")
            f_qk = sem("f_qk")
            f_max = sem("f_max")
            f_exp = sem("f_exp")
            f_inv = sem("f_inv")
            f_norm = sem("f_norm")
            f_turned = sem("f_turned")
            f_pt_hi = sem("f_pt_hi")
            f_pt = sem("f_pt")
            f_pv = sem("f_pv")
            f_o = sem("f_o")
            f_stored = sem("f_stored")

            block = main.enter_context(nc.Block())

            def col_rest(b):
                return COL_REST + P * (b - 1) - P * (B_G - B_FQ)

            @block.sync
            def _(sp):
                for t in range(2):
                    sp.dma_start(x_t[:, t, :], x2[:, t, :]).then_inc(x_loaded[t], 16)
                sp.dma_start(c_sb[:], c.rearrange("a (p k) -> p (a k)", p=P)).then_inc(c_loaded, 16)
                sp.dma_start(ada_rows[:], b_ada[0, 0:2 * D].rearrange("(r p) -> r p", p=P)).then_inc(c_loaded, 16)

                def load_ada(j, slot):
                    for s in range(2):
                        sp.dma_start(ada_raw[:, slot, :, s, :],
                                     ada_v[:, :, ds(s * D + j * P, P)]).then_inc(ada_loaded[slot], 16)

                load_ada(0, 0)
                load_ada(1, 1)
                with sp.Fori(1, 4) as g:
                    for t in range(2):
                        sp.wait_ge(x_turned, 4 * (2 * g + (t - 1)))
                        sp.dma_start(x_t[:, t, :], x2[:, ds(2 * g + t, 1), :]
                                     .rearrange("p a d -> p (a d)")).then_inc(x_loaded[t], 16)
                with sp.Fori(1, KD // 2) as g:
                    for t in range(2):
                        sp.wait_ge(ada_done, 2 * g + (t - 1))
                        load_ada(2 * g + t, t)

                def block_in(b, col, first=False):
                    for kh in range(2):
                        load_chunk(sp, 2 * b + kh, kh, w_in_v[:, 8 * kh:8 * kh + 8, ds(col, P)], first)

                block_in(0, COL_FLOG, first=True)
                with sp.Fori(B_SQ, B_FQ) as b:
                    block_in(b, COL_REST + P * (b - 1))
                for s in range(2):
                    sp.wait_ge(proj_stored[s], 16)
                sp.dma_start(fg[0][:], proj_d[0, 0:FOX_HEADS, :]).then_inc(fg_loaded, 16)
                sp.dma_start(bf_c[:], b_f.rearrange("a h -> h a"), allow_slow_non_contiguous=True).then_inc(fg_loaded, 16)
                sp.wait_ge(consts, 1)
                with sp.Fori(0, KD) as k:
                    block_in(k + B_FQ, P * k)
                    sp.wait_ge(gate_added, k)
                    sp.dma_start(gate_raw[:], ada_v[:, ds(k, 1), 2 * D:3 * D]
                                 .rearrange("p a n -> p (a n)")).then_inc(gate_loaded, 16)
                sp.wait_ge(gate_added, KD - 1)
                block_in(B_FQ + KD, P * KD)
                sp.wait_ge(gate_added, KD)
                sp.dma_start(gate_row, b_ada[:, 2 * D:3 * D]).then_inc(gate_loaded, 16)
                with sp.Fori(B_FQ + KD + 1, B_G) as b:
                    block_in(b, P * (b - B_FQ))

                sp.sem_inc(s_v, 2)
                for s in range(2):
                    sp.wait_ge(proj_stored[s], 16 * B_FQ)
                with sp.Fori(0, 2) as g:
                    with sp.Fori(0, 4) as m:
                        for par in range(2):
                            u = 8 * g + 2 * m + par
                            block_in(u + B_G, COL_REST + P * (u + (B_FQ - 1)))
                            sp.wait_ge(s_v, u + 1)
                            if par == 0:
                                sp.wait_ge(gate_stored, 16)
                                sp.wait_ge(cum_ready, 2)
                            t0 = (2 * m + par) * P
                            for e in range(2):
                                sp.dma_start(sq_raw[SWA_D * e:SWA_D * (e + 1), par],
                                             q_heads[:, ds(8 * g + 4 * e, 4), ds(t0, P)]
                                             ).then_inc(s_loaded[par], 16)
                            for base, dst in ((B_SK, sk_raw), (B_SV, sv_raw)):
                                sp.dma_start(dst[:, par, :], proj_d[ds(g + base, 1), :, ds(t0, P)]
                                             .rearrange("a p t -> p (a t)")).then_inc(s_loaded[par], 16)

                sp.sem_inc(f_q, 2)
                for s in range(2):
                    sp.wait_ge(proj_stored[s], 16 * B_G)
                with sp.Fori(0, FOX_HEADS) as h:
                    for i in range(8):
                        if i % 2 == 0:
                            block_in(4 * h + (B_M + i // 2), 4 * P * h + (col_rest(B_M) + P * (i // 2)))
                        if i == 0:
                            sp.wait_ge(s_o, 16)
                            sp.wait_ge(s_stored, 512)
                            sp.wait_ge(s_scaled, 2)
                            sp.wait_ge(f_k, h)
                            sp.wait_ge(f_vt, h)
                            for base, dst in ((B_FK, fk_raw), (B_FV, fv_raw)):
                                sp.dma_start(dst[:], proj_d[ds(h + base, 1), :, :]
                                             .rearrange("a p t -> p (a t)")).then_inc(f_kv_loaded, 16)
                        sp.wait_ge(f_q, 8 * h + (i + 1))
                        sp.dma_start(fq_raw[:, i % 2, :], proj_d[ds(h + B_FQ, 1), :, i * P:(i + 1) * P]
                                     .rearrange("a p t -> p (a t)")).then_inc(f_q_loaded[i % 2], 16)
                load_chunk(sp, TAIL, 0, wbf_v[:, :, 0:P])

            @block.gpsimd
            def _(pool):
                own = Steps(pool, pool_step)
                own.enter()
                own(nc.gpsimd.memset(ident[:], 0.0))
                nc.gpsimd.affine_select(out=ident[:], in_=ident[:], compare_op=ALU.not_equal, fill=1.0, base=0,
                                        pattern=[[-1, P]], channel_multiplier=1).then_inc(ident_ready, 1)
                own(nc.gpsimd.memset(head_sel[:], 0.0))
                for q in range(4):
                    own(nc.gpsimd.affine_select(out=head_sel[:], in_=head_sel[:], compare_op=ALU.not_equal, fill=1.0,
                                                base=-32 * q, pattern=[[-1, FOX_HEADS]], channel_multiplier=1))
                pool.wait_ge(h_ready, KD)
                own(nc.gpsimd.memset(gate_raw[:, 0:P], 0.0))
                own(nc.gpsimd.affine_select(out=gate_raw[:, 0:P], in_=gate_raw[:, 0:P], compare_op=ALU.is_ge,
                                            fill=NEG, base=0, pattern=[[-1, P]], channel_multiplier=1))
                own(nc.gpsimd.tensor_copy(mask_r[:], gate_raw[:, 0:P]))
                pool.wait_ge(ident_ready, 1)
                own(nc.gpsimd.tensor_copy(ident_r[:], ident[:]))
                for t in (cum_k, cum_q):
                    own(nc.gpsimd.memset(t[:].bitcast(F32), 0.0))
                for t, q in ((cum_q, 0), (cum_q, 32), (cum_k, 64), (cum_k, 96)):
                    own(nc.gpsimd.memset(t[q:q + FOX_HEADS, :].bitcast(F32), 1.0))
                own(nc.gpsimd.memset(ones[:], 1.0))
                nc.gpsimd.memset(gate_acc[:], 0.0).then_inc(consts, 1)

                pool.wait_ge(gate_stored, 16)
                pool.wait_ge(cum_ready, 2)
                for t in (sv_hi, sv_lo, sk_hi, sk_lo):
                    own(nc.gpsimd.memset(t[:].bitcast(F32), 0.0))
                own(nc.gpsimd.memset(no_prev[:], 0.0))
                own(nc.gpsimd.memset(no_prev[:, 0:1], NEG))
                pool.dma_start(sinks[:], attn_sinks.broadcast_to([P, SWA_HEADS])).then_inc(small_loaded, 16)
                own(nc.gpsimd.iota(dist[:], pattern=[[-P, 2], [-1, P]], base=P, channel_multiplier=1,
                                   allow_small_or_imprecise_dtypes=True))
                own(nc.gpsimd.affine_select(out=dist[:, 1, :], in_=dist[:, 1, :], compare_op=ALU.is_ge, fill=FAR,
                                            base=0, pattern=[[-1, P]], channel_multiplier=1))
                nc.gpsimd.affine_select(out=dist[:, 0, :], in_=dist[:, 0, :], compare_op=ALU.is_gt, fill=FAR,
                                        base=0, pattern=[[1, P]], channel_multiplier=-1).then_inc(consts, 1)
                with pool.Fori(0, 32) as s:
                    pool.wait_ge(s_inv, s + 1)
                    for i in range(4):
                        w = sp_w[:, i].rearrange("p k t -> p (k t)")
                        last = nc.gpsimd.tensor_tensor(w, w, row_inv[:, i:i + 1].broadcast_to([P, 2 * P]), ALU.mult)
                    last.then_inc(s_norm, 1)
                with pool.Fori(0, FOX_HEADS) as h:
                    for i in range(8):
                        pool.wait_ge(f_inv, 8 * h + (i + 1))
                        w = fp_w[:, 0:i + 1].rearrange("p j t -> p (j t)")
                        nc.gpsimd.tensor_tensor(w, w, row_inv[:, 0:1].broadcast_to([P, (i + 1) * P]),
                                                ALU.mult).then_inc(f_norm, 1)

            @block.scalar
            def _(act):
                with act.Fori(0, 8) as t:
                    act.wait_ge(x_var, t + 1)
                    nc.scalar.activation(sm[:, 1:2], sm[:, 0:1], ACT.Sqrt).then_inc(x_std, 1)
                    for q in range(4):
                        act.wait_ge(x_turned, 4 * t + (q + 1))
                        nc.scalar.copy(xnT[:, 4 * q:4 * q + 4, ds(t * P, P)],
                                       (sP if q < 2 else tP)[:, q % 2, :].rearrange("p (j t) -> p j t", j=4)
                                       ).then_inc(xt_copied, 1)
                with act.Fori(0, KD) as j:
                    act.wait_ge(mod_ready, j + 1)
                    nc.scalar.copy(h_hi[:, ds(j, 1), :], xnT[:, ds(j, 1), :]).then_inc(h_hi_ready, 1)

                def copy_proj(b, half):
                    if half == 0:
                        act.wait_ge(half0_done, b + 1)
                    else:
                        act.wait_ge(chunk_used, 2 * b + 2)
                    if not isinstance(b, int):
                        act.wait_ge(proj_stored[half], 16 * b)
                    nc.scalar.copy(stage[:, half, :], projP[:, half, :]).then_inc(proj_copied, 1)
                    act.wait_ge(proj_copied, 2 * b + (half + 1))
                    dst = proj_d[ds(b, 1), :, half * HALF:(half + 1) * HALF].rearrange("a p t -> p (a t)")
                    act.dma_start(dst, stage[:, half, :]).then_inc(proj_stored[half], 16)

                def proj_step(b):
                    split_hi(act, 2 * b + 1, 1, b + 1)
                    split_hi(act, 2 * b + 2, 0, b + 2)
                    copy_proj(b, 0)
                    copy_proj(b, 1)

                split_hi(act, 0, 0, 1)
                proj_step(0)
                with act.Fori(B_SQ, B_FQ) as b:
                    proj_step(b)
                act.wait_ge(fg_neg, 1)
                nc.scalar.activation(fg[2][:], fg[1][:], ACT.Exp).then_inc(fg_exp, 1)
                with act.Fori(B_FQ, B_FQ + KD) as b:
                    proj_step(b)
                act.wait_ge(cum_done, 1)
                nc.scalar.activation(cum_k[0:FOX_HEADS, :], fg[4][:], ACT.Copy, scale=-1.0).then_inc(cum_hi, 1)
                nc.scalar.copy(cum_q[64:64 + FOX_HEADS, :], fg[4][:]).then_inc(cum_hi, 1)
                act.wait_ge(gate_ready, 1)
                act.dma_start(gate_d, gate_row).then_inc(gate_stored, 16)
                with act.Fori(B_FQ + KD, B_G) as b:
                    proj_step(b)

                with act.Fori(0, 2) as g:
                    with act.Fori(0, 4) as m:
                        for par in range(2):
                            u = 8 * g + 2 * m + par
                            b = u + B_G
                            act.wait_ge(s_loaded[par], 64 * (4 * g + m + 1))
                            act.wait_ge(s_qk, 2 * u)
                            act.wait_ge(consts, 2)
                            nc.scalar.activation(sq_hi[:], sq_raw[:, par], ACT.Copy, scale=SWA_D ** -0.5)
                            nc.scalar.copy(sk_hi[:, par, :], sk_raw[:, par, :]).then_inc(s_hi, 1)
                            act.wait_ge(s_vt, u + 1)
                            nc.scalar.copy(sv_hi[:, par, 0, 0:SWA_D], tP[:, 0, 0:SWA_D])
                            nc.scalar.copy(sv_hi[:, par, 1, SWA_D:P], tP[:, 0, SWA_D:P]).then_inc(s_vt_hi, 1)
                            for e in range(2):
                                s = 2 * u + e
                                split_hi(act, 2 * b + (e + 1), 1 - e, b + (e + 1))
                                act.wait_ge(s_max, s + 1)
                                for i in range(4):
                                    nc.scalar.activation(sp_w[:, i], sp_w[:, i], ACT.Exp, bias=neg_max[:, i:i + 1],
                                                         accum_out=row_sum[:, i:i + 1])
                                nc.scalar.activation(sink_exp[:], sink_exp[:], ACT.Exp).then_inc(s_exp, 1)
                                if e == 1:
                                    copy_proj(b, 0)
                                for k in range(2):
                                    act.wait_ge(s_turned, 2 * s + (k + 1))
                                    nc.scalar.copy(spT_hi[:, k, :], tP[:, k, :]).then_inc(s_pt_hi, 1)
                            copy_proj(b, 1)
                            act.wait_ge(s_pv, u + 1)
                            act.wait_ge(s_stored, 32 * u)
                            nc.scalar.copy(so_st[:], oP[:, :].rearrange("p (i t) -> p i t", i=4)).then_inc(s_o, 1)
                            act.wait_ge(s_o, u + 1)
                            for e in range(2):
                                act.dma_start(o_heads[:, ds(8 * g + 4 * e, 4), ds((2 * m + par) * P, P)],
                                              so_st[SWA_D * e:SWA_D * (e + 1)]).then_inc(s_stored, 16)

                act.wait_ge(s_scaled, 2)
                with act.Fori(0, FOX_HEADS) as h:
                    def q_high(i):
                        act.wait_ge(f_q_loaded[i % 2], 64 * h + 16 * (i // 2 + 1))
                        act.wait_ge(f_qk, 8 * h + i)
                        nc.scalar.activation(fq_hi[:], fq_raw[:, i % 2, :], ACT.Copy,
                                             scale=float(P) ** -0.5).then_inc(f_q_hi, 1)

                    q_high(0)
                    act.wait_ge(f_kv_loaded, 32 * h + 32)
                    nc.scalar.copy(fk_hi[:], fk_raw[:]).then_inc(f_k_hi, 1)
                    act.wait_ge(f_vt, h + 1)
                    for k in range(2):
                        last = nc.scalar.copy(fv_hi[:, 4 * k:4 * k + 4, :],
                                              tP[:, k, :].rearrange("p (j t) -> p j t", j=4))
                    last.then_inc(f_vt_hi, 1)
                    turned = 0
                    for i in range(8):
                        b = 4 * h + (B_M + i // 2)
                        e = i % 2
                        split_hi(act, 2 * b + (e + 1), 1 - e, b + (e + 1))
                        act.wait_ge(f_max, 8 * h + (i + 1))
                        nc.scalar.activation(fp_w[:, 0:i + 1, :].rearrange("p j t -> p (j t)"),
                                             sP[:, :, :].rearrange("p a t -> p (a t)")[:, 0:(i + 1) * P], ACT.Exp,
                                             bias=neg_max[:, 0:1], accum_out=row_sum[:, 0:1]).then_inc(f_exp, 1)
                        if e == 1:
                            copy_proj(b, 0)
                        for k in range(i // 4 + 1):
                            turned += 1
                            n = min(4, i + 1 - 4 * k)
                            act.wait_ge(f_turned, 12 * h + turned)
                            nc.scalar.copy(fpT_hi[:, 4 * k:4 * k + n, :],
                                           tP[:, k, 0:n * P].rearrange("p (j t) -> p j t", j=n)).then_inc(f_pt_hi, 1)
                        if i < 7:
                            q_high(i + 1)
                        if e == 1:
                            copy_proj(b, 1)
                        act.wait_ge(f_pv, 8 * h + (i + 1))
                        act.wait_ge(f_stored, 128 * h + 16 * i)
                        nc.scalar.copy(fo_st[:], oP[:, 0:P]).then_inc(f_o, 1)
                        act.wait_ge(f_o, 8 * h + (i + 1))
                        act.dma_start(o_d[ds(h, 1), :, i * P:(i + 1) * P].rearrange("a p t -> p (a t)"),
                                      fo_st[:]).then_inc(f_stored, 16)
                for s in range(2):
                    act.wait_ge(proj_stored[s], 16 * BLOCKS)
                act.wait_ge(s_stored, 512)
                act.wait_ge(f_stored, 1024)

            @block.vector
            def _(dve):
                own = Steps(dve, dve_step)
                with dve.Fori(0, 4) as g:
                    own.enter(12 * g)
                    for slot in range(2):
                        t = 2 * g + slot
                        dve.wait_ge(x_loaded[slot], 16 * (g + 1))
                        for q in range(4):
                            last = nc.vector.bn_stats(bn[:, q, :], x_t[:, slot, q * HALF:(q + 1) * HALF])
                        last.then_inc(x_stats, 1)
                        dve.wait_ge(x_stats, t + 1)
                        nc.vector.memset(sm[:, 2:3], 0.0)
                        own(nc.vector.bn_aggr(mv[:], bn[:].rearrange("p a b -> p (a b)")))
                        nc.vector.tensor_scalar(sm[:, 0:1], mv[:, 1:2], LN_EPS, None, ALU.add).then_inc(x_var, 1)
                        dve.wait_ge(x_std, t + 1)
                        own(nc.vector.reciprocal(sm[:, 2:3], sm[:, 1:2]))
                        own(nc.vector.tensor_tensor(sm[:, 3:4], sm[:, 2:3], sm[:, 2:3], ALU.mult))
                        own(nc.vector.tensor_tensor(sm[:, 3:4], sm[:, 3:4], sm[:, 0:1], ALU.mult))
                        own(nc.vector.tensor_scalar(sm[:, 3:4], sm[:, 3:4], -0.5, 1.5, ALU.mult, ALU.add))
                        own(nc.vector.tensor_tensor(sm[:, 3:4], sm[:, 3:4], sm[:, 2:3], ALU.mult))
                        nc.vector.tensor_scalar(x_t[:, slot, :], x_t[:, slot, :], mv[:, 0:1], sm[:, 3:4],
                                                ALU.subtract, ALU.mult).then_inc(x_normed, 1)
                        dve.wait_ge(x_normed, t + 1)
                own.leave(48, 4)
                dve.wait_ge(ada_b_turned, 1)
                dve.wait_ge(xt_copied, 32)
                own.enter()
                nc.vector.tensor_copy(ada_b[:, 0, :], projP[:, 0, 0:KD])
                own(nc.vector.tensor_scalar(ada_b[:, 1, :], projP[:, 0, KD:2 * KD], 1.0, None, ALU.add))
                own.leave(1)
                with dve.Fori(0, KD // 2) as g:
                    for slot in range(2):
                        j = 2 * g + slot
                        dve.wait_ge(ada_done, j + 1)
                        nc.vector.tensor_tensor(ada_s[:, 0, :], (adaP if slot else oP)[:, 0:2],
                                                ada_b[:, :, ds(j, 1)].rearrange("p s a -> p (s a)"),
                                                ALU.add).then_inc(ada_read, 1)
                        dve.wait_ge(ada_read, j + 1)
                        nc.vector.tensor_scalar(xnT[:, ds(j, 1), :], xnT[:, ds(j, 1), :], ada_s[:, 0, 1:2],
                                                ada_s[:, 0, 0:1], ALU.mult, ALU.add).then_inc(mod_ready, 1)
                        dve.wait_ge(h_hi_ready, j + 1)
                        nc.vector.tensor_tensor(h_lo[:, ds(j, 1), :], xnT[:, ds(j, 1), :],
                                                h_hi[:, ds(j, 1), :].bitcast(F32), ALU.subtract).then_inc(h_ready, 1)

                def proj_step(b):
                    split_lo(dve, 2 * b + 1, 1)
                    split_lo(dve, 2 * b + 2, 0)

                split_lo(dve, 0, 0)
                proj_step(0)
                with dve.Fori(B_SQ, B_FQ) as b:
                    proj_step(b)
                z, a, e, t, acc = [f[:] for f in fg]
                dve.wait_ge(fg_loaded, 32)
                dve.wait_ge(consts, 1)
                own.enter()
                own(nc.vector.tensor_scalar(z, z, bf_c[:, 0:1], None, ALU.add))
                own(nc.vector.tensor_scalar(t, z, -1.0, None, ALU.mult))
                nc.vector.tensor_tensor(a, z, t, ALU.min).then_inc(fg_neg, 1)
                own(nc.vector.tensor_scalar(z, z, 0.0, None, ALU.min))
                dve.wait_ge(fg_exp, 1)
                own(nc.vector.tensor_scalar(t, e, 2.0, None, ALU.add))
                own(nc.vector.reciprocal(t, t))
                own(nc.vector.tensor_tensor(a, e, t, ALU.mult))
                own(nc.vector.tensor_tensor(t, a, a, ALU.mult))
                own(nc.vector.tensor_scalar(acc, t, 1.0 / 15.0, None, ALU.mult))
                own.leave(8)
                with dve.Fori(0, KD) as k:
                    proj_step(k + B_FQ)
                    dve.wait_ge(gate_loaded, 16 * (k + 1))
                    nc.vector.scalar_tensor_tensor(out=gate_acc[:], in0=gate_raw[:], scalar=c_sb[:, ds(k, 1)],
                                                   in1=gate_acc[:], op0=ALU.mult, op1=ALU.add).then_inc(gate_added, 1)
                    dve.wait_ge(gate_added, k + 1)
                own.enter()
                for n in range(6, 0, -1):
                    own(nc.vector.scalar_tensor_tensor(out=acc, in0=acc, scalar=1.0 / (2 * n + 1), in1=t,
                                                       op0=ALU.add, op1=ALU.mult))
                own(nc.vector.scalar_tensor_tensor(out=acc, in0=acc, scalar=1.0, in1=a, op0=ALU.add, op1=ALU.mult))
                own(nc.vector.scalar_tensor_tensor(out=a, in0=acc, scalar=-2.0, in1=z, op0=ALU.mult, op1=ALU.add))
                own(nc.vector.memset(t, 1.0))
                nc.vector.tensor_tensor_scan(acc, t, a, 0.0, ALU.mult, ALU.add).then_inc(cum_done, 1)
                dve.wait_ge(cum_done, 1)
                dve.wait_ge(cum_hi, 2)
                nc.vector.scalar_tensor_tensor(out=cum_k[32:32 + FOX_HEADS, :], in0=acc, scalar=-1.0,
                                               in1=cum_k[0:FOX_HEADS, :].bitcast(F32), op0=ALU.mult,
                                               op1=ALU.subtract).then_inc(cum_ready, 1)
                nc.vector.tensor_tensor(cum_q[96:96 + FOX_HEADS, :], cum_k[0:FOX_HEADS, :].bitcast(F32), acc,
                                        ALU.add).then_inc(cum_ready, 1)
                own.leave(9)
                dve.wait_ge(gate_loaded, 16 * (KD + 1))
                dve.wait_ge(gate_summed, 1)
                for q in range(4):
                    last = nc.vector.tensor_tensor(gate_row[:, q * HALF:(q + 1) * HALF],
                                                   (sP if q < 2 else tP)[0:1, q % 2, :],
                                                   gate_row[:, q * HALF:(q + 1) * HALF], ALU.add)
                last.then_inc(gate_ready, 1)
                with dve.Fori(B_FQ + KD, B_G) as b:
                    proj_step(b)

                dve.wait_ge(consts, 2)
                dve.wait_ge(small_loaded, 16)
                own.enter()
                own(nc.vector.tensor_scalar(neg_sinks[:], sinks[:], -1.0, None, ALU.mult))
                for e in range(2):
                    for i in range(4):
                        slope = 2.0 ** (-8.0 * (4 * e + i + 1) / SWA_HEADS)
                        own(nc.vector.tensor_scalar(s_bias[:, e, i], dist[:], -slope, None, ALU.mult))
                own.leave(9)
                with dve.Fori(0, 2) as g:
                    with dve.Fori(0, 4) as m:
                        own.enter(48 * g + 12 * m)
                        for par in range(2):
                            u = 8 * g + 2 * m + par
                            b = u + B_G
                            dve.wait_ge(s_hi, u + 1)
                            nc.vector.scalar_tensor_tensor(
                                out=sq_lo[:].rearrange("p i t -> p (i t)"),
                                in0=sq_raw[:, par].rearrange("p i t -> p (i t)"), scalar=SWA_D ** -0.5,
                                in1=sq_hi[:].bitcast(F32).rearrange("p i t -> p (i t)"),
                                op0=ALU.mult, op1=ALU.subtract).then_inc(s_prep, 1)
                            nc.vector.tensor_tensor(sk_lo[:, par, :], sk_raw[:, par, :],
                                                    sk_hi[:, par, :].bitcast(F32), ALU.subtract).then_inc(s_prep, 1)
                            dve.wait_ge(s_vt_hi, u + 1)
                            nc.vector.tensor_tensor(sv_lo[:, par, 0, 0:SWA_D], tP[:, 0, 0:SWA_D],
                                                    sv_hi[:, par, 0, 0:SWA_D].bitcast(F32), ALU.subtract)
                            nc.vector.tensor_tensor(sv_lo[:, par, 1, SWA_D:P], tP[:, 0, SWA_D:P],
                                                    sv_hi[:, par, 1, SWA_D:P].bitcast(F32),
                                                    ALU.subtract).then_inc(s_v, 1)
                            for e in range(2):
                                s = 2 * u + e
                                dve.wait_ge(s_qk, s + 1)
                                sc = sP[:].rearrange("p a (i k t) -> p (a i) k t", i=2, k=2)
                                for k in range(2):
                                    now = k == par
                                    if par == 0 and not now:
                                        ins = nc.vector.scalar_tensor_tensor(
                                            out=sp_w[:, :, k, :], in0=sc[:, :, k, :], scalar=no_prev[:, ds(m, 1)],
                                            in1=s_bias[:, e, :, 0, :], op0=ALU.add, op1=ALU.add)
                                    else:
                                        ins = nc.vector.tensor_tensor(sp_w[:, :, k, :], sc[:, :, k, :],
                                                                      s_bias[:, e, :, 1 if now else 0, :], ALU.add)
                                ins.then_inc(s_biased, 1)
                                dve.wait_ge(s_biased, s + 1)
                                own(nc.vector.tensor_reduce(neg_max[:], sp_w[:].rearrange("p i k t -> p i (k t)"),
                                                            AX.X, ALU.max, negate=True))
                                own(nc.vector.tensor_tensor(neg_max[:], neg_max[:],
                                                            neg_sinks[:, ds(8 * g + 4 * e, 4)], ALU.min))
                                nc.vector.tensor_tensor(sink_exp[:], neg_max[:], sinks[:, ds(8 * g + 4 * e, 4)],
                                                        ALU.add).then_inc(s_max, 1)
                                split_lo(dve, 2 * b + (e + 1), 1 - e)
                                dve.wait_ge(s_exp, s + 1)
                                own(nc.vector.tensor_tensor(row_inv[:], row_sum[:], sink_exp[:], ALU.add))
                                nc.vector.reciprocal(row_inv[:], row_inv[:]).then_inc(s_inv, 1)
                                for k in range(2):
                                    dve.wait_ge(s_pt_hi, 2 * s + (k + 1))
                                    nc.vector.tensor_tensor(spT_lo[:, k, :], tP[:, k, :],
                                                            spT_hi[:, k, :].bitcast(F32),
                                                            ALU.subtract).then_inc(s_pt, 1)
                    nc.vector.tensor_scalar(s_bias[:].rearrange("p e i k t -> p (e i k t)"),
                                            s_bias[:].rearrange("p e i k t -> p (e i k t)"), 1.0 / 16.0, None,
                                            ALU.mult).then_inc(s_scaled, 1)
                    dve.wait_ge(s_scaled, g + 1)
                own.leave(96, 8)

                with dve.Fori(0, FOX_HEADS) as h:
                    def q_low(i):
                        dve.wait_ge(f_q_hi, 8 * h + (i + 1))
                        nc.vector.scalar_tensor_tensor(out=fq_lo[:], in0=fq_raw[:, i % 2, :], scalar=float(P) ** -0.5,
                                                       in1=fq_hi[:].bitcast(F32), op0=ALU.mult, op1=ALU.subtract)
                        nc.vector.tensor_scalar(fcq[:], cum_q[:, i * P:(i + 1) * P].bitcast(F32),
                                                head_sel[:, ds(h, 1)], None, ALU.mult).then_inc(f_q, 1)

                    q_low(0)
                    dve.wait_ge(f_k_hi, h + 1)
                    nc.vector.tensor_tensor(fk_lo[:], fk_raw[:], fk_hi[:].bitcast(F32), ALU.subtract).then_inc(f_k, 1)
                    dve.wait_ge(f_vt_hi, h + 1)
                    for k in range(2):
                        last = nc.vector.tensor_tensor(
                            fv_lo[:, 4 * k:4 * k + 4, :].rearrange("p j t -> p (j t)"), tP[:, k, :],
                            fv_hi[:, 4 * k:4 * k + 4, :].bitcast(F32).rearrange("p j t -> p (j t)"), ALU.subtract)
                    last.then_inc(f_v, 1)
                    turned = 0
                    for i in range(8):
                        b = 4 * h + (B_M + i // 2)
                        e = i % 2
                        dve.wait_ge(f_qk, 8 * h + (i + 1))
                        nc.vector.tensor_reduce(neg_max[:, 0:1],
                                                sP[:, :, :].rearrange("p a t -> p (a t)")[:, 0:(i + 1) * P],
                                                AX.X, ALU.max, negate=True).then_inc(f_max, 1)
                        split_lo(dve, 2 * b + (e + 1), 1 - e)
                        dve.wait_ge(f_exp, 8 * h + (i + 1))
                        nc.vector.reciprocal(row_inv[:, 0:1], row_sum[:, 0:1]).then_inc(f_inv, 1)
                        for k in range(i // 4 + 1):
                            turned += 1
                            n = min(4, i + 1 - 4 * k)
                            dve.wait_ge(f_pt_hi, 12 * h + turned)
                            nc.vector.tensor_tensor(
                                fpT_lo[:, 4 * k:4 * k + n, :].rearrange("p j t -> p (j t)"), tP[:, k, 0:n * P],
                                fpT_hi[:, 4 * k:4 * k + n, :].bitcast(F32).rearrange("p j t -> p (j t)"),
                                ALU.subtract).then_inc(f_pt, 1)
                        if i < 7:
                            q_low(i + 1)
                dve.wait_ge(f_pt, 96)

            @block.tensor
            def _(pe):
                def turn(dst, src):
                    return nc.tensor.transpose(dst, src, ident[:])

                pe.wait_ge(ident_ready, 1)
                with pe.Fori(0, 4) as g:
                    for slot in range(2):
                        t = 2 * g + slot
                        pe.wait_ge(x_normed, t + 1)
                        pe.wait_ge(xt_copied, 4 * t)
                        for q in range(4):
                            for j in range(4):
                                last = turn((sP if q < 2 else tP)[:, q % 2, j * P:(j + 1) * P],
                                            x_t[:, slot, (4 * q + j) * P:(4 * q + j + 1) * P])
                            last.then_inc(x_turned, 1)

                def ada_chunk(g, slot, first):
                    j = 2 * g + slot
                    pe.wait_ge(ada_loaded[slot], 32 * (g + 1))
                    if not first:
                        pe.wait_ge(ada_read, j - 1)
                    for s in range(2):
                        for k in range(KD):
                            last = nc.tensor.matmul((adaP if slot else oP)[:, s:s + 1], ada_raw[:, slot, k, s, :],
                                                    c_sb[:, k:k + 1], start=(k == 0), stop=(k == KD - 1))
                    last.then_inc(ada_done, 1)

                pe.wait_ge(c_loaded, 32)
                nc.tensor.transpose(projP[:, 0, 0:2 * KD], ada_rows[:], ident[0:2 * KD, 0:2 * KD]
                                    ).then_inc(ada_b_turned, 1)
                ada_chunk(0, 0, True)
                ada_chunk(0, 1, True)
                with pe.Fori(1, KD // 2) as g:
                    for slot in range(2):
                        ada_chunk(g, slot, False)

                def proj(b, e, lo=0, hi=MMS):
                    for n in range(lo, hi):
                        half, k, part = n // 24, n // 3 % 8, n % 3
                        if n == 0:
                            pe.wait_ge(chunk_lo, 2 * b + (e + 1))
                        if n % 24 == 0 and e == 0 and not isinstance(b, int):
                            pe.wait_ge(proj_copied, 2 * b + (half - 1))
                        if isinstance(b, int) and half == 0 and part == 0:
                            pe.wait_ge(h_ready, 8 * e + k + 1)
                        w, hh = ((w_hi, h_hi), (w_hi, h_lo), (w_lo, h_hi))[part]
                        last = nc.tensor.matmul(projP[:, half, :], w[:, e, k * P:(k + 1) * P],
                                                hh[:, 8 * e + k, half * HALF:(half + 1) * HALF],
                                                start=(e == 0 and n % 24 == 0), stop=(e == 1 and n % 24 == 23))
                        if e == 1 and n == 23:
                            last.then_inc(half0_done, 1)
                        if n == MMS - 1:
                            last.then_inc(chunk_used, 1)

                proj(0, 0)
                proj(0, 1)
                with pe.Fori(B_SQ, B_FQ + KD) as b:
                    proj(b, 0)
                    proj(b, 1)
                pe.wait_ge(consts, 1)
                pe.wait_ge(gate_added, KD)
                for q in range(4):
                    last = nc.tensor.matmul((sP if q < 2 else tP)[0:1, q % 2, :], ones[:],
                                            gate_acc[:, q * HALF:(q + 1) * HALF], start=True, stop=True)
                last.then_inc(gate_summed, 1)
                with pe.Fori(B_FQ + KD, B_G) as b:
                    proj(b, 0)
                    proj(b, 1)

                with pe.Fori(0, 2) as g:
                    with pe.Fori(0, 4) as m:
                        for par in range(2):
                            u = 8 * g + 2 * m + par
                            b = u + B_G

                            def scores(e):
                                pe.wait_ge(s_prep, 2 * u + 2)
                                pe.wait_ge(gate_ready, 1)
                                pe.wait_ge(s_biased, 2 * u + e)
                                r = slice(SWA_D * e, SWA_D * (e + 1))
                                for i in range(4):
                                    dst = sP[:, i // 2, 2 * P * (i % 2):2 * P * (i % 2 + 1)]
                                    for part, (q, k) in enumerate(((sq_hi, sk_hi), (sq_hi, sk_lo), (sq_lo, sk_hi))):
                                        last = nc.tensor.matmul(dst, q[r, i, :], k[r, :, :],
                                                                start=(part == 0), stop=(part == 2))
                                last.then_inc(s_qk, 1)

                            def turn_weights(e):
                                pe.wait_ge(s_norm, 2 * u + (e + 1))
                                if e == 0:
                                    pe.wait_ge(s_v, u + 3)
                                for k in range(2):
                                    for i in range(4):
                                        last = turn(tP[:, k, i * P:(i + 1) * P], sp_w[:, i, k, :])
                                    last.then_inc(s_turned, 1)

                            def weigh(e):
                                pe.wait_ge(s_pt, 4 * u + 2 * (e + 1))
                                if e == 0:
                                    pe.wait_ge(s_o, u)
                                n = 0
                                for k in range(2):
                                    for v, w in ((sv_hi, spT_hi), (sv_hi, spT_lo), (sv_lo, spT_hi)):
                                        last = nc.tensor.matmul(oP[:, :], v[:, k, e, :], w[:, k, :],
                                                                start=(e == 0 and n == 0), stop=(e == 1 and n == 5))
                                        n += 1
                                if e == 1:
                                    last.then_inc(s_pv, 1)

                            pe.wait_ge(s_loaded[par], 64 * (4 * g + m + 1))
                            pe.wait_ge(s_pt, 4 * u)
                            turn(tP[:, 0, 0:P], sv_raw[:, par, :]).then_inc(s_vt, 1)
                            proj(b, 0, 0, 12)
                            scores(0)
                            proj(b, 0, 12, MMS)
                            turn_weights(0)
                            scores(1)
                            proj(b, 1, 0, 12)
                            weigh(0)
                            proj(b, 1, 12, 36)
                            turn_weights(1)
                            proj(b, 1, 36, MMS)
                            weigh(1)

                with pe.Fori(0, FOX_HEADS) as h:
                    pe.wait_ge(f_kv_loaded, 32 * h + 32)
                    pe.wait_ge(s_pt, 64)
                    pe.wait_ge(f_pt, 12 * h)
                    for j in range(8):
                        last = turn(tP[:, j // 4, (j % 4) * P:(j % 4 + 1) * P], fv_raw[:, j * P:(j + 1) * P])
                    last.then_inc(f_vt, 1)
                    turned = 0
                    for i in range(8):
                        b = 4 * h + (B_M + i // 2)
                        e = i % 2
                        first = 18 if i == 0 else 0
                        proj(b, e, 0, first)
                        pe.wait_ge(f_q, 8 * h + (i + 3))
                        if i == 0:
                            pe.wait_ge(f_k, h + 1)
                            pe.wait_ge(s_biased, 32)
                        pe.wait_ge(f_exp, 8 * h + i)
                        for a in range(i // 4 + 1):
                            c0, c1 = a * HALF, min((a + 1) * HALF, (i + 1) * P)
                            dst = sP[:, a, 0:c1 - c0]
                            nc.tensor.matmul(dst, fcq[:], cum_k[:, c0:c1], start=True, stop=False)
                            if a == i // 4:
                                nc.tensor.matmul(sP[:, a, (i % 4) * P:(i % 4 + 1) * P], ident_r[:], mask_r[:],
                                                 start=False, stop=False)
                            for part, (q, k) in enumerate(((fq_hi, fk_hi), (fq_hi, fk_lo), (fq_lo, fk_hi))):
                                last = nc.tensor.matmul(dst, q[:], k[:, c0:c1], start=False, stop=(part == 2))
                        last.then_inc(f_qk, 1)
                        proj(b, e, first, 36)
                        pe.wait_ge(f_norm, 8 * h + (i + 1))
                        if i == 0:
                            pe.wait_ge(f_v, h + 1)
                        for j in range(i + 1):
                            last = turn(tP[:, j // 4, (j % 4) * P:(j % 4 + 1) * P], fp_w[:, j, :])
                            if j == 3 or j == i:
                                last.then_inc(f_turned, 1)
                        turned += i // 4 + 1
                        proj(b, e, 36, MMS)
                        pe.wait_ge(f_pt, 12 * h + turned)
                        pe.wait_ge(f_o, 8 * h + i)
                        for j in range(i + 1):
                            for part, (v, w) in enumerate(((fv_hi, fpT_hi), (fv_hi, fpT_lo), (fv_lo, fpT_hi))):
                                last = nc.tensor.matmul(oP[:, 0:P], v[:, j, :], w[:, j, :],
                                                        start=(j == 0 and part == 0), stop=(j == i and part == 2))
                        last.then_inc(f_pv, 1)

        with ExitStack() as last_part:
            def sb2(name, shape, dt=F32):
                return sb(name, shape, dt, last_part)

            yP = last_part.enter_context(nc.psum_tensor("yP", [P, 2, HALF], F32))
            zP = last_part.enter_context(nc.psum_tensor("zP", [P, 4, HALF], F32))
            og_hi = sb2("og_hi", [P, KD, HALF], F32R)
            og_lo = sb2("og_lo", [P, KD, HALF], F32R)
            with ExitStack() as early:
                o_in = sb("o_in", [P, KD, HALF], F32, early)
                early_pad = sb("early_pad", [P, KD, HALF], F32, early)
                g_in = sb("g_in", [P, KD, HALF], F32, early)
            mg_hi = sb2("mg_hi", [P, KD, HALF], F32R)
            mg_lo = sb2("mg_lo", [P, KD, HALF], F32R)
            z = sb2("z", [P, 4, D])
            aux = sb2("aux", [P, 2, HALF])
            sg = sb2("sg", [P, 2, HALF])
            ta = sb2("ta", [P, HALF])
            tb_ = sb2("tb", [P, HALF])
            gate_sl = sb2("gate_sl", [P, HALF])
            lng = sb2("lng", [P, HALF])
            lnb = sb2("lnb", [P, HALF])
            z_bn = sb2("z_bn", [P, 4, 4, 6])
            z_mv = sb2("z_mv", [P, 4, 2])
            z_sm = sb2("z_sm", [P, 4, 4])

            og_in = [sem(f"og_in_{q}") for q in range(4)]
            og_sig = sem("og_sig")
            og_t = sem("og_t")
            og_g = sem("og_g")
            og_hi_ready = sem("og_hi_ready")
            og_ready = sem("og_ready")
            aux_loaded = sem("aux_loaded")
            sg_ready = sem("sg_ready")
            y_read = sem("y_read")
            t_ready = sem("t_ready")
            mg_hi_ready = sem("mg_hi_ready")
            mg_ready = sem("mg_ready")
            gate_loaded2 = sem("gate_slice_loaded")
            z_x = sem("z_x_loaded")
            z_done = sem("z_product_done")
            z_read = sem("z_read")
            z_added = sem("z_added")
            z_var = sem("z_var")
            z_std = sem("z_std")
            ln_ready = sem("ln_ready")
            ln_loaded = sem("ln_loaded")
            ln_done = sem("ln_done")
            out_stored = sem("out_stored")
            dve_step2 = sem("dve_step2")
            pool_step2 = sem("pool_step2")

            block = last_part.enter_context(nc.Block())

            def chunk_of(H, n):
                return n + (TAIL + 64 * H)

            @block.sync
            def _(sp):
                for q in range(4):
                    for src, base, dst in ((o_d, 0, o_in), (proj_d, B_G, g_in)):
                        sp.dma_start(dst[:, 4 * q:4 * q + 4, :],
                                     src[base + 4 * q:base + 4 * q + 4, :, 0:HALF].rearrange("k p t -> p k t")
                                     ).then_inc(og_in[q], 16)
                for H in range(2):
                    t0 = H * HALF

                    def branch_in(nb, first=False):
                        if not first:
                            load_chunk(sp, 2 * nb + (TAIL + 64 * H), 0, wbf_v[:, :, ds(nb * P, P)])
                        load_chunk(sp, 2 * nb + (TAIL + 64 * H + 1), 1, wbs_v[:, :, ds(nb * P, P)])
                        if H == 0 and not first:
                            sp.wait_ge(sg_ready, nb)
                        if H == 1:
                            sp.wait_ge(og_ready, 2 * KD)
                            sp.wait_ge(sg_ready, nb + 2 * KD)
                        for w in range(2):
                            sp.dma_start(aux[:, w, :], proj_d[ds(nb + (B_M + KD * w), 1), :, t0:t0 + HALF]
                                         .rearrange("a p t -> p (a t)")).then_inc(aux_loaded, 16)

                    if H == 0:
                        branch_in(0, first=True)
                    with sp.Fori(1 - H, KD) as nb:
                        branch_in(nb)
                    if H == 0:
                        sp.wait_ge(og_ready, KD)
                    else:
                        sp.wait_ge(out_stored, 64)
                    for tb in range(4):
                        sp.dma_start(z[:, tb, :], x2[:, 4 * H + tb, :]).then_inc(z_x, 16)
                    with sp.Fori(0, 4) as cg:
                        for kk in range(8):
                            load_chunk(sp, 8 * cg + (TAIL + 64 * H + 32 + kk), kk % 2,
                                       w_out_v[:, 2 * kk:2 * kk + 2, ds(cg * HALF, HALF)])
                            if kk == 3:
                                sp.wait_ge(z_read, 4 * cg + (16 * H + 4))
                                sp.dma_start(gate_sl[:], gate_d[0:1, ds(cg * HALF, HALF)].broadcast_to([P, HALF])
                                             ).then_inc(gate_loaded2, 16)
                            if H == 0 and kk % 2 == 1:
                                k = 4 * cg + kk // 2
                                sp.wait_ge(sg_ready, KD)
                                sp.wait_ge(og_ready, k + KD)
                                for w, src, base in ((0, o_d, 0), (1, proj_d, B_G)):
                                    sp.dma_start(aux[:, w, :], src[ds(k + base, 1), :, HALF:SEQ]
                                                 .rearrange("a p t -> p (a t)")).then_inc(aux_loaded, 16)

            @block.gpsimd
            def _(pool):
                for H in range(2):
                    pool.wait_ge(ln_ready, H + 1)
                    for cs in range(4):
                        n = 4 * cs + 16 * H
                        pool.wait_ge(ln_done, n)
                        cols = slice(cs * HALF, (cs + 1) * HALF)
                        pool.dma_start(lng[:], ln_g[0:1, cols].broadcast_to([P, HALF])).then_inc(ln_loaded, 16)
                        pool.dma_start(lnb[:], ln_b[0:1, cols].broadcast_to([P, HALF])).then_inc(ln_loaded, 16)
                        for tb in range(4):
                            nc.gpsimd.tensor_scalar(z[:, tb, cols], z[:, tb, cols], z_mv[:, tb, 0:1],
                                                    z_sm[:, 3, tb:tb + 1], ALU.subtract, ALU.mult
                                                    ).then_inc(pool_step2, 1)
                        pool.wait_ge(ln_loaded, 32 * cs + (128 * H + 32))
                        for tb in range(4):
                            pool.wait_ge(pool_step2, 8 * cs + (32 * H + 1 + tb))
                            nc.gpsimd.tensor_tensor(z[:, tb, cols], z[:, tb, cols], lng[:], ALU.mult
                                                    ).then_inc(pool_step2, 1)
                        for tb in range(4):
                            pool.wait_ge(pool_step2, 8 * cs + (32 * H + 5 + tb))
                            nc.gpsimd.tensor_tensor(z[:, tb, cols], z[:, tb, cols], lnb[:], ALU.add
                                                    ).then_inc(ln_done, 1)
                        pool.wait_ge(ln_done, n + 4)
                        pool.dma_start(out2[:, 4 * H:4 * H + 4, cols], z[:, :, cols]).then_inc(out_stored, 16)
                pool.wait_ge(out_stored, 128)

            def loads_of(H, n):
                return n // 2 + (TAIL // 2 + 32 * H + 1)

            @block.scalar
            def _(act):
                for q in range(4):
                    act.wait_ge(og_in[q], 32)
                    for r in range(4):
                        k = 4 * q + r
                        if k >= 2:
                            act.wait_ge(og_t, k - 1)
                        nc.scalar.activation(sg[:, k % 2, :], g_in[:, k, :], ACT.Sigmoid).then_inc(og_sig, 1)
                        if k >= 1:
                            act.wait_ge(og_t, k)
                            nc.scalar.copy(og_hi[:, k - 1, :], o_in[:, k - 1, :]).then_inc(og_hi_ready, 1)
                act.wait_ge(og_t, KD)
                nc.scalar.copy(og_hi[:, KD - 1, :], o_in[:, KD - 1, :]).then_inc(og_hi_ready, 1)

                for H in range(2):
                    with act.Fori(0, KD) as nb:
                        c0 = 2 * nb + (TAIL + 64 * H)
                        split_hi(act, c0 + 1, 1, nb + (TAIL // 2 + 32 * H + 1))
                        act.wait_ge(aux_loaded, 32 * nb + (1024 * H + 32))
                        nc.scalar.activation(sg[:], aux[:], ACT.Sigmoid).then_inc(sg_ready, 1)
                        split_hi(act, c0 + 2, 0, nb + (TAIL // 2 + 32 * H + 2))
                        act.wait_ge(t_ready, nb + (KD * H + 1))
                        nc.scalar.copy(mg_hi[:, ds(nb, 1), :].rearrange("p a t -> p (a t)"), ta[:]
                                       ).then_inc(mg_hi_ready, 1)

                    def out_step(cg, last):
                        for kk in range(8):
                            c = 8 * cg + (TAIL + 64 * H + 32 + kk)
                            if not (last and kk == 7):
                                split_hi(act, c + 1, (kk + 1) % 2, 4 * cg + (TAIL // 2 + 32 * H + 17 + (kk + 1) // 2))
                            if H == 0 and kk % 2 == 1:
                                k = 4 * cg + kk // 2
                                act.wait_ge(aux_loaded, 32 * k + (32 * KD + 32))
                                nc.scalar.activation(sg[:, 0, :], aux[:, 1, :], ACT.Sigmoid).then_inc(sg_ready, 1)
                                act.wait_ge(og_t, k + (KD + 1))
                                nc.scalar.copy(og_hi[:, ds(k, 1), :].rearrange("p a t -> p (a t)"), aux[:, 0, :]
                                               ).then_inc(og_hi_ready, 1)

                    with act.Fori(0, 4 - H) as cg:
                        out_step(cg, False)
                    if H == 1:
                        out_step(3, True)
                    act.wait_ge(z_var, H + 1)
                    nc.scalar.activation(z_sm[:, 1, :], z_sm[:, 0, :], ACT.Sqrt).then_inc(z_std, 1)

            @block.vector
            def _(dve):
                own = Steps(dve, dve_step2)
                own.enter()
                for k in range(KD + 1):
                    if k < KD:
                        dve.wait_ge(og_in[k // 4], 32)
                        dve.wait_ge(og_sig, k + 1)
                        own(nc.vector.tensor_tensor(g_in[:, k, :], g_in[:, k, :], sg[:, k % 2, :], ALU.mult))
                        nc.vector.tensor_tensor(o_in[:, k, :], o_in[:, k, :], g_in[:, k, :], ALU.mult
                                                ).then_inc(og_t, 1)
                    if k >= 1:
                        dve.wait_ge(og_hi_ready, k)
                        nc.vector.tensor_tensor(og_lo[:, k - 1, :], o_in[:, k - 1, :],
                                                og_hi[:, k - 1, :].bitcast(F32), ALU.subtract).then_inc(og_ready, 1)
                own.leave(KD)
                for H in range(2):
                    with dve.Fori(0, KD) as nb:
                        c0 = 2 * nb + (TAIL + 64 * H)
                        split_lo(dve, c0 + 1, 1)
                        dve.wait_ge(sg_ready, nb + (32 * H + 1))
                        dve.wait_ge(mg_ready, nb + KD * H)
                        dve.wait_ge(chunk_used, c0 + 1)
                        nc.vector.tensor_tensor(ta[:], yP[:, 0, :], sg[:, 0, :], ALU.mult).then_inc(y_read, 1)
                        split_lo(dve, c0 + 2, 0)
                        dve.wait_ge(chunk_used, c0 + 2)
                        nc.vector.tensor_tensor(tb_[:], yP[:, 1, :], sg[:, 1, :], ALU.mult).then_inc(y_read, 1)
                        dve.wait_ge(y_read, 2 * nb + (2 * KD * H + 3))
                        nc.vector.tensor_tensor(ta[:], ta[:], tb_[:], ALU.add).then_inc(t_ready, 1)
                        dve.wait_ge(mg_hi_ready, nb + (KD * H + 1))
                        nc.vector.tensor_tensor(mg_lo[:, ds(nb, 1), :].rearrange("p a t -> p (a t)"), ta[:],
                                                mg_hi[:, ds(nb, 1), :].bitcast(F32).rearrange("p a t -> p (a t)"),
                                                ALU.subtract).then_inc(mg_ready, 1)

                    def out_step(cg, last):
                        own.enter(4 * cg)
                        for kk in range(8):
                            c = 8 * cg + (TAIL + 64 * H + 32 + kk)
                            if not (last and kk == 7):
                                split_lo(dve, c + 1, (kk + 1) % 2)
                            if H == 0 and kk % 2 == 1:
                                k = 4 * cg + kk // 2
                                dve.wait_ge(sg_ready, k + (KD + 1))
                                nc.vector.tensor_tensor(tb_[:], aux[:, 1, :], sg[:, 0, :], ALU.mult).then_inc(og_g, 1)
                                dve.wait_ge(og_g, k + 1)
                                nc.vector.tensor_tensor(aux[:, 0, :], aux[:, 0, :], tb_[:], ALU.mult).then_inc(og_t, 1)
                                dve.wait_ge(og_hi_ready, k + (KD + 1))
                                nc.vector.tensor_tensor(
                                    og_lo[:, ds(k, 1), :].rearrange("p a t -> p (a t)"), aux[:, 0, :],
                                    og_hi[:, ds(k, 1), :].bitcast(F32).rearrange("p a t -> p (a t)"),
                                    ALU.subtract).then_inc(og_ready, 1)
                        cols = ds(cg * HALF, HALF)
                        dve.wait_ge(gate_loaded2, 16 * cg + (64 * H + 16))
                        dve.wait_ge(z_x, 64 * (H + 1))
                        for tb in range(4):
                            if tb < 3:
                                dve.wait_ge(z_done, 3 * cg + (12 * H + tb + 1))
                            else:
                                dve.wait_ge(chunk_used, 8 * cg + (TAIL + 64 * H + 40))
                            tmp = (ta, tb_)[tb % 2]
                            nc.vector.tensor_tensor(tmp[:], zP[:, tb, :], gate_sl[:], ALU.mult).then_inc(z_read, 1)
                            dve.wait_ge(z_read, 4 * cg + (16 * H + 5 + tb))
                            own(nc.vector.scalar_tensor_tensor(out=z[:, tb, cols], in0=z[:, tb, cols], scalar=ALPHA,
                                                               in1=tmp[:], op0=ALU.mult, op1=ALU.add))
                            nc.vector.bn_stats(z_bn[:, tb, ds(cg, 1), :].rearrange("p a s -> p (a s)"),
                                               z[:, tb, cols]).then_inc(z_added, 1)

                    with dve.Fori(0, 4 - H) as cg:
                        out_step(cg, False)
                    if H == 1:
                        out_step(3, True)
                    own.leave(16, per=4)
                    dve.wait_ge(z_added, 16 * (H + 1))
                    own.enter()
                    for tb in range(4):
                        last = nc.vector.bn_aggr(z_mv[:, tb, :], z_bn[:, tb, :, :].rearrange("p c s -> p (c s)"))
                    own(last)
                    nc.vector.tensor_scalar(z_sm[:, 0, :], z_mv[:, :, 1], LN_EPS, None, ALU.add).then_inc(z_var, 1)
                    dve.wait_ge(z_std, H + 1)
                    r, w = z_sm[:, 2, :], z_sm[:, 3, :]
                    own(nc.vector.reciprocal(r, z_sm[:, 1, :]))
                    own(nc.vector.tensor_tensor(w, r, r, ALU.mult))
                    own(nc.vector.tensor_tensor(w, w, z_sm[:, 0, :], ALU.mult))
                    own(nc.vector.tensor_scalar(w, w, -0.5, 1.5, ALU.mult, ALU.add))
                    nc.vector.tensor_tensor(w, w, r, ALU.mult).then_inc(ln_ready, 1)
                    own.leave(5, per=5)

            @block.tensor
            def _(pe):
                pe.sem_inc(y_read, 1)
                pe.sem_inc(z_read, 4)

                def branch(H, nb, first=False):
                    for br in range(2):
                        pe.wait_ge(chunk_lo, 2 * nb + (TAIL + 64 * H + 1 + br))
                        pe.wait_ge(y_read, 2 * nb + (2 * KD * H + br))
                        for k in range(8):
                            if first:
                                pe.wait_ge(og_ready, 8 * br + k + 1)
                            for part, (w, o) in enumerate(((w_hi, og_hi), (w_hi, og_lo), (w_lo, og_hi))):
                                last = nc.tensor.matmul(yP[:, br, :], w[:, br, k * P:(k + 1) * P], o[:, 8 * br + k, :],
                                                        start=(k == 0 and part == 0), stop=(k == 7 and part == 2))
                        last.then_inc(chunk_used, 1)

                for H in range(2):
                    if H == 0:
                        branch(0, 0, first=True)
                    else:
                        pe.wait_ge(og_ready, 2 * KD)
                    with pe.Fori(1 - H, KD) as nb:
                        branch(H, nb)
                    pe.wait_ge(mg_ready, KD * (H + 1))
                    with pe.Fori(0, 4) as cg:
                        for kk in range(8):
                            c = 8 * cg + (TAIL + 64 * H + 32 + kk)
                            pe.wait_ge(chunk_lo, c + 1)
                            for tb in range(4):
                                if kk == 0:
                                    pe.wait_ge(z_read, 4 * cg + (16 * H + tb + 1))
                                for k2 in range(2):
                                    for part, (m, w) in enumerate(((mg_hi, w_hi), (mg_hi, w_lo), (mg_lo, w_hi))):
                                        last = nc.tensor.matmul(
                                            zP[:, tb, :], m[:, 2 * kk + k2, tb * P:(tb + 1) * P],
                                            w[:, kk % 2, k2 * HALF:(k2 + 1) * HALF],
                                            start=(kk == 0 and k2 == 0 and part == 0),
                                            stop=(kk == 7 and k2 == 1 and part == 2))
                                if kk == 7 and tb < 3:
                                    last.then_inc(z_done, 1)
                            last.then_inc(chunk_used, 1)


_INS = ['x', 'c', 'w_ada', 'b_ada', 'w_in', 'b_f', 'attn_sinks', 'w_br_fox', 'w_br_swa', 'w_out', 'ln_g', 'ln_b']


def kernel(**inputs):
    import numpy as _np
    import concourse.bacc as _bacc
    from concourse import mybir as _mybir
    from concourse.bass_utils import run_bass_kernel_spmd as _run

    nc = _bacc.Bacc("TRN2", target_bir_lowering=False, num_devices=1)
    arrays, args = {}, []
    for name in _INS:
        a = _np.ascontiguousarray(inputs[name])
        arrays[f"in_{name}_dram"] = a
        args.append(nc.dram_tensor(f"in_{name}_dram", a.shape, _mybir.dt.from_np(a.dtype), kind="ExternalInput").ap())
    out = nc.dram_tensor("out_dram", inputs["x"].shape, F32, kind="ExternalOutput").ap()
    build(nc, *args, out)
    r = _run(nc, [arrays], core_ids=[0])
    return r.results[0]["out_dram"]
```

```python
from contextlib import ExitStack

import concourse.bass as bass
from concourse import mybir

F32 = mybir.dt.float32
F32R = mybir.dt.float32r
ALU = mybir.AluOpType
ACT = mybir.ActivationFunctionType
AX = mybir.AxisListType
ds = bass.ds

P = 128
D = 2048
SEQ = 1024
HALF = 512
KD = D // P
FOX_HEADS = 8
FOX_WIDTH = 1024
SWA_HEADS = 16
SWA_KV = 4
SWA_D = 64
SWA_WIDTH = 1024
LN_EPS = 1e-5
NEG = -1e30
FAR = 1e34
ALPHA = 2.0 ** 0.25

COL_FLOG = 3 * FOX_WIDTH
COL_REST = COL_FLOG + FOX_HEADS
B_SQ = 1
B_SK = B_SQ + SWA_WIDTH // P
B_SV = B_SK + SWA_KV * SWA_D // P
B_FQ = B_SV + SWA_KV * SWA_D // P
B_FK = B_FQ + FOX_WIDTH // P
B_FV = B_FK + FOX_WIDTH // P
B_G = B_FV + FOX_WIDTH // P
B_M = B_G + (FOX_WIDTH + SWA_WIDTH) // P
BLOCKS = B_M + 2 * D // P
ADA_DVE = 6
MMS = 48
OG_ORDER = [*range(8, KD), *range(8)]
OG_GROUPS = [(0, 2), (2, 4), (4, 8), (8, 12), (12, 16)]
TAIL = 2 * BLOCKS


class Steps:

    def __init__(self, eng, sem):
        self.eng, self.sem, self.total, self.base, self.n = eng, sem, 0, 0, 0

    def enter(self, before=0):
        self.base, self.n = self.total + before, 0

    def leave(self, steps, times=1, per=None):
        assert self.n == (steps // times if per is None else per), (self.n, steps, times)
        self.total += steps

    def __call__(self, ins):
        self.n += 1
        ins.then_inc(self.sem, 1)
        self.eng.wait_ge(self.sem, self.base + self.n)


def build(nc, x, c, w_ada, b_ada, w_in, b_f, attn_sinks, w_br_fox, w_br_swa, w_out, ln_g, ln_b, out):
    x2 = x.rearrange("a (t p) d -> p (a t) d", p=P)
    out2 = out.rearrange("a (t p) d -> p (a t) d", p=P)
    ada_v = w_ada.rearrange("a (p k) n -> p (a k) n", p=P)
    w_in_v = w_in.rearrange("a (k p) n -> p (a k) n", p=P)
    wbf_v = w_br_fox.rearrange("a (k p) n -> p (a k) n", p=P)
    wbs_v = w_br_swa.rearrange("a (k p) n -> p (a k) n", p=P)
    w_out_v = w_out.rearrange("a (k p) n -> p (a k) n", p=P)

    proj_d = nc.dram_tensor("proj_scratch", (BLOCKS, P, SEQ), F32).ap()
    o_d = nc.dram_tensor("o_scratch", (KD, P, SEQ), F32).ap()
    gate_d = nc.dram_tensor("gate_scratch", (1, D), F32).ap()
    q_heads = proj_d[B_SQ:B_SK].rearrange("b (e d) t -> d (b e) t", d=SWA_D)
    o_heads = o_d[FOX_HEADS:KD].rearrange("b (e d) t -> d (b e) t", d=SWA_D)

    ctx = ExitStack()
    with ctx:
        def sem(name):
            return ctx.enter_context(nc.semaphore(name))

        def psum(name, shape):
            return ctx.enter_context(nc.psum_tensor(name, shape, F32))

        def sb(name, shape, dt=F32, scope=ctx):
            return scope.enter_context(nc.sbuf_tensor(name, shape, dt))

        w_raw = sb("w_raw", [P, 2, 1024])
        w_hi = sb("w_hi", [P, 2, 1024], F32R)
        w_lo = sb("w_lo", [P, 2, 1024], F32R)
        chunk_loaded = [sem("chunk_loaded_0"), sem("chunk_loaded_1")]
        chunk_hi = sem("chunk_hi")
        chunk_lo = sem("chunk_lo")
        chunk_used = sem("chunk_used")
        dve_step = sem("dve_step")
        act_step = sem("act_step")

        def load_chunk(sp, n, slot, source, first=False):
            if not first:
                sp.wait_ge(chunk_lo, n - 1)
            dst = w_raw[:, slot, :].rearrange("p (k n) -> p k n", k=source.shape[1])
            sp.dma_start(dst, source).then_inc(chunk_loaded[slot], 16)

        def split_hi(act, n, slot, loads):
            act.wait_ge(chunk_loaded[slot], 16 * loads)
            if not (isinstance(n, int) and n < 2):
                act.wait_ge(chunk_used, n - 1)
            nc.scalar.copy(w_hi[:, slot, :], w_raw[:, slot, :]).then_inc(chunk_hi, 1)

        def split_lo(dve, n, slot):
            dve.wait_ge(chunk_hi, n + 1)
            nc.vector.tensor_tensor(w_lo[:, slot, :], w_raw[:, slot, :], w_hi[:, slot, :].bitcast(F32),
                                    ALU.subtract).then_inc(chunk_lo, 1)

        def load_og(sp, q):
            n0, n1 = OG_GROUPS[q]
            k0 = OG_ORDER[n0]
            for half, (src, base) in enumerate(((proj_d, B_G), (o_d, 0))):
                sp.dma_start(go_in[:, n0:n1, half, :],
                             src[base + k0:base + k0 + n1 - n0, :, 0:HALF].rearrange("k p t -> p k t")
                             ).then_inc(og_in[q], 16)

        main = ExitStack()
        with main:
            psums = ExitStack()
            main.enter_context(psums)

            def pst(name, shape):
                return psums.enter_context(nc.psum_tensor(name, shape, F32))

            projP = pst("projP", [P, 2, HALF])
            sP = pst("sP", [P, 2, HALF])
            tP = pst("tP", [P, 2, HALF])
            oP = pst("oP", [P, HALF])
            adaP = pst("adaP", [P, HALF])

            with ExitStack() as x_scope:
                x_t = sb("x_t", [P, 2, D], F32, x_scope)
            h_hi = sb("h_hi", [P, KD, SEQ], F32R, main)
            with ExitStack() as before_h_lo:
                xnT = sb("xnT", [P, KD, SEQ], F32, before_h_lo)
            with ExitStack() as after_h_lo:
                go_in = sb("go_in", [P, KD, 2, HALF], F32, after_h_lo)
            h_lo = sb("h_lo", [P, KD, SEQ], F32R, main)
            stage = sb("stage", [P, 2, HALF], F32, main)
            ident = sb("ident", [P, P], F32, main)
            ident_r = sb("ident_r", [P, P], F32R, main)
            mask_r = sb("mask_r", [P, P], F32R, main)
            cum_k = sb("cum_k", [P, SEQ], F32R, main)
            cum_q = sb("cum_q", [P, SEQ], F32R, main)
            head_sel = sb("head_sel", [P, FOX_HEADS], F32, main)
            c_sb = sb("c_sb", [P, KD + 1], F32, main)
            neg_max = sb("neg_max", [P, 4], F32, main)
            row_sum = sb("row_sum", [P, 4], F32, main)
            row_inv = sb("row_inv", [P, 4], F32, main)
            sink_exp = sb("sink_exp", [P, 4], F32, main)

            with ExitStack() as s0:
                ada_raw = sb("ada_raw", [P, 2, KD, 2, P], F32, s0)
                ada_rows = sb("ada_rows", [2 * KD, P], F32, s0)
                ada_b = sb("ada_b", [P, 2, KD], F32, s0)
                ada_s = sb("ada_s", [P, KD, 2], F32, s0)
                ada_acc = sb("ada_acc", [P, 2, 2 * P], F32, s0)
                ada_row = sb("ada_row", [1, 2, 2 * P], F32, s0)
                bn = sb("bn", [P, 4, 6], F32, s0)
                mv = sb("mv", [P, 2], F32, s0)
                sm = sb("sm", [P, 4], F32, s0)
            with ExitStack() as s1:
                gate_raw = sb("gate_raw", [P, D], F32, s1)
                gate_acc = sb("gate_acc", [P, D], F32, s1)
                fg = [sb(f"fg{i}", [FOX_HEADS, SEQ], F32, s1) for i in range(5)]
                bf_c = sb("bf_c", [FOX_HEADS, 1], F32, s1)
                ones = sb("ones", [P, 1], F32, s1)
            gate_row = gate_raw[0:1, :]
            with ExitStack() as s2:
                sq_raw = sb("sq_raw", [P, 2, 4, P], F32, s2)
                sk_raw = sb("sk_raw", [P, 2, P], F32, s2)
                sv_raw = sb("sv_raw", [P, 2, P], F32, s2)
                sq_hi = sb("sq_hi", [P, 4, P], F32R, s2)
                sq_lo = sb("sq_lo", [P, 4, P], F32R, s2)
                sk_hi = sb("sk_hi", [P, 2, P], F32R, s2)
                sk_lo = sb("sk_lo", [P, 2, P], F32R, s2)
                sv_hi = sb("sv_hi", [P, 2, 2, P], F32R, s2)
                sv_lo = sb("sv_lo", [P, 2, 2, P], F32R, s2)
                s_bias = sb("s_bias", [P, 2, 4, 2, P], F32, s2)
                dist = sb("dist", [P, 2, P], F32, s2)
                no_prev = sb("no_prev", [P, 4], F32, s2)
                sinks = sb("sinks", [P, SWA_HEADS], F32, s2)
                neg_sinks = sb("neg_sinks", [P, SWA_HEADS], F32, s2)
                sp_w = sb("sp_w", [P, 4, 2, P], F32, s2)
                spT_hi = sb("spT_hi", [P, 2, 4 * P], F32R, s2)
                spT_lo = sb("spT_lo", [P, 2, 4 * P], F32R, s2)
                so_st = sb("so_st", [P, 4, P], F32, s2)
            with ExitStack() as s3:
                fq_raw = sb("fq_raw", [P, 2, P], F32, s3)
                fv_raw = sb("fv_raw", [P, SEQ], F32, s3)
                fk_raw = sb("fk_raw", [P, SEQ], F32, s3)
                fq_hi = sb("fq_hi", [P, P], F32R, s3)
                fq_lo = sb("fq_lo", [P, P], F32R, s3)
                fk_hi = sb("fk_hi", [P, SEQ], F32R, s3)
                fk_lo = sb("fk_lo", [P, SEQ], F32R, s3)
                fv_hi = sb("fv_hi", [P, 8, P], F32R, s3)
                fv_lo = sb("fv_lo", [P, 8, P], F32R, s3)
                fcq = sb("fcq", [P, P], F32R, s3)
                fp_w = sb("fp_w", [P, 8, P], F32, s3)
                fpT = sb("fpT", [P, 8, 2, P], F32R, s3)
                fo_st = sb("fo_st", [P, P], F32, s3)

            og_in = [sem(f"og_in_{q}") for q in range(len(OG_GROUPS))]
            x_loaded = [sem("x_loaded_0"), sem("x_loaded_1")]
            x_normed = sem("x_normed")
            x_var = sem("x_var")
            x_std = sem("x_std")
            x_turned = sem("x_turned")
            xt_copied = sem("xt_copied")
            ada_loaded = [sem("ada_loaded_0"), sem("ada_loaded_1")]
            ada_done = sem("ada_done")
            small_loaded = sem("small_loaded")
            mod_ready = sem("mod_ready")
            ada_summed = sem("ada_summed")
            ada_row_ready = sem("ada_row_ready")
            ada_turned = sem("ada_turned")
            ada_b_ready = sem("ada_b_ready")
            c_one = sem("c_one")
            c_loaded = sem("c_loaded")
            x_stats = sem("x_stats")
            ada_b_turned = sem("ada_b_turned")
            ada_read = sem("ada_read")
            s_scaled = sem("s_scaled")
            h_hi_ready = sem("h_hi_ready")
            h_ready = sem("h_ready")
            consts = sem("consts")
            pool_step = sem("pool_step")
            ident_ready = sem("ident_ready")
            half0_done = sem("half0_done")
            proj_copied = sem("proj_copied")
            proj_stored = [sem("proj_stored_0"), sem("proj_stored_1")]
            gate_loaded = sem("gate_loaded")
            gate_added = sem("gate_added")
            gate_summed = sem("gate_summed")
            gate_ready = sem("gate_ready")
            gate_stored = sem("gate_stored")
            fg_loaded = sem("fg_loaded")
            fg_neg = sem("fg_neg")
            fg_exp = sem("fg_exp")
            cum_done = sem("cum_done")
            cum_hi = sem("cum_hi")
            cum_ready = sem("cum_ready")
            s_loaded = [sem("s_loaded_0"), sem("s_loaded_1")]
            s_hi = sem("s_hi")
            s_prep = sem("s_prep")
            s_vt = sem("s_vt")
            s_vt_hi = sem("s_vt_hi")
            s_v = sem("s_v")
            s_qk = sem("s_qk")
            s_biased = sem("s_biased")
            s_max = sem("s_max")
            s_exp = sem("s_exp")
            s_inv = sem("s_inv")
            s_norm = sem("s_norm")
            s_turned = sem("s_turned")
            s_pt_hi = sem("s_pt_hi")
            s_pt = sem("s_pt")
            s_pv = sem("s_pv")
            s_o = sem("s_o")
            s_stored = sem("s_stored")
            f_q_loaded = [sem("f_q_loaded_0"), sem("f_q_loaded_1")]
            f_kv_loaded = sem("f_kv_loaded")
            f_k_hi = sem("f_k_hi")
            f_k = sem("f_k")
            f_vt = sem("f_vt")
            f_vt_hi = sem("f_vt_hi")
            f_v = sem("f_v")
            f_q_hi = sem("f_q_hi")
            f_q = sem("f_q")
            f_qk = sem("f_qk")
            f_max = sem("f_max")
            f_exp = sem("f_exp")
            f_inv = sem("f_inv")
            f_norm = sem("f_norm")
            f_turned = sem("f_turned")
            f_pt_hi = sem("f_pt_hi")
            f_pt = sem("f_pt")
            f_pv = sem("f_pv")
            f_half = sem("f_half")
            f_o = sem("f_o")
            f_stored = sem("f_stored")

            block = main.enter_context(nc.Block())

            def col_rest(b):
                return COL_REST + P * (b - 1) - P * (B_G - B_FQ)

            @block.sync
            def _(sp):
                def load_ada(j, slot):
                    for s in range(2):
                        sp.dma_start(ada_raw[:, slot, :, s, :],
                                     ada_v[:, :, ds(s * D + j * P, P)]).then_inc(ada_loaded[slot], 16)

                sp.dma_start(x_t[:, 0, :], x2[:, 0, :]).then_inc(x_loaded[0], 16)
                sp.dma_start(c_sb[:, 0:KD], c.rearrange("a (p k) -> p (a k)", p=P)).then_inc(c_loaded, 16)
                sp.dma_start(ada_rows[:], b_ada[0, 0:2 * D].rearrange("(r p) -> r p", p=P)).then_inc(c_loaded, 16)
                load_ada(0, 0)
                sp.dma_start(x_t[:, 1, :], x2[:, 1, :]).then_inc(x_loaded[1], 16)
                load_ada(1, 1)
                with sp.Fori(1, 4) as g:
                    for t in range(2):
                        sp.wait_ge(ada_done, 2 * g + (t - 1))
                        load_ada(2 * g + t, t)
                        sp.wait_ge(x_turned, 4 * (2 * g + (t - 1)))
                        sp.dma_start(x_t[:, t, :], x2[:, ds(2 * g + t, 1), :]
                                     .rearrange("p a d -> p (a d)")).then_inc(x_loaded[t], 16)

                def block_in(b, col, first=False):
                    for kh in range(2):
                        load_chunk(sp, 2 * b + kh, kh, w_in_v[:, 8 * kh:8 * kh + 8, ds(col, P)], first)

                block_in(0, COL_FLOG, first=True)
                with sp.Fori(4, KD // 2) as g:
                    for t in range(2):
                        sp.wait_ge(ada_done, 2 * g + (t - 1))
                        load_ada(2 * g + t, t)
                with sp.Fori(B_SQ, B_FQ) as b:
                    block_in(b, COL_REST + P * (b - 1))
                for s in range(2):
                    sp.wait_ge(proj_stored[s], 16)
                sp.dma_start(fg[0][:], proj_d[0, 0:FOX_HEADS, :]).then_inc(fg_loaded, 16)
                sp.dma_start(bf_c[:], b_f.rearrange("a h -> h a"), allow_slow_non_contiguous=True).then_inc(fg_loaded, 16)
                sp.wait_ge(consts, 1)
                with sp.Fori(0, KD) as k:
                    block_in(k + B_FQ, P * k)
                    sp.wait_ge(gate_added, k + 1)
                    sp.dma_start(gate_raw[:], ada_v[:, ds(k, 1), 2 * D:3 * D]
                                 .rearrange("p a n -> p (a n)")).then_inc(gate_loaded, 16)
                sp.wait_ge(gate_added, KD)
                block_in(B_FQ + KD, P * KD)
                sp.wait_ge(gate_added, KD + 1)
                sp.dma_start(gate_row, b_ada[:, 2 * D:3 * D]).then_inc(gate_loaded, 16)
                with sp.Fori(B_FQ + KD + 1, B_G) as b:
                    block_in(b, P * (b - B_FQ))

                sp.sem_inc(s_v, 2)
                for s in range(2):
                    sp.wait_ge(proj_stored[s], 16 * B_FQ)
                with sp.Fori(0, 2) as g:
                    with sp.Fori(0, 4) as m:
                        for par in range(2):
                            u = 8 * g + 2 * m + par
                            block_in(u + B_G, COL_REST + P * (u + (B_FQ - 1)))
                            sp.wait_ge(s_v, u + 1)
                            if par == 0:
                                sp.wait_ge(gate_stored, 16)
                                sp.wait_ge(cum_ready, 2)
                            t0 = (2 * m + par) * P
                            for e in range(2):
                                sp.dma_start(sq_raw[SWA_D * e:SWA_D * (e + 1), par],
                                             q_heads[:, ds(8 * g + 4 * e, 4), ds(t0, P)]
                                             ).then_inc(s_loaded[par], 16)
                            for base, dst in ((B_SK, sk_raw), (B_SV, sv_raw)):
                                sp.dma_start(dst[:, par, :], proj_d[ds(g + base, 1), :, ds(t0, P)]
                                             .rearrange("a p t -> p (a t)")).then_inc(s_loaded[par], 16)

                sp.sem_inc(f_q, 2)
                for s in range(2):
                    sp.wait_ge(proj_stored[s], 16 * B_G)
                with sp.Fori(0, FOX_HEADS) as h:
                    for i in range(8):
                        if i % 2 == 0:
                            block_in(4 * h + (B_M + i // 2), 4 * P * h + (col_rest(B_M) + P * (i // 2)))
                        if i == 0:
                            sp.wait_ge(s_v, 16 + 2)
                            sp.wait_ge(s_qk, 32 + 1)
                            sp.wait_ge(f_k, h + 1)
                            sp.wait_ge(f_vt, h + 1)
                            for base, dst in ((B_FK, fk_raw), (B_FV, fv_raw)):
                                sp.dma_start(dst[:], proj_d[ds(h + base, 1), :, :]
                                             .rearrange("a p t -> p (a t)")).then_inc(f_kv_loaded, 16)
                        sp.wait_ge(f_q, 8 * h + (i + 1))
                        sp.dma_start(fq_raw[:, i % 2, :], proj_d[ds(h + B_FQ, 1), :, i * P:(i + 1) * P]
                                     .rearrange("a p t -> p (a t)")).then_inc(f_q_loaded[i % 2], 16)
                load_chunk(sp, TAIL, 0, wbs_v[:, :, 0:P])
                sp.wait_ge(chunk_used, TAIL - 1)
                sp.wait_ge(s_stored, 512 + 1)
                load_og(sp, 0)
                load_og(sp, 1)
                load_chunk(sp, TAIL + 1, 1, wbs_v[:, :, P:2 * P])
                load_og(sp, 2)

            @block.gpsimd
            def _(pool):
                own = Steps(pool, pool_step)
                for signal in (gate_added, s_qk, s_biased, s_pt, s_o, s_stored, f_k, f_vt, f_qk, f_exp, f_pt, f_o,
                               f_stored):
                    pool.sem_inc(signal, 1)
                own.enter()
                own(nc.gpsimd.memset(ident[:], 0.0))
                nc.gpsimd.affine_select(out=ident[:], in_=ident[:], compare_op=ALU.not_equal, fill=1.0, base=0,
                                        pattern=[[-1, P]], channel_multiplier=1).then_inc(ident_ready, 1)
                own(nc.gpsimd.memset(head_sel[:], 0.0))
                for q in range(4):
                    own(nc.gpsimd.affine_select(out=head_sel[:], in_=head_sel[:], compare_op=ALU.not_equal, fill=1.0,
                                                base=-32 * q, pattern=[[-1, FOX_HEADS]], channel_multiplier=1))
                pool.wait_ge(h_ready, KD)
                own(nc.gpsimd.memset(gate_raw[:, 0:P], 0.0))
                own(nc.gpsimd.affine_select(out=gate_raw[:, 0:P], in_=gate_raw[:, 0:P], compare_op=ALU.is_ge,
                                            fill=NEG, base=0, pattern=[[-1, P]], channel_multiplier=1))
                own(nc.gpsimd.tensor_copy(mask_r[:], gate_raw[:, 0:P]))
                pool.wait_ge(ident_ready, 1)
                own(nc.gpsimd.tensor_copy(ident_r[:], ident[:]))
                for t in (cum_k, cum_q):
                    own(nc.gpsimd.memset(t[:].bitcast(F32), 0.0))
                for t, q in ((cum_q, 0), (cum_q, 32), (cum_k, 64), (cum_k, 96)):
                    own(nc.gpsimd.memset(t[q:q + FOX_HEADS, :].bitcast(F32), 1.0))
                own(nc.gpsimd.memset(ones[:], 1.0))
                nc.gpsimd.memset(gate_acc[:], 0.0).then_inc(consts, 1)

                pool.wait_ge(gate_stored, 16)
                pool.wait_ge(cum_ready, 2)
                for t in (sv_hi, sv_lo, sk_hi, sk_lo):
                    own(nc.gpsimd.memset(t[:].bitcast(F32), 0.0))
                own(nc.gpsimd.memset(no_prev[:], 0.0))
                own(nc.gpsimd.memset(no_prev[:, 0:1], NEG))
                pool.dma_start(sinks[:], attn_sinks.broadcast_to([P, SWA_HEADS])).then_inc(small_loaded, 16)
                own(nc.gpsimd.iota(dist[:], pattern=[[-P, 2], [-1, P]], base=P, channel_multiplier=1,
                                   allow_small_or_imprecise_dtypes=True))
                own(nc.gpsimd.affine_select(out=dist[:, 1, :], in_=dist[:, 1, :], compare_op=ALU.is_ge, fill=FAR,
                                            base=0, pattern=[[-1, P]], channel_multiplier=1))
                nc.gpsimd.affine_select(out=dist[:, 0, :], in_=dist[:, 0, :], compare_op=ALU.is_gt, fill=FAR,
                                        base=0, pattern=[[1, P]], channel_multiplier=-1).then_inc(consts, 1)
                with pool.Fori(0, 32) as s:
                    pool.wait_ge(s_inv, s + 1)
                    for i in range(4):
                        w = sp_w[:, i].rearrange("p k t -> p (k t)")
                        last = nc.gpsimd.tensor_tensor(w, w, row_inv[:, i:i + 1].broadcast_to([P, 2 * P]), ALU.mult)
                    last.then_inc(s_norm, 1)
                with pool.Fori(0, FOX_HEADS) as h:
                    for i in range(8):
                        pool.wait_ge(f_inv, 8 * h + (i + 1))
                        w = fp_w[:, 0:i + 1].rearrange("p j t -> p (j t)")
                        nc.gpsimd.tensor_tensor(w, w, row_inv[:, 0:1].broadcast_to([P, (i + 1) * P]),
                                                ALU.mult).then_inc(f_norm, 1)

            @block.scalar
            def _(act):
                def ada_row_out(j, slot, first=False):
                    act.wait_ge(ada_done, j + 1)
                    if not first:
                        act.wait_ge(ada_turned, j - 1)
                    nc.scalar.copy(ada_row[:, slot, :], (adaP if slot else oP)[0:1, 0:2 * P]
                                   ).then_inc(ada_row_ready, 1)

                def x_step(t, slot, first=False):
                    act.wait_ge(x_var, t + 1)
                    nc.scalar.activation(sm[:, 1:2], sm[:, 0:1], ACT.Sqrt).then_inc(x_std, 1)
                    ada_row_out(t, slot, first)
                    for q in range(4):
                        act.wait_ge(x_turned, 4 * t + (q + 1))
                        nc.scalar.copy(xnT[:, 4 * q:4 * q + 4, ds(t * P, P)],
                                       (sP if q < 2 else tP)[:, q % 2, :].rearrange("p (j t) -> p j t", j=4)
                                       ).then_inc(xt_copied, 1)

                def modulate(j):
                    act.wait_ge(ada_read, j + 1)
                    nc.scalar.activation(xnT[:, ds(j, 1), :], xnT[:, ds(j, 1), :], ACT.Identity,
                                         bias=ada_s[:, ds(j, 1), 0:1].rearrange("p a s -> p (a s)"),
                                         scale=ada_s[:, ds(j, 1), 1:2].rearrange("p a s -> p (a s)")
                                         ).then_inc(mod_ready, 1)
                    act.wait_ge(mod_ready, j + 1)
                    nc.scalar.copy(h_hi[:, ds(j, 1), :], xnT[:, ds(j, 1), :]).then_inc(h_hi_ready, 1)

                for slot in range(2):
                    x_step(slot, slot, first=True)
                with act.Fori(1, 4) as g:
                    for slot in range(2):
                        x_step(2 * g + slot, slot)
                for e in range(2):
                    split_hi(act, e, e, 1)
                act.wait_ge(xt_copied, 32)
                with act.Fori(4, 7) as g:
                    for slot in range(2):
                        j = 2 * g + slot
                        modulate(2 * (j - 8))
                        modulate(2 * (j - 8) + 1)
                        ada_row_out(j, slot)
                for slot in range(2):
                    modulate(KD - 4 + slot)
                    ada_row_out(KD - 2 + slot, slot)
                modulate(KD - 2)
                modulate(KD - 1)

                def copy_proj(b, half):
                    if half == 0:
                        act.wait_ge(half0_done, b + 1)
                    else:
                        act.wait_ge(chunk_used, 2 * b + 2)
                    if not (isinstance(b, int) and b == 0):
                        act.wait_ge(proj_stored[half], 16 * b)
                    nc.scalar.copy(stage[:, half, :], projP[:, half, :]).then_inc(proj_copied, 1)
                    act.wait_ge(proj_copied, 2 * b + (half + 1))
                    dst = proj_d[ds(b, 1), :, half * HALF:(half + 1) * HALF].rearrange("a p t -> p (a t)")
                    act.dma_start(dst, stage[:, half, :]).then_inc(proj_stored[half], 16)

                def proj_step(b, first=False):
                    if not first:
                        split_hi(act, 2 * b + 1, 1, b + 1)
                    split_hi(act, 2 * b + 2, 0, b + 2)
                    copy_proj(b, 0)
                    copy_proj(b, 1)

                proj_step(0, first=True)
                with act.Fori(B_SQ, B_FQ) as b:
                    proj_step(b)
                act.wait_ge(fg_neg, 1)
                nc.scalar.activation(fg[2][:], fg[1][:], ACT.Exp).then_inc(fg_exp, 1)
                with act.Fori(B_FQ, B_FQ + KD) as b:
                    proj_step(b)
                act.wait_ge(cum_done, 1)
                nc.scalar.activation(cum_k[0:FOX_HEADS, :], fg[4][:], ACT.Copy, scale=-1.0).then_inc(cum_hi, 1)
                nc.scalar.copy(cum_q[64:64 + FOX_HEADS, :], fg[4][:]).then_inc(cum_hi, 1)
                proj_step(B_FQ + KD)
                act.wait_ge(gate_ready, 1)
                act.dma_start(gate_d, gate_row).then_inc(gate_stored, 16)
                with act.Fori(B_FQ + KD + 1, B_G) as b:
                    proj_step(b)

                def high_parts(slot, loads, u):
                    act.wait_ge(s_loaded[slot], 64 * loads)
                    act.wait_ge(s_qk, 2 * u + 1)
                    nc.scalar.activation(sq_hi[:], sq_raw[:, slot], ACT.Copy, scale=SWA_D ** -0.5)
                    nc.scalar.copy(sk_hi[:, slot, :], sk_raw[:, slot, :]).then_inc(s_hi, 1)

                def unit(g, m, par, last=False):
                    u = 8 * g + 2 * m + par
                    b = u + B_G
                    act.wait_ge(s_vt, u + 1)
                    nc.scalar.copy(sv_hi[:, par, 0, 0:SWA_D], tP[:, 0, 0:SWA_D])
                    nc.scalar.copy(sv_hi[:, par, 1, SWA_D:P], tP[:, 0, SWA_D:P]).then_inc(s_vt_hi, 1)
                    for e in range(2):
                        s = 2 * u + e
                        split_hi(act, 2 * b + (e + 1), 1 - e, b + (e + 1))
                        act.wait_ge(s_max, s + 1)
                        for i in range(4):
                            nc.scalar.activation(sp_w[:, i], sp_w[:, i], ACT.Exp, bias=neg_max[:, i:i + 1],
                                                 accum_out=row_sum[:, i:i + 1])
                        nc.scalar.activation(sink_exp[:], sink_exp[:], ACT.Exp).then_inc(s_exp, 1)
                        if e == 1:
                            copy_proj(b, 0)
                        for k in range(2):
                            act.wait_ge(s_turned, 2 * s + (k + 1))
                            nc.scalar.copy(spT_hi[:, k, :], tP[:, k, :]).then_inc(s_pt_hi, 1)
                    if not last:
                        high_parts(1 - par, 4 * g + m + (par + 1), u + 1)
                    copy_proj(b, 1)
                    act.wait_ge(s_pv, u + 1)
                    act.wait_ge(s_stored, 32 * u + 1)
                    nc.scalar.copy(so_st[:], oP[:, :].rearrange("p (i t) -> p i t", i=4)).then_inc(s_o, 1)
                    act.wait_ge(s_o, u + 2)
                    for e in range(2):
                        act.dma_start(o_heads[:, ds(8 * g + 4 * e, 4), ds((2 * m + par) * P, P)],
                                      so_st[SWA_D * e:SWA_D * (e + 1)]).then_inc(s_stored, 16)

                act.wait_ge(consts, 2)
                high_parts(0, 1, 0)
                for g in range(2):
                    with act.Fori(0, 4 - g) as m:
                        unit(g, m, 0)
                        unit(g, m, 1)
                unit(1, 3, 0)
                unit(1, 3, 1, last=True)

                with act.Fori(0, FOX_HEADS) as h:
                    def q_high(i):
                        act.wait_ge(f_q_loaded[i % 2], 64 * h + 16 * (i // 2 + 1))
                        act.wait_ge(f_qk, 8 * h + i + 1)
                        nc.scalar.activation(fq_hi[:], fq_raw[:, i % 2, :], ACT.Copy,
                                             scale=float(P) ** -0.5).then_inc(f_q_hi, 1)

                    q_high(0)
                    act.wait_ge(f_kv_loaded, 32 * h + 32)
                    nc.scalar.copy(fk_hi[:], fk_raw[:]).then_inc(f_k_hi, 1)
                    act.wait_ge(f_vt, h + 2)
                    for k in range(2):
                        last = nc.scalar.copy(fv_hi[:, 4 * k:4 * k + 4, :],
                                              tP[:, k, :].rearrange("p (j t) -> p j t", j=4))
                    last.then_inc(f_vt_hi, 1)
                    turned = 0
                    for i in range(8):
                        b = 4 * h + (B_M + i // 2)
                        e = i % 2
                        split_hi(act, 2 * b + (e + 1), 1 - e, b + (e + 1))
                        act.wait_ge(f_max, 8 * h + (i + 1))
                        nc.scalar.activation(fp_w[:, 0:i + 1, :].rearrange("p j t -> p (j t)"),
                                             sP[:, :, :].rearrange("p a t -> p (a t)")[:, 0:(i + 1) * P], ACT.Exp,
                                             bias=neg_max[:, 0:1], accum_out=row_sum[:, 0:1]).then_inc(f_exp, 1)
                        if e == 1:
                            copy_proj(b, 0)
                        for k in range(i // 4 + 1):
                            turned += 1
                            n = min(4, i + 1 - 4 * k)
                            act.wait_ge(f_turned, 12 * h + turned)
                            nc.scalar.copy(fpT[:, 4 * k:4 * k + n, 0, :],
                                           tP[:, k, 0:n * P].rearrange("p (j t) -> p j t", j=n)).then_inc(f_pt_hi, 1)
                        if i < 7:
                            q_high(i + 1)
                        if e == 1:
                            copy_proj(b, 1)
                        act.wait_ge(f_pv, 8 * h + (i + 1))
                        act.wait_ge(s_stored, 512 + 1)
                        act.wait_ge(f_stored, 128 * h + 16 * i + 1)
                        nc.scalar.copy(fo_st[:], oP[:, 0:P]).then_inc(f_half, 1)
                        act.wait_ge(f_o, 8 * h + (i + 2))
                        act.dma_start(o_d[ds(h, 1), :, i * P:(i + 1) * P].rearrange("a p t -> p (a t)"),
                                      fo_st[:]).then_inc(f_stored, 16)

            @block.vector
            def _(dve):
                own = Steps(dve, dve_step)
                nc.vector.memset(c_sb[:, KD:KD + 1], 1.0).then_inc(c_one, 1)
                dve.wait_ge(ada_b_turned, 1)
                nc.vector.tensor_copy(ada_b[:, 0, :], projP[:, 0, 0:KD])
                nc.vector.tensor_scalar(ada_b[:, 1, :], projP[:, 0, KD:2 * KD], 1.0, None, ALU.add
                                        ).then_inc(ada_b_ready, 1)
                dve.wait_ge(ada_b_ready, 1)

                def ada_sum(slot, loads):
                    dve.wait_ge(ada_loaded[slot], 32 * loads)
                    w = ada_raw[:, slot].rearrange("p k s n -> p k (s n)")
                    a = ada_acc[:, slot, :]
                    own(nc.vector.tensor_scalar(a, w[:, 0, :], c_sb[:, 0:1], None, ALU.mult))
                    for k in range(1, ADA_DVE):
                        ins = nc.vector.scalar_tensor_tensor(out=a, in0=w[:, k, :], scalar=c_sb[:, k:k + 1], in1=a,
                                                             op0=ALU.mult, op1=ALU.add)
                        if k < ADA_DVE - 1:
                            own(ins)
                    ins.then_inc(ada_summed, 1)

                def ada_take(j, slot):
                    dve.wait_ge(ada_turned, j + 1)
                    nc.vector.tensor_tensor(ada_s[:, ds(j, 1), :].rearrange("p a s -> p (a s)"),
                                            projP[:, slot, 0:2],
                                            ada_b[:, :, ds(j, 1)].rearrange("p s a -> p (s a)"),
                                            ALU.add).then_inc(ada_read, 1)

                def x_step(t, slot, loads, first=False):
                    dve.wait_ge(x_loaded[slot], 16 * loads)
                    for q in range(4):
                        last = nc.vector.bn_stats(bn[:, q, :], x_t[:, slot, q * HALF:(q + 1) * HALF])
                    last.then_inc(x_stats, 1)
                    dve.wait_ge(x_stats, t + 1)
                    nc.vector.memset(sm[:, 2:3], 0.0)
                    own(nc.vector.bn_aggr(mv[:], bn[:].rearrange("p a b -> p (a b)")))
                    nc.vector.tensor_scalar(sm[:, 0:1], mv[:, 1:2], LN_EPS, None, ALU.add).then_inc(x_var, 1)
                    if first and slot == 0:
                        dve.wait_ge(c_loaded, 32)
                    ada_sum(slot, loads)
                    if not first:
                        ada_take(t - 2, slot)
                    dve.wait_ge(x_std, t + 1)
                    own(nc.vector.reciprocal(sm[:, 2:3], sm[:, 1:2]))
                    own(nc.vector.tensor_tensor(sm[:, 3:4], sm[:, 2:3], sm[:, 2:3], ALU.mult))
                    own(nc.vector.tensor_tensor(sm[:, 3:4], sm[:, 3:4], sm[:, 0:1], ALU.mult))
                    own(nc.vector.tensor_scalar(sm[:, 3:4], sm[:, 3:4], -0.5, 1.5, ALU.mult, ALU.add))
                    own(nc.vector.tensor_tensor(sm[:, 3:4], sm[:, 3:4], sm[:, 2:3], ALU.mult))
                    nc.vector.tensor_scalar(x_t[:, slot, :], x_t[:, slot, :], mv[:, 0:1], sm[:, 3:4],
                                            ALU.subtract, ALU.mult).then_inc(x_normed, 1)
                    dve.wait_ge(x_normed, t + 1)

                def h_low(j):
                    dve.wait_ge(h_hi_ready, j + 1)
                    nc.vector.tensor_tensor(h_lo[:, ds(j, 1), :], xnT[:, ds(j, 1), :],
                                            h_hi[:, ds(j, 1), :].bitcast(F32), ALU.subtract).then_inc(h_ready, 1)

                XS = 6 + ADA_DVE - 1
                own.enter()
                for slot in range(2):
                    x_step(slot, slot, 1, first=True)
                own.leave(2 * XS)
                with dve.Fori(0, 3) as g:
                    own.enter(2 * XS * g)
                    for slot in range(2):
                        x_step(2 * g + (slot + 2), slot, g + 2)
                own.leave(6 * XS, 3)
                for e in range(2):
                    split_lo(dve, e, e)
                AS = ADA_DVE - 1
                with dve.Fori(0, 3) as g:
                    own.enter(2 * AS * g)
                    for slot in range(2):
                        j = 2 * g + (slot + 8)
                        ada_sum(slot, g + 5)
                        ada_take(j - 2, slot)
                        h_low(2 * (2 * g + slot))
                        h_low(2 * (2 * g + slot) + 1)
                own.leave(6 * AS, 3)
                own.enter()
                for slot in range(2):
                    j = KD - 2 + slot
                    ada_sum(slot, KD // 2)
                    ada_take(j - 2, slot)
                    h_low(KD - 4 + slot)
                own.leave(2 * AS)
                for j in range(KD - 2, KD):
                    ada_take(j, j % 2)
                for j in range(KD - 2, KD):
                    h_low(j)

                def proj_step(b, first=False):
                    if not first:
                        split_lo(dve, 2 * b + 1, 1)
                    split_lo(dve, 2 * b + 2, 0)

                proj_step(0, first=True)
                with dve.Fori(B_SQ, B_FQ) as b:
                    proj_step(b)
                z, a, e, t, acc = [f[:] for f in fg]
                dve.wait_ge(fg_loaded, 32)
                dve.wait_ge(consts, 1)

                def gate_step(k):
                    proj_step(k + B_FQ)
                    dve.wait_ge(gate_loaded, 16 * (k + 1))
                    nc.vector.scalar_tensor_tensor(out=gate_acc[:], in0=gate_raw[:], scalar=c_sb[:, ds(k, 1)],
                                                   in1=gate_acc[:], op0=ALU.mult, op1=ALU.add).then_inc(gate_added, 1)
                    dve.wait_ge(gate_added, k + 2)

                own.enter()
                own(nc.vector.tensor_scalar(z, z, bf_c[:, 0:1], None, ALU.add))
                own(nc.vector.tensor_scalar(t, z, -1.0, None, ALU.mult))
                nc.vector.tensor_tensor(a, z, t, ALU.min).then_inc(fg_neg, 1)
                own(nc.vector.tensor_scalar(z, z, 0.0, None, ALU.min))
                own.leave(3)
                gate_step(0)
                own.enter()
                dve.wait_ge(fg_exp, 1)
                own(nc.vector.tensor_scalar(t, e, 2.0, None, ALU.add))
                own(nc.vector.reciprocal(t, t))
                own.leave(2)
                gate_step(1)
                own.enter()
                own(nc.vector.tensor_tensor(a, e, t, ALU.mult))
                own(nc.vector.tensor_tensor(t, a, a, ALU.mult))
                own(nc.vector.tensor_scalar(acc, t, 1.0 / 15.0, None, ALU.mult))
                own.leave(3)
                gate_step(2)

                def series(n):
                    own(nc.vector.scalar_tensor_tensor(out=acc, in0=acc, scalar=1.0 / (2 * n + 1), in1=t,
                                                       op0=ALU.add, op1=ALU.mult))

                for k in range(3):
                    own.enter()
                    series(6 - 2 * k)
                    series(5 - 2 * k)
                    own.leave(2)
                    gate_step(3 + k)
                own.enter()
                own(nc.vector.scalar_tensor_tensor(out=acc, in0=acc, scalar=1.0, in1=a, op0=ALU.add, op1=ALU.mult))
                own(nc.vector.scalar_tensor_tensor(out=a, in0=acc, scalar=-2.0, in1=z, op0=ALU.mult, op1=ALU.add))
                own(nc.vector.memset(t, 1.0))
                own.leave(3)
                gate_step(6)
                nc.vector.tensor_tensor_scan(acc, t, a, 0.0, ALU.mult, ALU.add).then_inc(cum_done, 1)
                with dve.Fori(7, KD) as k:
                    gate_step(k)
                dve.wait_ge(cum_done, 1)
                dve.wait_ge(cum_hi, 2)
                nc.vector.scalar_tensor_tensor(out=cum_k[32:32 + FOX_HEADS, :], in0=acc, scalar=-1.0,
                                               in1=cum_k[0:FOX_HEADS, :].bitcast(F32), op0=ALU.mult,
                                               op1=ALU.subtract).then_inc(cum_ready, 1)
                nc.vector.tensor_tensor(cum_q[96:96 + FOX_HEADS, :], cum_k[0:FOX_HEADS, :].bitcast(F32), acc,
                                        ALU.add).then_inc(cum_ready, 1)
                proj_step(B_FQ + KD)
                dve.wait_ge(gate_loaded, 16 * (KD + 1))
                dve.wait_ge(gate_summed, 1)
                for q in range(4):
                    last = nc.vector.tensor_tensor(gate_row[:, q * HALF:(q + 1) * HALF],
                                                   (sP if q < 2 else tP)[0:1, q % 2, :],
                                                   gate_row[:, q * HALF:(q + 1) * HALF], ALU.add)
                last.then_inc(gate_ready, 1)
                with dve.Fori(B_FQ + KD + 1, B_G) as b:
                    proj_step(b)

                dve.wait_ge(consts, 2)
                dve.wait_ge(small_loaded, 16)
                own.enter()
                own(nc.vector.tensor_scalar(neg_sinks[:], sinks[:], -1.0, None, ALU.mult))
                for e in range(2):
                    for i in range(4):
                        slope = 2.0 ** (-8.0 * (4 * e + i + 1) / SWA_HEADS)
                        own(nc.vector.tensor_scalar(s_bias[:, e, i], dist[:], -slope, None, ALU.mult))
                own.leave(9)
                def low_parts(slot, u):
                    dve.wait_ge(s_hi, u + 1)
                    nc.vector.scalar_tensor_tensor(
                        out=sq_lo[:].rearrange("p i t -> p (i t)"),
                        in0=sq_raw[:, slot].rearrange("p i t -> p (i t)"), scalar=SWA_D ** -0.5,
                        in1=sq_hi[:].bitcast(F32).rearrange("p i t -> p (i t)"),
                        op0=ALU.mult, op1=ALU.subtract).then_inc(s_prep, 1)
                    nc.vector.tensor_tensor(sk_lo[:, slot, :], sk_raw[:, slot, :],
                                            sk_hi[:, slot, :].bitcast(F32), ALU.subtract).then_inc(s_prep, 1)

                def unit(g, m, par, last=False):
                    u = 8 * g + 2 * m + par
                    b = u + B_G
                    dve.wait_ge(s_vt_hi, u + 1)
                    nc.vector.tensor_tensor(sv_lo[:, par, 0, 0:SWA_D], tP[:, 0, 0:SWA_D],
                                            sv_hi[:, par, 0, 0:SWA_D].bitcast(F32), ALU.subtract)
                    nc.vector.tensor_tensor(sv_lo[:, par, 1, SWA_D:P], tP[:, 0, SWA_D:P],
                                            sv_hi[:, par, 1, SWA_D:P].bitcast(F32),
                                            ALU.subtract).then_inc(s_v, 1)
                    for e in range(2):
                        s = 2 * u + e
                        dve.wait_ge(s_qk, s + 2)
                        sc = sP[:].rearrange("p a (i k t) -> p (a i) k t", i=2, k=2)
                        for k in range(2):
                            now = k == par
                            if par == 0 and not now:
                                ins = nc.vector.scalar_tensor_tensor(
                                    out=sp_w[:, :, k, :], in0=sc[:, :, k, :], scalar=no_prev[:, ds(m, 1)],
                                    in1=s_bias[:, e, :, 0, :], op0=ALU.add, op1=ALU.add)
                            else:
                                ins = nc.vector.tensor_tensor(sp_w[:, :, k, :], sc[:, :, k, :],
                                                              s_bias[:, e, :, 1 if now else 0, :], ALU.add)
                        ins.then_inc(s_biased, 1)
                        dve.wait_ge(s_biased, s + 2)
                        own(nc.vector.tensor_reduce(neg_max[:], sp_w[:].rearrange("p i k t -> p i (k t)"),
                                                    AX.X, ALU.max, negate=True))
                        own(nc.vector.tensor_tensor(neg_max[:], neg_max[:],
                                                    neg_sinks[:, ds(8 * g + 4 * e, 4)], ALU.min))
                        nc.vector.tensor_tensor(sink_exp[:], neg_max[:], sinks[:, ds(8 * g + 4 * e, 4)],
                                                ALU.add).then_inc(s_max, 1)
                        split_lo(dve, 2 * b + (e + 1), 1 - e)
                        dve.wait_ge(s_exp, s + 1)
                        own(nc.vector.tensor_tensor(row_inv[:], row_sum[:], sink_exp[:], ALU.add))
                        nc.vector.reciprocal(row_inv[:], row_inv[:]).then_inc(s_inv, 1)
                        for k in range(2):
                            dve.wait_ge(s_pt_hi, 2 * s + (k + 1))
                            nc.vector.tensor_tensor(spT_lo[:, k, :], tP[:, k, :], spT_hi[:, k, :].bitcast(F32),
                                                    ALU.subtract).then_inc(s_pt, 1)
                    if not last:
                        low_parts(1 - par, u + 1)

                low_parts(0, 0)
                for g in range(2):
                    with dve.Fori(0, 4 - g) as m:
                        own.enter(12 * m)
                        unit(g, m, 0)
                        unit(g, m, 1)
                    own.leave(48 - 12 * g, 4 - g)
                    if g == 0:
                        nc.vector.tensor_scalar(s_bias[:].rearrange("p e i k t -> p (e i k t)"),
                                                s_bias[:].rearrange("p e i k t -> p (e i k t)"), 1.0 / 16.0, None,
                                                ALU.mult).then_inc(s_scaled, 1)
                        dve.wait_ge(s_scaled, 1)
                own.enter()
                unit(1, 3, 0)
                unit(1, 3, 1, last=True)
                own.leave(12)

                with dve.Fori(0, FOX_HEADS) as h:
                    def q_low(i):
                        dve.wait_ge(f_q_hi, 8 * h + (i + 1))
                        nc.vector.scalar_tensor_tensor(out=fq_lo[:], in0=fq_raw[:, i % 2, :], scalar=float(P) ** -0.5,
                                                       in1=fq_hi[:].bitcast(F32), op0=ALU.mult, op1=ALU.subtract)
                        nc.vector.tensor_scalar(fcq[:], cum_q[:, i * P:(i + 1) * P].bitcast(F32),
                                                head_sel[:, ds(h, 1)], None, ALU.mult).then_inc(f_q, 1)

                    q_low(0)
                    dve.wait_ge(f_k_hi, h + 1)
                    nc.vector.tensor_tensor(fk_lo[:], fk_raw[:], fk_hi[:].bitcast(F32), ALU.subtract).then_inc(f_k, 1)
                    dve.wait_ge(f_vt_hi, h + 1)
                    for k in range(2):
                        last = nc.vector.tensor_tensor(
                            fv_lo[:, 4 * k:4 * k + 4, :].rearrange("p j t -> p (j t)"), tP[:, k, :],
                            fv_hi[:, 4 * k:4 * k + 4, :].bitcast(F32).rearrange("p j t -> p (j t)"), ALU.subtract)
                    last.then_inc(f_v, 1)
                    turned = 0
                    for i in range(8):
                        b = 4 * h + (B_M + i // 2)
                        e = i % 2
                        dve.wait_ge(f_qk, 8 * h + (i + 2))
                        nc.vector.tensor_reduce(neg_max[:, 0:1],
                                                sP[:, :, :].rearrange("p a t -> p (a t)")[:, 0:(i + 1) * P],
                                                AX.X, ALU.max, negate=True).then_inc(f_max, 1)
                        split_lo(dve, 2 * b + (e + 1), 1 - e)
                        dve.wait_ge(f_exp, 8 * h + (i + 2))
                        nc.vector.reciprocal(row_inv[:, 0:1], row_sum[:, 0:1]).then_inc(f_inv, 1)
                        for k in range(i // 4 + 1):
                            turned += 1
                            n = min(4, i + 1 - 4 * k)
                            dve.wait_ge(f_pt_hi, 12 * h + turned)
                            nc.vector.tensor_tensor(
                                fpT[:, 4 * k:4 * k + n, 1, :],
                                tP[:, k, 0:n * P].rearrange("p (j t) -> p j t", j=n),
                                fpT[:, 4 * k:4 * k + n, 0, :].bitcast(F32), ALU.subtract).then_inc(f_pt, 1)
                        if i < 7:
                            q_low(i + 1)
                        dve.wait_ge(f_half, 8 * h + (i + 1))
                        nc.vector.tensor_tensor(fo_st[:], oP[:, P:2 * P], fo_st[:], ALU.add).then_inc(f_o, 1)

            @block.tensor
            def _(pe):
                def turn(dst, src):
                    return nc.tensor.transpose(dst, src, ident[:])

                pe.wait_ge(ident_ready, 1)
                pe.wait_ge(c_loaded, 32)
                nc.tensor.transpose(projP[:, 0, 0:2 * KD], ada_rows[:], ident[0:2 * KD, 0:2 * KD]
                                    ).then_inc(ada_b_turned, 1)
                pe.wait_ge(c_one, 1)

                def ada_turn(j, slot):
                    pe.wait_ge(ada_row_ready, j + 1)
                    if isinstance(j, int) and j < 2:
                        pe.wait_ge(ada_b_ready, 1)
                    else:
                        pe.wait_ge(ada_read, j - 1)
                    for s in range(2):
                        last = nc.tensor.matmul(projP[:, slot, s:s + 1], ada_row[:, slot, s * P:(s + 1) * P],
                                                c_sb[0:1, KD:KD + 1], start=True, stop=True)
                    last.then_inc(ada_turned, 1)

                def ada_chunk(j, slot, loads, first=False):
                    row = (adaP if slot else oP)[0:1, 0:2 * P]
                    w = ada_raw[:, slot].rearrange("p k s n -> p k (s n)")
                    pe.wait_ge(ada_loaded[slot], 32 * loads)
                    if not first:
                        pe.wait_ge(ada_row_ready, j - 1)
                    for k in range(ADA_DVE, KD):
                        nc.tensor.matmul(row, c_sb[:, k:k + 1], w[:, k, :], start=(k == ADA_DVE), stop=False)
                    if not (isinstance(j, int) and j == 0):
                        ada_turn(j - 1, 1 - slot)
                    pe.wait_ge(ada_summed, j + 1)
                    nc.tensor.matmul(row, c_sb[:, KD:KD + 1], ada_acc[:, slot, :], start=False, stop=True
                                     ).then_inc(ada_done, 1)

                def x_turn(t, slot, first=False):
                    pe.wait_ge(x_normed, t + 1)
                    if not first:
                        pe.wait_ge(xt_copied, 4 * t)
                    for q in range(4):
                        for j in range(4):
                            last = turn((sP if q < 2 else tP)[:, q % 2, j * P:(j + 1) * P],
                                        x_t[:, slot, (4 * q + j) * P:(4 * q + j + 1) * P])
                        last.then_inc(x_turned, 1)

                for t in range(2):
                    ada_chunk(t, t, 1, first=True)
                    x_turn(t, t, first=(t == 0))
                with pe.Fori(1, 4) as g:
                    for slot in range(2):
                        ada_chunk(2 * g + slot, slot, g + 1)
                        x_turn(2 * g + slot, slot)
                with pe.Fori(4, KD // 2) as g:
                    for slot in range(2):
                        ada_chunk(2 * g + slot, slot, g + 1)
                ada_turn(KD - 1, 1)
                pe.wait_ge(ada_read, KD)

                def proj(b, e, lo=0, hi=MMS):
                    for n in range(lo, hi):
                        half, k, part = n // 24, n // 3 % 8, n % 3
                        if n == 0:
                            pe.wait_ge(chunk_lo, 2 * b + (e + 1))
                        if n % 24 == 0 and e == 0 and not isinstance(b, int):
                            pe.wait_ge(proj_copied, 2 * b + (half - 1))
                        if isinstance(b, int) and half == 0 and part == 0:
                            pe.wait_ge(h_ready, 8 * e + k + 1)
                        w, hh = ((w_hi, h_hi), (w_hi, h_lo), (w_lo, h_hi))[part]
                        last = nc.tensor.matmul(projP[:, half, :], w[:, e, k * P:(k + 1) * P],
                                                hh[:, 8 * e + k, half * HALF:(half + 1) * HALF],
                                                start=(e == 0 and n % 24 == 0), stop=(e == 1 and n % 24 == 23))
                        if e == 1 and n == 23:
                            last.then_inc(half0_done, 1)
                        if n == MMS - 1:
                            last.then_inc(chunk_used, 1)

                proj(0, 0)
                proj(0, 1)
                with pe.Fori(B_SQ, B_FQ + KD) as b:
                    proj(b, 0)
                    proj(b, 1)
                pe.wait_ge(consts, 1)
                pe.wait_ge(gate_added, KD + 1)
                for q in range(4):
                    last = nc.tensor.matmul((sP if q < 2 else tP)[0:1, q % 2, :], ones[:],
                                            gate_acc[:, q * HALF:(q + 1) * HALF], start=True, stop=True)
                last.then_inc(gate_summed, 1)
                with pe.Fori(B_FQ + KD, B_G) as b:
                    proj(b, 0)
                    proj(b, 1)

                with pe.Fori(0, 2) as g:
                    with pe.Fori(0, 4) as m:
                        for par in range(2):
                            u = 8 * g + 2 * m + par
                            b = u + B_G

                            def scores(e):
                                pe.wait_ge(s_prep, 2 * u + 2)
                                pe.wait_ge(gate_ready, 1)
                                pe.wait_ge(s_biased, 2 * u + e + 1)
                                r = slice(SWA_D * e, SWA_D * (e + 1))
                                for i in range(4):
                                    dst = sP[:, i // 2, 2 * P * (i % 2):2 * P * (i % 2 + 1)]
                                    for part, (q, k) in enumerate(((sq_hi, sk_hi), (sq_hi, sk_lo), (sq_lo, sk_hi))):
                                        last = nc.tensor.matmul(dst, q[r, i, :], k[r, :, :],
                                                                start=(part == 0), stop=(part == 2))
                                last.then_inc(s_qk, 1)

                            def turn_weights(e):
                                pe.wait_ge(s_norm, 2 * u + (e + 1))
                                if e == 0:
                                    pe.wait_ge(s_v, u + 3)
                                for k in range(2):
                                    for i in range(4):
                                        last = turn(tP[:, k, i * P:(i + 1) * P], sp_w[:, i, k, :])
                                    last.then_inc(s_turned, 1)

                            def weigh(e):
                                pe.wait_ge(s_pt, 4 * u + 2 * (e + 1) + 1)
                                if e == 0:
                                    pe.wait_ge(s_o, u + 1)
                                n = 0
                                for k in range(2):
                                    for v, w in ((sv_hi, spT_hi), (sv_hi, spT_lo), (sv_lo, spT_hi)):
                                        last = nc.tensor.matmul(oP[:, :], v[:, k, e, :], w[:, k, :],
                                                                start=(e == 0 and n == 0), stop=(e == 1 and n == 5))
                                        n += 1
                                if e == 1:
                                    last.then_inc(s_pv, 1)

                            pe.wait_ge(s_loaded[par], 64 * (4 * g + m + 1))
                            pe.wait_ge(s_pt, 4 * u + 1)
                            turn(tP[:, 0, 0:P], sv_raw[:, par, :]).then_inc(s_vt, 1)
                            proj(b, 0, 0, 12)
                            scores(0)
                            proj(b, 0, 12, MMS)
                            turn_weights(0)
                            scores(1)
                            proj(b, 1, 0, 12)
                            weigh(0)
                            proj(b, 1, 12, 36)
                            turn_weights(1)
                            proj(b, 1, 36, MMS)
                            weigh(1)

                with pe.Fori(0, FOX_HEADS) as h:
                    pe.wait_ge(f_kv_loaded, 32 * h + 32)
                    pe.wait_ge(s_pt, 64 + 1)
                    pe.wait_ge(f_pt, 12 * h + 1)
                    for j in range(8):
                        last = turn(tP[:, j // 4, (j % 4) * P:(j % 4 + 1) * P], fv_raw[:, j * P:(j + 1) * P])
                    last.then_inc(f_vt, 1)
                    turned = 0
                    for i in range(8):
                        b = 4 * h + (B_M + i // 2)
                        e = i % 2
                        first = 18 if i == 0 else 0
                        proj(b, e, 0, first)
                        pe.wait_ge(f_q, 8 * h + (i + 3))
                        if i == 0:
                            pe.wait_ge(f_k, h + 2)
                            pe.wait_ge(s_biased, 32 + 1)
                        pe.wait_ge(f_exp, 8 * h + i + 1)
                        for a in range(i // 4 + 1):
                            c0, c1 = a * HALF, min((a + 1) * HALF, (i + 1) * P)
                            dst = sP[:, a, 0:c1 - c0]
                            nc.tensor.matmul(dst, fcq[:], cum_k[:, c0:c1], start=True, stop=False)
                            if a == i // 4:
                                nc.tensor.matmul(sP[:, a, (i % 4) * P:(i % 4 + 1) * P], ident_r[:], mask_r[:],
                                                 start=False, stop=False)
                            for part, (q, k) in enumerate(((fq_hi, fk_hi), (fq_hi, fk_lo), (fq_lo, fk_hi))):
                                last = nc.tensor.matmul(dst, q[:], k[:, c0:c1], start=False, stop=(part == 2))
                        last.then_inc(f_qk, 1)
                        proj(b, e, first, 36)
                        pe.wait_ge(f_norm, 8 * h + (i + 1))
                        if i == 0:
                            pe.wait_ge(f_v, h + 1)
                        for j in range(i + 1):
                            last = turn(tP[:, j // 4, (j % 4) * P:(j % 4 + 1) * P], fp_w[:, j, :])
                            if j == 3 or j == i:
                                last.then_inc(f_turned, 1)
                        turned += i // 4 + 1
                        proj(b, e, 36, MMS)
                        pe.wait_ge(f_pt, 12 * h + turned + 1)
                        pe.wait_ge(f_o, 8 * h + i + 1)
                        for j in range(i + 1):
                            nc.tensor.matmul(oP[:, 0:2 * P], fv_hi[:, j, :], fpT[:, j, :, :],
                                             start=(j == 0), stop=False)
                            last = nc.tensor.matmul(oP[:, 0:P], fv_lo[:, j, :], fpT[:, j, 0, :],
                                                    start=False, stop=(j == i))
                        last.then_inc(f_pv, 1)

        with ExitStack() as last_part:
            def sb2(name, shape, dt=F32):
                return sb(name, shape, dt, last_part)

            yP = last_part.enter_context(nc.psum_tensor("yP", [P, 4, HALF], F32))
            zP = last_part.enter_context(nc.psum_tensor("zP", [P, 4, HALF], F32))
            with ExitStack() as late:
                lng_all = sb("lng_all", [P, D], F32, late)
                lnb_all = sb("lnb_all", [P, D], F32, late)
            og_hi = sb2("og_hi", [P, KD, HALF], F32R)
            og_lo = sb2("og_lo", [P, KD, HALF], F32R)
            mg_hi = sb2("mg_hi", [P, KD, HALF], F32R)
            mg_lo = sb2("mg_lo", [P, KD, HALF], F32R)
            z = sb2("z", [P, 4, D])
            aux = sb2("aux", [P, 2, HALF])
            sg = sb2("sg", [P, 2, HALF])
            z_tmp = sb2("z_tmp", [P, 4, HALF])
            ta, tb_ = z_tmp[:, 0, :], z_tmp[:, 1, :]
            gate_sl = sb2("gate_sl", [P, HALF])
            lng = sb2("lng", [P, HALF])
            lnb = sb2("lnb", [P, HALF])
            z_bn = sb2("z_bn", [P, 4, 4, 6])
            z_mv = sb2("z_mv", [P, 4, 2])
            z_sm = sb2("z_sm", [P, 6, 4])

            og_sig = sem("og_sig")
            og_t = sem("og_t")
            og_g = sem("og_g")
            og_hi_ready = sem("og_hi_ready")
            og_ready = sem("og_ready")
            aux_loaded = sem("aux_loaded")
            sg_ready = sem("sg_ready")
            y_read = sem("y_read")
            t_ready = sem("t_ready")
            mg_hi_ready = sem("mg_hi_ready")
            mg_ready = sem("mg_ready")
            gate_loaded2 = sem("gate_slice_loaded")
            z_x = sem("z_x_loaded")
            z_done = sem("z_product_done")
            z_read = sem("z_read")
            z_added = sem("z_added")
            z_summed = sem("z_summed")
            z_var = sem("z_var")
            z_std = sem("z_std")
            ln_ready = sem("ln_ready")
            ln_loaded = sem("ln_loaded")
            ln_done = sem("ln_done")
            out_stored = sem("out_stored")
            dve_step2 = sem("dve_step2")
            pool_step2 = sem("pool_step2")
            ln_all_loaded = sem("ln_all_loaded")
            z_normed = sem("z_normed")
            ln_part = sem("ln_part")
            dve_out = sem("dve_out")
            pool_out = sem("pool_out")
            last_stored = sem("last_stored")

            block = last_part.enter_context(nc.Block())

            DVE_COLS = 1408
            @block.sync
            def _(sp):
                def aux_in(nb, H):
                    for w in range(2):
                        sp.dma_start(aux[:, w, :], proj_d[ds(nb + (B_M + KD * w), 1), :, H * HALF:(H + 1) * HALF]
                                     .rearrange("a p t -> p (a t)")).then_inc(aux_loaded, 16)

                sp.wait_ge(f_stored, 1024 + 1)
                load_og(sp, 3)
                load_chunk(sp, TAIL + 2, 0, wbf_v[:, :, 0:P])
                load_og(sp, 4)
                for s in range(2):
                    sp.wait_ge(proj_stored[s], 16 * BLOCKS)
                aux_in(0, 0)
                load_chunk(sp, TAIL + 3, 1, wbf_v[:, :, P:2 * P])
                sp.wait_ge(sg_ready, 1)
                aux_in(1, 0)
                for H in range(2):
                    with sp.Fori(2 - 2 * H, KD) as nb:
                        load_chunk(sp, 2 * nb + (TAIL + 64 * H), 0, wbf_v[:, :, ds(nb * P, P)])
                        load_chunk(sp, 2 * nb + (TAIL + 64 * H + 1), 1, wbs_v[:, :, ds(nb * P, P)])
                        sp.wait_ge(sg_ready, nb + 2 * KD * H)
                        if H == 1:
                            sp.wait_ge(og_ready, 2 * KD)
                        aux_in(nb, H)
                    with sp.Fori(0, 4) as cg:
                        for kk in range(8):
                            load_chunk(sp, 8 * cg + (TAIL + 64 * H + 32 + kk), kk % 2,
                                       w_out_v[:, 2 * kk:2 * kk + 2, ds(cg * HALF, HALF)])
                            if kk == 1:
                                sp.wait_ge(*((og_ready, KD) if H == 0 else (out_stored, 64)))
                                cols = ds(cg * HALF, HALF)
                                sp.dma_start(z[:, :, cols], x2[:, 4 * H:4 * H + 4, cols]).then_inc(z_x, 16)
                            if kk == 5 and H == 1:
                                sp.wait_ge(chunk_used, TAIL + 96)
                                for src, dst in ((ln_g, lng_all), (ln_b, lnb_all)):
                                    sp.dma_start(dst[:, ds(cg * HALF, HALF)],
                                                 src[0:1, ds(cg * HALF, HALF)].broadcast_to([P, HALF])
                                                 ).then_inc(ln_all_loaded, 16)
                            if kk == 3:
                                sp.wait_ge(z_read, 4 * cg + (16 * H + 4))
                                sp.dma_start(gate_sl[:], gate_d[0:1, ds(cg * HALF, HALF)].broadcast_to([P, HALF])
                                             ).then_inc(gate_loaded2, 16)
                            if H == 0 and kk % 2 == 0:
                                k = 4 * cg + kk // 2
                                sp.wait_ge(sg_ready, KD)
                                sp.wait_ge(og_ready, k + KD)
                                for w, src, base in ((0, o_d, 0), (1, proj_d, B_G)):
                                    sp.dma_start(aux[:, w, :], src[ds(k + base, 1), :, HALF:SEQ]
                                                 .rearrange("a p t -> p (a t)")).then_inc(aux_loaded, 16)
                for tb in range(4):
                    for done, cols in ((dve_out, slice(0, DVE_COLS)), (pool_out, slice(DVE_COLS, D))):
                        sp.wait_ge(done, tb + 1)
                        sp.dma_start(out2[:, 4 + tb, cols], z[:, tb, cols]).then_inc(last_stored, 16)
                sp.wait_ge(last_stored, 128)

            @block.gpsimd
            def _(pool):
                for n in range(KD):
                    pool.wait_ge(og_sig, n + 1)
                    nc.gpsimd.tensor_tensor(go_in[:, n, 0, :], go_in[:, n, 0, :], z_tmp[:, n % 2, :], ALU.mult
                                            ).then_inc(og_g, 1)
                for H in range(1):
                    pool.wait_ge(ln_ready, H + 1)
                    for cs in range(4):
                        n = 4 * cs + 16 * H
                        if n:
                            pool.wait_ge(ln_done, n)
                        cols = slice(cs * HALF, (cs + 1) * HALF)
                        pool.dma_start(lng[:], ln_g[0:1, cols].broadcast_to([P, HALF])).then_inc(ln_loaded, 16)
                        pool.dma_start(lnb[:], ln_b[0:1, cols].broadcast_to([P, HALF])).then_inc(ln_loaded, 16)
                        for tb in range(4):
                            nc.gpsimd.tensor_scalar(z[:, tb, cols], z[:, tb, cols], z_mv[:, tb, 0:1],
                                                    z_sm[:, 3, tb:tb + 1], ALU.subtract, ALU.mult
                                                    ).then_inc(pool_step2, 1)
                        pool.wait_ge(ln_loaded, 32 * cs + (128 * H + 32))
                        for tb in range(4):
                            pool.wait_ge(pool_step2, 8 * cs + (32 * H + 1 + tb))
                            nc.gpsimd.tensor_tensor(z[:, tb, cols], z[:, tb, cols], lng[:], ALU.mult
                                                    ).then_inc(pool_step2, 1)
                        for tb in range(4):
                            pool.wait_ge(pool_step2, 8 * cs + (32 * H + 5 + tb))
                            nc.gpsimd.tensor_tensor(z[:, tb, cols], z[:, tb, cols], lnb[:], ALU.add
                                                    ).then_inc(ln_done, 1)
                        pool.wait_ge(ln_done, n + 4)
                        pool.dma_start(out2[:, 4 * H:4 * H + 4, cols], z[:, :, cols]).then_inc(out_stored, 16)
                pool.wait_ge(ln_all_loaded, 128)
                for tb in range(4):
                    cols = slice(DVE_COLS, D)
                    pool.wait_ge(z_normed, tb + 1)
                    nc.gpsimd.tensor_tensor(z[:, tb, cols], z[:, tb, cols], lng_all[:, cols], ALU.mult
                                            ).then_inc(pool_step2, 1)
                    pool.wait_ge(pool_step2, 33 + tb)
                    nc.gpsimd.tensor_tensor(z[:, tb, cols], z[:, tb, cols], lnb_all[:, cols], ALU.add
                                            ).then_inc(pool_out, 1)
                pool.wait_ge(out_stored, 64)

            @block.scalar
            def _(act):
                def root_and_back(H):
                    act.wait_ge(z_var, H + 1)
                    nc.scalar.activation(z_sm[:, 1, :], z_sm[:, 0, :], ACT.Sqrt).then_inc(z_std, 1)
                    if H == 0:
                        nc.scalar.activation(z_sm[:, 5, :], z_sm[:, 0, :], ACT.Sigmoid)

                def og_high(n):
                    k = OG_ORDER[n]
                    act.wait_ge(og_t, n + 1)
                    nc.scalar.copy(og_hi[:, k, :], go_in[:, n, 1, :]).then_inc(og_hi_ready, 1)

                def merge_gates(nb, H):
                    act.wait_ge(aux_loaded, 32 * nb + (1024 * H + 32))
                    nc.scalar.activation(sg[:], aux[:], ACT.Sigmoid).then_inc(sg_ready, 1)

                def merged_high(nb, H):
                    act.wait_ge(t_ready, nb + (KD * H + 1))
                    nc.scalar.copy(mg_hi[:, ds(nb, 1), :].rearrange("p a t -> p (a t)"), ta
                                   ).then_inc(mg_hi_ready, 1)

                split_hi(act, TAIL + 1, 1, TAIL // 2 + 1)
                for n in range(KD):
                    for q, (n0, _) in enumerate(OG_GROUPS):
                        if n == n0:
                            act.wait_ge(og_in[q], 32)
                    if n >= 2:
                        act.wait_ge(og_g, n - 1)
                    nc.scalar.activation(z_tmp[:, n % 2, :], go_in[:, n, 0, :], ACT.Sigmoid).then_inc(og_sig, 1)
                    if n == 1:
                        og_high(0)
                    if n >= 3:
                        og_high(n - 2)
                    if n == 11:
                        split_hi(act, TAIL + 2, 0, TAIL // 2 + 2)
                    if n == 13:
                        split_hi(act, TAIL + 3, 1, TAIL // 2 + 2)
                        merge_gates(0, 0)
                og_high(KD - 2)
                og_high(KD - 1)
                split_hi(act, TAIL + 4, 0, TAIL // 2 + 3)
                split_hi(act, TAIL + 5, 1, TAIL // 2 + 3)
                merged_high(0, 0)
                merge_gates(1, 0)
                merged_high(1, 0)

                for H in range(2):
                    def branch_step(nb):
                        c0 = 2 * nb + (TAIL + 64 * H)
                        if H == 1 and isinstance(nb, int):
                            root_and_back(0)
                        merge_gates(nb, H)
                        for e in range(2):
                            split_hi(act, c0 + (2 + e), e, nb + (TAIL // 2 + 32 * H + 2))
                        merged_high(nb, H)

                    if H == 1:
                        branch_step(0)
                    with act.Fori(2 - H, KD) as nb:
                        branch_step(nb)

                    def out_step(cg, last):
                        for kk in range(8):
                            c = 8 * cg + (TAIL + 64 * H + 32 + kk)
                            if H == 0 and kk % 2 == 0:
                                k = 4 * cg + kk // 2
                                act.wait_ge(aux_loaded, 32 * k + (32 * KD + 32))
                                nc.scalar.activation(sg[:, 0, :], aux[:, 1, :], ACT.Sigmoid).then_inc(sg_ready, 1)
                                act.wait_ge(og_t, k + (KD + 1))
                                nc.scalar.copy(og_hi[:, ds(k, 1), :].rearrange("p a t -> p (a t)"), aux[:, 0, :]
                                               ).then_inc(og_hi_ready, 1)
                            if not (last and kk >= 6):
                                split_hi(act, c + 2, kk % 2, 4 * cg + (TAIL // 2 + 32 * H + 18 + kk // 2))

                    with act.Fori(0, 4 - H) as cg:
                        out_step(cg, False)
                    if H == 1:
                        out_step(3, True)
                root_and_back(1)
                act.wait_ge(ln_ready, 2)
                for tb in range(4):
                    cols = slice(DVE_COLS, D)
                    nc.scalar.activation(z[:, tb, cols], z[:, tb, cols], ACT.Identity, bias=z_sm[:, 4, tb:tb + 1],
                                         scale=z_sm[:, 3, tb:tb + 1]).then_inc(z_normed, 1)

            @block.vector
            def _(dve):
                own = Steps(dve, dve_step2)

                def og_low(n):
                    k = OG_ORDER[n]
                    dve.wait_ge(og_hi_ready, n + 1)
                    nc.vector.tensor_tensor(og_lo[:, k, :], go_in[:, n, 1, :], og_hi[:, k, :].bitcast(F32),
                                            ALU.subtract).then_inc(og_ready, 1)

                def y_weigh(nb, H, br, bank):
                    c0 = 2 * nb + (TAIL + 64 * H)
                    dve.wait_ge(sg_ready, nb + (2 * KD * H + 1))
                    if br == 0 and not (isinstance(nb, int) and nb == 0 and H == 0):
                        dve.wait_ge(mg_ready, nb + KD * H)
                    dve.wait_ge(chunk_used, c0 + (br + 1))
                    nc.vector.tensor_tensor((ta, tb_)[br], yP[:, 2 * bank + br, :], sg[:, br, :], ALU.mult
                                            ).then_inc(y_read, 1)

                def merge(nb, H):
                    dve.wait_ge(y_read, 2 * nb + (2 * KD * H + 2))
                    nc.vector.tensor_tensor(ta, ta, tb_, ALU.add).then_inc(t_ready, 1)
                    if not (isinstance(nb, int) and nb == 1 and H == 0):
                        split_lo(dve, 2 * nb + (TAIL + 64 * H + (5 if isinstance(nb, int) and H == 0 else 3)), 1)
                    dve.wait_ge(mg_hi_ready, nb + (KD * H + 1))
                    nc.vector.tensor_tensor(mg_lo[:, ds(nb, 1), :].rearrange("p a t -> p (a t)"), ta,
                                            mg_hi[:, ds(nb, 1), :].bitcast(F32).rearrange("p a t -> p (a t)"),
                                            ALU.subtract).then_inc(mg_ready, 1)

                split_lo(dve, TAIL + 1, 1)
                for n in range(KD):
                    for q, (n0, _) in enumerate(OG_GROUPS):
                        if n == n0:
                            dve.wait_ge(og_in[q], 32)
                    dve.wait_ge(og_g, n + 1)
                    nc.vector.tensor_tensor(go_in[:, n, 1, :], go_in[:, n, 1, :], go_in[:, n, 0, :], ALU.mult
                                            ).then_inc(og_t, 1)
                    if n == 1:
                        og_low(0)
                    if n >= 3:
                        og_low(n - 2)
                    if n == 11:
                        split_lo(dve, TAIL + 2, 0)
                    if n == 13:
                        split_lo(dve, TAIL + 3, 1)
                og_low(KD - 2)
                og_low(KD - 1)
                split_lo(dve, TAIL + 4, 0)
                dve.wait_ge(chunk_used, TAIL + 4)
                y_weigh(0, 0, 0, 0)
                y_weigh(0, 0, 1, 0)
                merge(0, 0)
                y_weigh(1, 0, 0, 1)
                y_weigh(1, 0, 1, 1)
                merge(1, 0)

                def z_rest(cg, H, tbs):
                    for tb in tbs:
                        nc.vector.bn_stats(z_bn[:, tb, ds(cg, 1), :].rearrange("p a s -> p (a s)"),
                                           z[:, tb, ds(cg * HALF, HALF)]).then_inc(z_added, 1)

                def norm_scalars(H):
                    dve.wait_ge(z_added, 16 * (H + 1))
                    for tb in range(4):
                        last = nc.vector.bn_aggr(z_mv[:, tb, :], z_bn[:, tb, :, :].rearrange("p c s -> p (c s)"))
                    own(last)
                    nc.vector.tensor_scalar(z_sm[:, 0, :], z_mv[:, :, 1], LN_EPS, None, ALU.add).then_inc(z_var, 1)
                    dve.wait_ge(z_std, H + 1)
                    r, w = z_sm[:, 2, :], z_sm[:, 3, :]
                    own(nc.vector.reciprocal(r, z_sm[:, 1, :]))
                    own(nc.vector.tensor_tensor(w, r, r, ALU.mult))
                    own(nc.vector.tensor_tensor(w, w, z_sm[:, 0, :], ALU.mult))
                    own(nc.vector.tensor_scalar(w, w, -0.5, 1.5, ALU.mult, ALU.add))
                    own(nc.vector.tensor_tensor(w, w, r, ALU.mult))
                    nc.vector.scalar_tensor_tensor(out=z_sm[:, 4, :], in0=w, scalar=-1.0, in1=z_mv[:, :, 0],
                                                   op0=ALU.mult, op1=ALU.mult).then_inc(ln_ready, 1)

                for H in range(2):
                    def branch_step(nb, bank):
                        c0 = 2 * nb + (TAIL + 64 * H)
                        if H == 1 and isinstance(nb, int) and nb == 0:
                            own.enter()
                            z_rest(3, 0, range(4))
                            norm_scalars(0)
                            own.leave(6)
                        y_weigh(nb, H, 0, bank)
                        split_lo(dve, c0 + 2, 0)
                        y_weigh(nb, H, 1, bank)
                        merge(nb, H)

                    if H == 1:
                        branch_step(0, 0)
                        branch_step(1, 1)
                    with dve.Fori(1, KD // 2) as pair:
                        for bank in range(2):
                            branch_step(2 * pair + bank, bank)

                    def out_step(cg, last=False):
                        for kk in range(8):
                            c = 8 * cg + (TAIL + 64 * H + 32 + kk)
                            if kk == 1 and not (isinstance(cg, int) and cg == 0):
                                z_rest(cg - 1, H, range(4))
                            if H == 0 and kk % 2 == 0:
                                k = 4 * cg + kk // 2
                                dve.wait_ge(sg_ready, k + (KD + 1))
                                nc.vector.tensor_tensor(tb_, aux[:, 1, :], sg[:, 0, :], ALU.mult).then_inc(og_g, 1)
                                dve.wait_ge(og_g, k + (KD + 1))
                                nc.vector.tensor_tensor(aux[:, 0, :], aux[:, 0, :], tb_, ALU.mult).then_inc(og_t, 1)
                                dve.wait_ge(og_hi_ready, k + (KD + 1))
                                nc.vector.tensor_tensor(
                                    og_lo[:, ds(k, 1), :].rearrange("p a t -> p (a t)"), aux[:, 0, :],
                                    og_hi[:, ds(k, 1), :].bitcast(F32).rearrange("p a t -> p (a t)"),
                                    ALU.subtract).then_inc(og_ready, 1)
                            if kk < 6 or (kk == 6 and not last):
                                split_lo(dve, c + 2, kk % 2)
                        cols = ds(cg * HALF, HALF)
                        dve.wait_ge(gate_loaded2, 16 * cg + (64 * H + 16))
                        dve.wait_ge(z_x, 16 * cg + (64 * H + 16))
                        for tb in range(4):
                            if tb < 3:
                                dve.wait_ge(z_done, 3 * cg + (12 * H + tb + 1))
                            else:
                                dve.wait_ge(chunk_used, 8 * cg + (TAIL + 64 * H + 40))
                            nc.vector.tensor_tensor(z_tmp[:, tb, :], zP[:, tb, :], gate_sl[:], ALU.mult
                                                    ).then_inc(z_read, 1)
                            dve.wait_ge(z_read, 4 * cg + (16 * H + 5 + tb))
                            nc.vector.scalar_tensor_tensor(out=z[:, tb, cols], in0=z[:, tb, cols], scalar=ALPHA,
                                                           in1=z_tmp[:, tb, :], op0=ALU.mult, op1=ALU.add
                                                           ).then_inc(z_summed, 1)
                        dve.wait_ge(z_summed, 4 * cg + (16 * H + 4))
                        if not last:
                            split_lo(dve, 8 * cg + (TAIL + 64 * H + 41), 1)

                    out_step(0)
                    with dve.Fori(1, 4 - H) as cg:
                        out_step(cg)
                    if H == 1:
                        out_step(3, last=True)
                own.enter()
                z_rest(3, 1, range(4))
                norm_scalars(1)
                own.leave(6)
                dve.wait_ge(ln_ready, 2)
                dve.wait_ge(ln_all_loaded, 128)
                cols = slice(0, DVE_COLS)
                for tb in range(4):
                    nc.vector.scalar_tensor_tensor(out=z[:, tb, cols], in0=z[:, tb, cols], scalar=z_mv[:, tb, 0:1],
                                                   in1=lng_all[:, cols], op0=ALU.subtract, op1=ALU.mult
                                                   ).then_inc(ln_part, 1)
                    dve.wait_ge(ln_part, tb + 1)
                    nc.vector.scalar_tensor_tensor(out=z[:, tb, cols], in0=z[:, tb, cols],
                                                   scalar=z_sm[:, 3, tb:tb + 1], in1=lnb_all[:, cols],
                                                   op0=ALU.mult, op1=ALU.add).then_inc(dve_out, 1)

            @block.tensor
            def _(pe):
                pe.sem_inc(z_read, 4)

                def y_product(br, bank, slot, k):
                    for part, (w, o) in enumerate(((w_hi, og_hi), (w_hi, og_lo), (w_lo, og_hi))):
                        last = nc.tensor.matmul(yP[:, 2 * bank + br, :], w[:, slot, k * P:(k + 1) * P],
                                                o[:, 8 * br + k, :],
                                                start=(k == 0 and part == 0), stop=(k == 7 and part == 2))
                    return last

                for turn_of, br in enumerate((1, 0)):
                    for n in range(12):
                        for nb in range(2):
                            k = n - 4 * nb
                            if 0 <= k < 8:
                                if k == 0:
                                    pe.wait_ge(chunk_lo, TAIL + 1 + 2 * turn_of + nb)
                                if nb == 0:
                                    pe.wait_ge(og_ready, 8 * turn_of + k + 1)
                                last = y_product(br, nb, nb, k)
                                if k == 7:
                                    last.then_inc(chunk_used, 1)

                def branch(H, nb, bank):
                    for br in range(2):
                        pe.wait_ge(chunk_lo, 2 * nb + (TAIL + 64 * H + 1 + br))
                        pe.wait_ge(y_read, 2 * nb + (2 * KD * H - 3 + br))
                        for k in range(8):
                            last = y_product(br, bank, br, k)
                        last.then_inc(chunk_used, 1)

                for H in range(2):
                    if H == 1:
                        pe.wait_ge(og_ready, 2 * KD)
                    with pe.Fori(1 - H, KD // 2) as pair:
                        for bank in range(2):
                            branch(H, 2 * pair + bank, bank)
                    with pe.Fori(0, 4) as cg:
                        for kk in range(8):
                            c = 8 * cg + (TAIL + 64 * H + 32 + kk)
                            pe.wait_ge(mg_ready, KD * H + 2 * kk + 2)
                            pe.wait_ge(chunk_lo, c + 1)
                            for tb in range(4):
                                if kk == 0:
                                    pe.wait_ge(z_read, 4 * cg + (16 * H + tb + 1))
                                for k2 in range(2):
                                    for part, (m, w) in enumerate(((mg_hi, w_hi), (mg_hi, w_lo), (mg_lo, w_hi))):
                                        last = nc.tensor.matmul(
                                            zP[:, tb, :], m[:, 2 * kk + k2, tb * P:(tb + 1) * P],
                                            w[:, kk % 2, k2 * HALF:(k2 + 1) * HALF],
                                            start=(kk == 0 and k2 == 0 and part == 0),
                                            stop=(kk == 7 and k2 == 1 and part == 2))
                                if kk == 7 and tb < 3:
                                    last.then_inc(z_done, 1)
                            last.then_inc(chunk_used, 1)


_INS = ['x', 'c', 'w_ada', 'b_ada', 'w_in', 'b_f', 'attn_sinks', 'w_br_fox', 'w_br_swa', 'w_out', 'ln_g', 'ln_b']


def kernel(**inputs):
    import numpy as _np
    import concourse.bacc as _bacc
    from concourse import mybir as _mybir
    from concourse.bass_utils import run_bass_kernel_spmd as _run

    nc = _bacc.Bacc("TRN2", target_bir_lowering=False, num_devices=1)
    arrays, args = {}, []
    for name in _INS:
        a = _np.ascontiguousarray(inputs[name])
        arrays[f"in_{name}_dram"] = a
        args.append(nc.dram_tensor(f"in_{name}_dram", a.shape, _mybir.dt.from_np(a.dtype), kind="ExternalInput").ap())
    out = nc.dram_tensor("out_dram", inputs["x"].shape, F32, kind="ExternalOutput").ap()
    build(nc, *args, out)
    r = _run(nc, [arrays], core_ids=[0])
    return r.results[0]["out_dram"]
```

```python
from contextlib import ExitStack

import concourse.bass as bass
from concourse import mybir

F32 = mybir.dt.float32
F32R = mybir.dt.float32r
ALU = mybir.AluOpType
ACT = mybir.ActivationFunctionType
AX = mybir.AxisListType
ds = bass.ds

P = 128
D = 2048
SEQ = 1024
HALF = 512
KD = D // P
FOX_HEADS = 8
FOX_WIDTH = 1024
SWA_HEADS = 16
SWA_KV = 4
SWA_D = 64
SWA_WIDTH = 1024
LN_EPS = 1e-5
NEG = -1e30
FAR = 1e34
ALPHA = 2.0 ** 0.25

COL_FLOG = 3 * FOX_WIDTH
COL_REST = COL_FLOG + FOX_HEADS
B_SQ = 1
B_SK = B_SQ + SWA_WIDTH // P
B_SV = B_SK + SWA_KV * SWA_D // P
B_FQ = B_SV + SWA_KV * SWA_D // P
B_FK = B_FQ + FOX_WIDTH // P
B_FV = B_FK + FOX_WIDTH // P
B_G = B_FV + FOX_WIDTH // P
B_M = B_G + (FOX_WIDTH + SWA_WIDTH) // P
BLOCKS = B_M + 2 * D // P
ADA_DVE = 6
DVE_COLS = 1408
MMS = 48
OG_ORDER = [*range(8, KD), *range(8)]
OG_GROUPS = [(0, 2), (2, 4), (4, 8), (8, 12), (12, 16)]
TAIL = 2 * BLOCKS


class Steps:

    def __init__(self, eng, sem):
        self.eng, self.sem, self.total, self.base, self.n = eng, sem, 0, 0, 0

    def enter(self, before=0):
        self.base, self.n = self.total + before, 0

    def leave(self, steps, times=1, per=None):
        assert self.n == (steps // times if per is None else per), (self.n, steps, times)
        self.total += steps

    def __call__(self, ins):
        self.n += 1
        ins.then_inc(self.sem, 1)
        self.eng.wait_ge(self.sem, self.base + self.n)


def build(nc, x, c, w_ada, b_ada, w_in, b_f, attn_sinks, w_br_fox, w_br_swa, w_out, ln_g, ln_b, out):
    x2 = x.rearrange("a (t p) d -> p (a t) d", p=P)
    out2 = out.rearrange("a (t p) d -> p (a t) d", p=P)
    ada_v = w_ada.rearrange("a (p k) n -> p (a k) n", p=P)
    w_in_v = w_in.rearrange("a (k p) n -> p (a k) n", p=P)
    wbf_v = w_br_fox.rearrange("a (k p) n -> p (a k) n", p=P)
    wbs_v = w_br_swa.rearrange("a (k p) n -> p (a k) n", p=P)
    w_out_v = w_out.rearrange("a (k p) n -> p (a k) n", p=P)

    proj_d = nc.dram_tensor("proj_scratch", (BLOCKS, P, SEQ), F32).ap()
    o_d = nc.dram_tensor("o_scratch", (KD, P, SEQ), F32).ap()
    gate_d = nc.dram_tensor("gate_scratch", (1, D), F32).ap()
    q_heads = proj_d[B_SQ:B_SK].rearrange("b (e d) t -> d (b e) t", d=SWA_D)
    k_heads = proj_d[B_SK:B_SV].rearrange("b (e d) t -> d (b e) t", d=SWA_D)
    o_heads = o_d[FOX_HEADS:KD].rearrange("b (e d) t -> d (b e) t", d=SWA_D)

    ctx = ExitStack()
    with ctx:
        def sem(name):
            return ctx.enter_context(nc.semaphore(name))

        def psum(name, shape):
            return ctx.enter_context(nc.psum_tensor(name, shape, F32))

        def sb(name, shape, dt=F32, scope=ctx):
            return scope.enter_context(nc.sbuf_tensor(name, shape, dt))

        w_raw = sb("w_raw", [P, 2, 1024])
        w_hi = sb("w_hi", [P, 2, 1024], F32R)
        w_lo = sb("w_lo", [P, 2, 1024], F32R)
        chunk_loaded = [sem("chunk_loaded_0"), sem("chunk_loaded_1")]
        chunk_hi = sem("chunk_hi")
        chunk_lo = sem("chunk_lo")
        chunk_used = sem("chunk_used")
        dve_step = sem("dve_step")
        act_step = sem("act_step")

        def load_chunk(sp, n, slot, source, first=False):
            if not first:
                sp.wait_ge(chunk_lo, n - 1)
            dst = w_raw[:, slot, :].rearrange("p (k n) -> p k n", k=source.shape[1])
            sp.dma_start(dst, source).then_inc(chunk_loaded[slot], 16)

        def split_hi(act, n, slot, loads):
            act.wait_ge(chunk_loaded[slot], 16 * loads)
            if not (isinstance(n, int) and n < 2):
                act.wait_ge(chunk_used, n - 1)
            nc.scalar.copy(w_hi[:, slot, :], w_raw[:, slot, :]).then_inc(chunk_hi, 1)

        def split_lo(dve, n, slot):
            dve.wait_ge(chunk_hi, n + 1)
            nc.vector.tensor_tensor(w_lo[:, slot, :], w_raw[:, slot, :], w_hi[:, slot, :].bitcast(F32),
                                    ALU.subtract).then_inc(chunk_lo, 1)

        def load_og(sp, q):
            n0, n1 = OG_GROUPS[q]
            k0 = OG_ORDER[n0]
            for half, (src, base) in enumerate(((proj_d, B_G), (o_d, 0))):
                sp.dma_start(go_in[:, n0:n1, half, :],
                             src[base + k0:base + k0 + n1 - n0, :, 0:HALF].rearrange("k p t -> p k t")
                             ).then_inc(og_in[q], 16)

        main = ExitStack()
        with main:
            psums = ExitStack()
            main.enter_context(psums)

            def pst(name, shape):
                return psums.enter_context(nc.psum_tensor(name, shape, F32))

            projP = pst("projP", [P, 2, HALF])
            sP = pst("sP", [P, 2, HALF])
            tP = pst("tP", [P, 2, HALF])
            oP = pst("oP", [P, HALF])
            adaP = pst("adaP", [P, HALF])

            with ExitStack() as x_scope:
                x_t = sb("x_t", [P, 2, D], F32, x_scope)
            h_hi = sb("h_hi", [P, KD, SEQ], F32R, main)
            with ExitStack() as before_h_lo:
                xnT = sb("xnT", [P, KD, SEQ], F32, before_h_lo)
            with ExitStack() as after_h_lo:
                go_in = sb("go_in", [P, KD, 2, HALF], F32, after_h_lo)
            h_lo = sb("h_lo", [P, KD, SEQ], F32R, main)
            stage = sb("stage", [P, 2, HALF], F32, main)
            ident = sb("ident", [P, P], F32, main)
            ident_r = sb("ident_r", [P, P], F32R, main)
            mask_r = sb("mask_r", [P, P], F32R, main)
            cum_k = sb("cum_k", [P, SEQ], F32R, main)
            cum_q = sb("cum_q", [P, SEQ], F32R, main)
            head_sel = sb("head_sel", [P, FOX_HEADS], F32, main)
            c_sb = sb("c_sb", [P, KD + 1], F32, main)
            neg_max = sb("neg_max", [P, 4], F32, main)
            row_sum = sb("row_sum", [P, 4], F32, main)
            row_inv = sb("row_inv", [P, 4], F32, main)
            sink_exp = sb("sink_exp", [P, 4], F32, main)

            with ExitStack() as s0:
                ada_raw = sb("ada_raw", [P, 2, KD, 2, P], F32, s0)
                ada_rows = sb("ada_rows", [2 * KD, P], F32, s0)
                ada_b = sb("ada_b", [P, 2, KD], F32, s0)
                ada_s = sb("ada_s", [P, KD, 2], F32, s0)
                ada_acc = sb("ada_acc", [P, 2, 2 * P], F32, s0)
                ada_row = sb("ada_row", [1, 2, 2 * P], F32, s0)
                bn = sb("bn", [P, 4, 6], F32, s0)
                mv = sb("mv", [P, 2], F32, s0)
                sm = sb("sm", [P, 4], F32, s0)
            with ExitStack() as s1:
                gate_raw = sb("gate_raw", [P, D], F32, s1)
                gate_acc = sb("gate_acc", [P, D], F32, s1)
                fg = [sb(f"fg{i}", [FOX_HEADS, SEQ], F32, s1) for i in range(5)]
                bf_c = sb("bf_c", [FOX_HEADS, 1], F32, s1)
                ones = sb("ones", [P, 1], F32, s1)
            gate_row = gate_raw[0:1, :]
            with ExitStack() as s2:
                sq_raw = sb("sq_raw", [P, 8, P], F32, s2)
                sk_raw = sb("sk_raw", [P, 2, P], F32, s2)
                sv_raw = sb("sv_raw", [P, 2, P], F32, s2)
                sq = sb("sq", [P, 8, P], F32R, s2)
                sk_hi = sb("sk_hi", [P, 2, 2, P], F32R, s2)
                sk_lo = sb("sk_lo", [SWA_D, 2, 2, P], F32R, s2)
                sv = sb("sv", [P, 2, 2, 2, SWA_D], F32R, s2)
                s_bias = sb("s_bias", [P, 2, 4, 2, P], F32, s2)
                dist = sb("dist", [P, 2, P], F32, s2)
                no_prev = sb("no_prev", [P, 4], F32, s2)
                sinks = sb("sinks", [P, SWA_HEADS], F32, s2)
                neg_sinks = sb("neg_sinks", [P, SWA_HEADS], F32, s2)
                sp_w = sb("sp_w", [P, 4, 2, P], F32, s2)
                spT_hi = sb("spT_hi", [P, 2, 4 * P], F32R, s2)
                spT_lo = sb("spT_lo", [P, 2, 4 * P], F32R, s2)
                so_st = sb("so_st", [SWA_D, 2, HALF], F32, s2)
            with ExitStack() as s3:
                fq_raw = sb("fq_raw", [P, 2, P], F32, s3)
                fv_raw = sb("fv_raw", [P, SEQ], F32, s3)
                fk_raw = sb("fk_raw", [P, SEQ], F32, s3)
                fq_hi = sb("fq_hi", [P, P], F32R, s3)
                fq_lo = sb("fq_lo", [P, P], F32R, s3)
                fk_hi = sb("fk_hi", [P, SEQ], F32R, s3)
                fk_lo = sb("fk_lo", [P, SEQ], F32R, s3)
                fv_hi = sb("fv_hi", [P, 8, P], F32R, s3)
                fv_lo = sb("fv_lo", [P, 8, P], F32R, s3)
                fcq = sb("fcq", [P, P], F32R, s3)
                fp_w = sb("fp_w", [P, 8, P], F32, s3)
                fpT = sb("fpT", [P, 8, 2, P], F32R, s3)
                fo_st = sb("fo_st", [P, P], F32, s3)

            og_in = [sem(f"og_in_{q}") for q in range(len(OG_GROUPS))]
            x_loaded = [sem("x_loaded_0"), sem("x_loaded_1")]
            x_normed = sem("x_normed")
            x_var = sem("x_var")
            x_std = sem("x_std")
            x_turned = sem("x_turned")
            xt_copied = sem("xt_copied")
            ada_loaded = [sem(f"ada_loaded_{slot}_{half}") for slot in range(2) for half in range(2)]
            ada_half = sem("ada_half")
            ada_done = sem("ada_done")
            small_loaded = sem("small_loaded")
            mod_ready = sem("mod_ready")
            ada_summed = sem("ada_summed")
            ada_row_ready = sem("ada_row_ready")
            ada_turned = sem("ada_turned")
            ada_b_ready = sem("ada_b_ready")
            c_one = sem("c_one")
            c_loaded = sem("c_loaded")
            x_stats = sem("x_stats")
            ada_b_turned = sem("ada_b_turned")
            ada_read = sem("ada_read")
            s_scaled = sem("s_scaled")
            h_hi_ready = sem("h_hi_ready")
            h_ready = sem("h_ready")
            consts = sem("consts")
            pool_step = sem("pool_step")
            ident_ready = sem("ident_ready")
            half0_done = sem("half0_done")
            proj_copied = sem("proj_copied")
            proj_stored = [sem("proj_stored_0"), sem("proj_stored_1")]
            gate_loaded = sem("gate_loaded")
            gate_added = sem("gate_added")
            gate_summed = sem("gate_summed")
            gate_ready = sem("gate_ready")
            gate_stored = sem("gate_stored")
            fg_loaded = sem("fg_loaded")
            fg_neg = sem("fg_neg")
            fg_exp = sem("fg_exp")
            cum_done = sem("cum_done")
            cum_hi = sem("cum_hi")
            cum_ready = sem("cum_ready")
            s_loaded = [sem("s_loaded_0"), sem("s_loaded_1")]
            s_hi = sem("s_hi")
            s_prep = sem("s_prep")
            s_vt = sem("s_vt")
            s_vt_hi = sem("s_vt_hi")
            s_v = sem("s_v")
            s_qk = sem("s_qk")
            s_biased = sem("s_biased")
            s_max = sem("s_max")
            s_exp = sem("s_exp")
            s_inv = sem("s_inv")
            s_norm = sem("s_norm")
            s_turned = sem("s_turned")
            s_pt_hi = sem("s_pt_hi")
            s_pt = sem("s_pt")
            s_pv = sem("s_pv")
            s_half = sem("s_half")
            s_o = sem("s_o")
            s_stored = sem("s_stored")
            f_q_loaded = [sem("f_q_loaded_0"), sem("f_q_loaded_1")]
            f_kv_loaded = sem("f_kv_loaded")
            f_k_hi = sem("f_k_hi")
            f_k = sem("f_k")
            f_vt = sem("f_vt")
            f_vt_hi = sem("f_vt_hi")
            f_v = sem("f_v")
            f_q_hi = sem("f_q_hi")
            f_q = sem("f_q")
            f_qk = sem("f_qk")
            f_max = sem("f_max")
            f_exp = sem("f_exp")
            f_inv = sem("f_inv")
            f_norm = sem("f_norm")
            f_turned = sem("f_turned")
            f_pt_hi = sem("f_pt_hi")
            f_pt = sem("f_pt")
            f_pv = sem("f_pv")
            f_half = sem("f_half")
            f_o = sem("f_o")
            f_stored = sem("f_stored")

            block = main.enter_context(nc.Block())

            def col_rest(b):
                return COL_REST + P * (b - 1) - P * (B_G - B_FQ)

            @block.sync
            def _(sp):
                def load_ada(j, slot, first=False):
                    for kh in range(2):
                        if not first and kh == 0:
                            sp.wait_ge(ada_summed, j - 1)
                            sp.wait_ge(ada_half, j - 1)
                        if not first and kh == 1:
                            sp.wait_ge(ada_done, j - 1)
                        for s in range(2):
                            sp.dma_start(ada_raw[:, slot, 8 * kh:8 * kh + 8, s, :],
                                         ada_v[:, 8 * kh:8 * kh + 8, ds(s * D + j * P, P)]
                                         ).then_inc(ada_loaded[2 * slot + kh], 16)

                sp.dma_start(x_t[:, 0, :], x2[:, 0, :]).then_inc(x_loaded[0], 16)
                sp.dma_start(c_sb[:, 0:KD], c.rearrange("a (p k) -> p (a k)", p=P)).then_inc(c_loaded, 16)
                sp.dma_start(ada_rows[:], b_ada[0, 0:2 * D].rearrange("(r p) -> r p", p=P)).then_inc(c_loaded, 16)
                load_ada(0, 0, first=True)
                sp.dma_start(x_t[:, 1, :], x2[:, 1, :]).then_inc(x_loaded[1], 16)
                load_ada(1, 1, first=True)
                with sp.Fori(1, 4) as g:
                    for t in range(2):
                        load_ada(2 * g + t, t)
                        sp.wait_ge(x_turned, 4 * (2 * g + (t - 1)))
                        sp.dma_start(x_t[:, t, :], x2[:, ds(2 * g + t, 1), :]
                                     .rearrange("p a d -> p (a d)")).then_inc(x_loaded[t], 16)

                def block_in(b, col, first=False):
                    for kh in range(2):
                        load_chunk(sp, 2 * b + kh, kh, w_in_v[:, 8 * kh:8 * kh + 8, ds(col, P)], first)

                block_in(0, COL_FLOG, first=True)
                with sp.Fori(4, KD // 2) as g:
                    for t in range(2):
                        load_ada(2 * g + t, t)
                with sp.Fori(B_SQ, B_FQ) as b:
                    block_in(b, COL_REST + P * (b - 1))
                for s in range(2):
                    sp.wait_ge(proj_stored[s], 16)
                sp.dma_start(fg[0][:], proj_d[0, 0:FOX_HEADS, :]).then_inc(fg_loaded, 16)
                sp.dma_start(bf_c[:], b_f.rearrange("a h -> h a"), allow_slow_non_contiguous=True).then_inc(fg_loaded, 16)
                sp.wait_ge(consts, 1)
                with sp.Fori(0, KD) as k:
                    block_in(k + B_FQ, P * k)
                    sp.wait_ge(gate_added, k + 1)
                    sp.dma_start(gate_raw[:], ada_v[:, ds(k, 1), 2 * D:3 * D]
                                 .rearrange("p a n -> p (a n)")).then_inc(gate_loaded, 16)
                sp.wait_ge(gate_added, KD)
                block_in(B_FQ + KD, P * KD)
                sp.wait_ge(gate_added, KD + 1)
                sp.dma_start(gate_row, b_ada[:, 2 * D:3 * D]).then_inc(gate_loaded, 16)
                with sp.Fori(B_FQ + KD + 1, B_G) as b:
                    block_in(b, P * (b - B_FQ))

                for s in range(2):
                    sp.wait_ge(proj_stored[s], 16 * B_FQ)
                with sp.Fori(0, 2) as g:
                    with sp.Fori(0, 4) as m:
                        for par in range(2):
                            u = 8 * g + 2 * m + par
                            block_in(u + B_G, COL_REST + P * (u + (B_FQ - 1)))
                            sp.wait_ge(s_prep, 2 * u + 1)
                            if par == 0:
                                sp.wait_ge(gate_stored, 16)
                                sp.wait_ge(cum_ready, 2)
                            t0 = (2 * m + par) * P
                            for r in (slice(0, SWA_D), slice(SWA_D, P)):
                                sp.dma_start(sq_raw[r], q_heads[:, ds(8 * g, 8), ds(t0, P)]
                                             ).then_inc(s_loaded[par], 16)
                                sp.dma_start(sk_raw[r], k_heads[:, ds(2 * g, 2), ds(t0, P)]
                                             ).then_inc(s_loaded[par], 16)
                            sp.dma_start(sv_raw[:, par, :], proj_d[ds(g + B_SV, 1), :, ds(t0, P)]
                                         .rearrange("a p t -> p (a t)")).then_inc(s_loaded[par], 16)

                sp.sem_inc(f_q, 2)
                for s in range(2):
                    sp.wait_ge(proj_stored[s], 16 * B_G)
                with sp.Fori(0, FOX_HEADS) as h:
                    for i in range(8):
                        if i % 2 == 0:
                            block_in(4 * h + (B_M + i // 2), 4 * P * h + (col_rest(B_M) + P * (i // 2)))
                        if i == 0:
                            sp.wait_ge(s_v, 16)
                            sp.wait_ge(s_qk, 32 + 1)
                            sp.wait_ge(f_k, h + 1)
                            sp.wait_ge(f_vt, h + 1)
                            for base, dst in ((B_FK, fk_raw), (B_FV, fv_raw)):
                                sp.dma_start(dst[:], proj_d[ds(h + base, 1), :, :]
                                             .rearrange("a p t -> p (a t)")).then_inc(f_kv_loaded, 16)
                        sp.wait_ge(f_q, 8 * h + (i + 1))
                        sp.dma_start(fq_raw[:, i % 2, :], proj_d[ds(h + B_FQ, 1), :, i * P:(i + 1) * P]
                                     .rearrange("a p t -> p (a t)")).then_inc(f_q_loaded[i % 2], 16)
                load_chunk(sp, TAIL, 0, wbs_v[:, :, 0:P])
                sp.wait_ge(chunk_used, TAIL - 1)
                sp.wait_ge(s_stored, 256 + 1)
                load_og(sp, 0)
                load_og(sp, 1)
                load_chunk(sp, TAIL + 1, 1, wbs_v[:, :, P:2 * P])
                load_og(sp, 2)

            @block.gpsimd
            def _(pool):
                own = Steps(pool, pool_step)
                for signal in (gate_added, s_prep, s_qk, s_biased, s_pt, s_o, s_stored, f_k, f_vt, f_qk, f_exp, f_pt, f_o,
                               f_stored):
                    pool.sem_inc(signal, 1)
                own.enter()
                own(nc.gpsimd.memset(ident[:], 0.0))
                nc.gpsimd.affine_select(out=ident[:], in_=ident[:], compare_op=ALU.not_equal, fill=1.0, base=0,
                                        pattern=[[-1, P]], channel_multiplier=1).then_inc(ident_ready, 1)
                own(nc.gpsimd.memset(head_sel[:], 0.0))
                for q in range(4):
                    own(nc.gpsimd.affine_select(out=head_sel[:], in_=head_sel[:], compare_op=ALU.not_equal, fill=1.0,
                                                base=-32 * q, pattern=[[-1, FOX_HEADS]], channel_multiplier=1))
                pool.wait_ge(h_ready, KD)
                own(nc.gpsimd.memset(gate_raw[:, 0:P], 0.0))
                own(nc.gpsimd.affine_select(out=gate_raw[:, 0:P], in_=gate_raw[:, 0:P], compare_op=ALU.is_ge,
                                            fill=NEG, base=0, pattern=[[-1, P]], channel_multiplier=1))
                own(nc.gpsimd.tensor_copy(mask_r[:], gate_raw[:, 0:P]))
                pool.wait_ge(ident_ready, 1)
                own(nc.gpsimd.tensor_copy(ident_r[:], ident[:]))
                for t in (cum_k, cum_q):
                    own(nc.gpsimd.memset(t[:].bitcast(F32), 0.0))
                for t, q in ((cum_q, 0), (cum_q, 32), (cum_k, 64), (cum_k, 96)):
                    own(nc.gpsimd.memset(t[q:q + FOX_HEADS, :].bitcast(F32), 1.0))
                own(nc.gpsimd.memset(ones[:], 1.0))
                nc.gpsimd.memset(gate_acc[:], 0.0).then_inc(consts, 1)

                pool.wait_ge(gate_stored, 16)
                pool.wait_ge(cum_ready, 2)
                for t in (sv, sk_hi, sk_lo):
                    own(nc.gpsimd.memset(t[:].bitcast(F32), 0.0))
                own(nc.gpsimd.memset(no_prev[:], 0.0))
                own(nc.gpsimd.memset(no_prev[:, 0:1], NEG))
                pool.dma_start(sinks[:], attn_sinks.broadcast_to([P, SWA_HEADS])).then_inc(small_loaded, 16)
                own(nc.gpsimd.iota(dist[:], pattern=[[-P, 2], [-1, P]], base=P, channel_multiplier=1,
                                   allow_small_or_imprecise_dtypes=True))
                own(nc.gpsimd.affine_select(out=dist[:, 1, :], in_=dist[:, 1, :], compare_op=ALU.is_ge, fill=FAR,
                                            base=0, pattern=[[-1, P]], channel_multiplier=1))
                nc.gpsimd.affine_select(out=dist[:, 0, :], in_=dist[:, 0, :], compare_op=ALU.is_gt, fill=FAR,
                                        base=0, pattern=[[1, P]], channel_multiplier=-1).then_inc(consts, 1)
                with pool.Fori(0, 32) as s:
                    pool.wait_ge(s_inv, s + 1)
                    for i in range(2):
                        w = sp_w[:, i].rearrange("p k t -> p (k t)")
                        last = nc.gpsimd.tensor_tensor(w, w, row_inv[:, i:i + 1].broadcast_to([P, 2 * P]), ALU.mult)
                    last.then_inc(s_norm, 1)
                with pool.Fori(0, FOX_HEADS) as h:
                    for i in range(8):
                        pool.wait_ge(f_inv, 8 * h + (i + 1))
                        w = fp_w[:, 0:i + 1].rearrange("p j t -> p (j t)")
                        nc.gpsimd.tensor_tensor(w, w, row_inv[:, 0:1].broadcast_to([P, (i + 1) * P]),
                                                ALU.mult).then_inc(f_norm, 1)

            @block.scalar
            def _(act):
                def ada_row_out(j, slot, first=False):
                    act.wait_ge(ada_done, j + 1)
                    if not first:
                        act.wait_ge(ada_turned, j - 1)
                    nc.scalar.copy(ada_row[:, slot, :], (adaP if slot else oP)[0:1, 0:2 * P]
                                   ).then_inc(ada_row_ready, 1)

                def x_step(t, slot, first=False):
                    act.wait_ge(x_var, t + 1)
                    nc.scalar.activation(sm[:, 1:2], sm[:, 0:1], ACT.Sqrt).then_inc(x_std, 1)
                    ada_row_out(t, slot, first)
                    for q in range(4):
                        act.wait_ge(x_turned, 4 * t + (q + 1))
                        nc.scalar.copy(xnT[:, 4 * q:4 * q + 4, ds(t * P, P)],
                                       (sP if q < 2 else tP)[:, q % 2, :].rearrange("p (j t) -> p j t", j=4)
                                       ).then_inc(xt_copied, 1)

                def modulate(j):
                    act.wait_ge(ada_read, j + 1)
                    nc.scalar.activation(xnT[:, ds(j, 1), :], xnT[:, ds(j, 1), :], ACT.Identity,
                                         bias=ada_s[:, ds(j, 1), 0:1].rearrange("p a s -> p (a s)"),
                                         scale=ada_s[:, ds(j, 1), 1:2].rearrange("p a s -> p (a s)")
                                         ).then_inc(mod_ready, 1)
                    act.wait_ge(mod_ready, j + 1)
                    nc.scalar.copy(h_hi[:, ds(j, 1), :], xnT[:, ds(j, 1), :]).then_inc(h_hi_ready, 1)

                for slot in range(2):
                    x_step(slot, slot, first=True)
                with act.Fori(1, 4) as g:
                    for slot in range(2):
                        x_step(2 * g + slot, slot)
                for e in range(2):
                    split_hi(act, e, e, 1)
                act.wait_ge(xt_copied, 32)
                with act.Fori(4, 7) as g:
                    for slot in range(2):
                        j = 2 * g + slot
                        modulate(2 * (j - 8))
                        modulate(2 * (j - 8) + 1)
                        ada_row_out(j, slot)
                for slot in range(2):
                    modulate(KD - 4 + slot)
                    ada_row_out(KD - 2 + slot, slot)
                modulate(KD - 2)
                modulate(KD - 1)

                def copy_proj(b, half):
                    if half == 0:
                        act.wait_ge(half0_done, b + 1)
                    else:
                        act.wait_ge(chunk_used, 2 * b + 2)
                    if not (isinstance(b, int) and b == 0):
                        act.wait_ge(proj_stored[half], 16 * b)
                    nc.scalar.copy(stage[:, half, :], projP[:, half, :]).then_inc(proj_copied, 1)
                    act.wait_ge(proj_copied, 2 * b + (half + 1))
                    dst = proj_d[ds(b, 1), :, half * HALF:(half + 1) * HALF].rearrange("a p t -> p (a t)")
                    act.dma_start(dst, stage[:, half, :]).then_inc(proj_stored[half], 16)

                def proj_step(b, first=False):
                    if not first:
                        split_hi(act, 2 * b + 1, 1, b + 1)
                    split_hi(act, 2 * b + 2, 0, b + 2)
                    copy_proj(b, 0)
                    copy_proj(b, 1)

                proj_step(0, first=True)
                with act.Fori(B_SQ, B_FQ) as b:
                    proj_step(b)
                act.wait_ge(fg_neg, 1)
                nc.scalar.activation(fg[2][:], fg[1][:], ACT.Exp).then_inc(fg_exp, 1)
                with act.Fori(B_FQ, B_FQ + KD) as b:
                    proj_step(b)
                act.wait_ge(cum_done, 1)
                nc.scalar.activation(cum_k[0:FOX_HEADS, :], fg[4][:], ACT.Copy, scale=-1.0).then_inc(cum_hi, 1)
                nc.scalar.copy(cum_q[64:64 + FOX_HEADS, :], fg[4][:]).then_inc(cum_hi, 1)
                proj_step(B_FQ + KD)
                act.wait_ge(gate_ready, 1)
                act.dma_start(gate_d, gate_row).then_inc(gate_stored, 16)
                with act.Fori(B_FQ + KD + 1, B_G) as b:
                    proj_step(b)

                def high_parts(slot, loads, u):
                    act.wait_ge(s_loaded[slot], 80 * loads)
                    act.wait_ge(s_qk, 2 * u + 1)
                    nc.scalar.activation(sq[:], sq_raw[:], ACT.Copy, scale=SWA_D ** -0.5)
                    nc.scalar.copy(sk_hi[:, slot], sk_raw[:]).then_inc(s_hi, 1)

                def unit(g, m, par, last=False):
                    u = 8 * g + 2 * m + par
                    b = u + B_G
                    act.wait_ge(s_vt, u + 1)
                    nc.scalar.copy(sv[:, par, :, 0, :], tP[:, 0, 0:P].rearrange("p (e d) -> p e d", e=2)
                                   ).then_inc(s_vt_hi, 1)
                    for e in range(2):
                        s = 2 * u + e
                        split_hi(act, 2 * b + (e + 1), 1 - e, b + (e + 1))
                        act.wait_ge(s_max, s + 1)
                        for i in range(4):
                            nc.scalar.activation(sp_w[:, i], sp_w[:, i], ACT.Exp, bias=neg_max[:, i:i + 1],
                                                 accum_out=row_sum[:, i:i + 1])
                        nc.scalar.activation(sink_exp[:], sink_exp[:], ACT.Exp).then_inc(s_exp, 1)
                        if e == 1:
                            copy_proj(b, 0)
                        for k in range(2):
                            act.wait_ge(s_turned, 2 * s + (k + 1))
                            nc.scalar.copy(spT_hi[:, k, :], tP[:, k, :]).then_inc(s_pt_hi, 1)
                    if not last:
                        high_parts(1 - par, 4 * g + m + (par + 1), u + 1)
                    copy_proj(b, 1)
                    act.wait_ge(s_pv, 2 * u + 2)
                    act.wait_ge(s_stored, 16 * u + 1)
                    for e in range(2):
                        nc.scalar.copy(so_st[:, e, :], (oP, adaP)[e][SWA_D:P, :]).then_inc(s_half, 1)
                    act.wait_ge(s_o, 2 * u + 3)
                    act.dma_start(o_heads[:, ds(8 * g, 8), ds((2 * m + par) * P, P)],
                                  so_st[:].rearrange("d e (i t) -> d (e i) t", i=4)).then_inc(s_stored, 16)

                act.wait_ge(consts, 2)
                high_parts(0, 1, 0)
                for g in range(2):
                    with act.Fori(0, 4 - g) as m:
                        unit(g, m, 0)
                        unit(g, m, 1)
                unit(1, 3, 0)
                unit(1, 3, 1, last=True)

                with act.Fori(0, FOX_HEADS) as h:
                    def q_high(i):
                        act.wait_ge(f_q_loaded[i % 2], 64 * h + 16 * (i // 2 + 1))
                        act.wait_ge(f_qk, 8 * h + i + 1)
                        nc.scalar.activation(fq_hi[:], fq_raw[:, i % 2, :], ACT.Copy,
                                             scale=float(P) ** -0.5).then_inc(f_q_hi, 1)

                    q_high(0)
                    act.wait_ge(f_kv_loaded, 32 * h + 32)
                    nc.scalar.copy(fk_hi[:], fk_raw[:]).then_inc(f_k_hi, 1)
                    act.wait_ge(f_vt, h + 2)
                    for k in range(2):
                        last = nc.scalar.copy(fv_hi[:, 4 * k:4 * k + 4, :],
                                              tP[:, k, :].rearrange("p (j t) -> p j t", j=4))
                    last.then_inc(f_vt_hi, 1)
                    turned = 0
                    for i in range(8):
                        b = 4 * h + (B_M + i // 2)
                        e = i % 2
                        split_hi(act, 2 * b + (e + 1), 1 - e, b + (e + 1))
                        act.wait_ge(f_max, 8 * h + (i + 1))
                        nc.scalar.activation(fp_w[:, 0:i + 1, :].rearrange("p j t -> p (j t)"),
                                             sP[:, :, :].rearrange("p a t -> p (a t)")[:, 0:(i + 1) * P], ACT.Exp,
                                             bias=neg_max[:, 0:1], accum_out=row_sum[:, 0:1]).then_inc(f_exp, 1)
                        if e == 1:
                            copy_proj(b, 0)
                        for k in range(i // 4 + 1):
                            turned += 1
                            n = min(4, i + 1 - 4 * k)
                            act.wait_ge(f_turned, 12 * h + turned)
                            nc.scalar.copy(fpT[:, 4 * k:4 * k + n, 0, :],
                                           tP[:, k, 0:n * P].rearrange("p (j t) -> p j t", j=n)).then_inc(f_pt_hi, 1)
                        if i < 7:
                            q_high(i + 1)
                        if e == 1:
                            copy_proj(b, 1)
                        act.wait_ge(f_pv, 8 * h + (i + 1))
                        act.wait_ge(s_stored, 256 + 1)
                        act.wait_ge(f_stored, 128 * h + 16 * i + 1)
                        nc.scalar.copy(fo_st[:], oP[:, 0:P]).then_inc(f_half, 1)
                        act.wait_ge(f_o, 8 * h + (i + 2))
                        act.dma_start(o_d[ds(h, 1), :, i * P:(i + 1) * P].rearrange("a p t -> p (a t)"),
                                      fo_st[:]).then_inc(f_stored, 16)

            @block.vector
            def _(dve):
                own = Steps(dve, dve_step)
                nc.vector.memset(c_sb[:, KD:KD + 1], 1.0).then_inc(c_one, 1)
                dve.wait_ge(ada_b_turned, 1)
                nc.vector.tensor_copy(ada_b[:, 0, :], projP[:, 0, 0:KD])
                nc.vector.tensor_scalar(ada_b[:, 1, :], projP[:, 0, KD:2 * KD], 1.0, None, ALU.add
                                        ).then_inc(ada_b_ready, 1)
                dve.wait_ge(ada_b_ready, 1)

                def ada_sum(slot, loads):
                    dve.wait_ge(ada_loaded[2 * slot], 32 * loads)
                    w = ada_raw[:, slot].rearrange("p k s n -> p k (s n)")
                    a = ada_acc[:, slot, :]
                    own(nc.vector.tensor_scalar(a, w[:, 0, :], c_sb[:, 0:1], None, ALU.mult))
                    for k in range(1, ADA_DVE):
                        ins = nc.vector.scalar_tensor_tensor(out=a, in0=w[:, k, :], scalar=c_sb[:, k:k + 1], in1=a,
                                                             op0=ALU.mult, op1=ALU.add)
                        if k < ADA_DVE - 1:
                            own(ins)
                    ins.then_inc(ada_summed, 1)

                def ada_take(j, slot, bank=projP):
                    dve.wait_ge(ada_turned, j + 1)
                    nc.vector.tensor_tensor(ada_s[:, ds(j, 1), :].rearrange("p a s -> p (a s)"),
                                            bank[:, slot, 0:2],
                                            ada_b[:, :, ds(j, 1)].rearrange("p s a -> p (s a)"),
                                            ALU.add).then_inc(ada_read, 1)

                def x_step(t, slot, loads, first=False):
                    dve.wait_ge(x_loaded[slot], 16 * loads)
                    for q in range(4):
                        last = nc.vector.bn_stats(bn[:, q, :], x_t[:, slot, q * HALF:(q + 1) * HALF])
                    last.then_inc(x_stats, 1)
                    dve.wait_ge(x_stats, t + 1)
                    nc.vector.memset(sm[:, 2:3], 0.0)
                    own(nc.vector.bn_aggr(mv[:], bn[:].rearrange("p a b -> p (a b)")))
                    nc.vector.tensor_scalar(sm[:, 0:1], mv[:, 1:2], LN_EPS, None, ALU.add).then_inc(x_var, 1)
                    if first and slot == 0:
                        dve.wait_ge(c_loaded, 32)
                    ada_sum(slot, loads)
                    if not first:
                        ada_take(t - 2, slot)
                    dve.wait_ge(x_std, t + 1)
                    own(nc.vector.reciprocal(sm[:, 2:3], sm[:, 1:2]))
                    own(nc.vector.tensor_tensor(sm[:, 3:4], sm[:, 2:3], sm[:, 2:3], ALU.mult))
                    own(nc.vector.tensor_tensor(sm[:, 3:4], sm[:, 3:4], sm[:, 0:1], ALU.mult))
                    own(nc.vector.tensor_scalar(sm[:, 3:4], sm[:, 3:4], -0.5, 1.5, ALU.mult, ALU.add))
                    own(nc.vector.tensor_tensor(sm[:, 3:4], sm[:, 3:4], sm[:, 2:3], ALU.mult))
                    nc.vector.tensor_scalar(x_t[:, slot, :], x_t[:, slot, :], mv[:, 0:1], sm[:, 3:4],
                                            ALU.subtract, ALU.mult).then_inc(x_normed, 1)
                    dve.wait_ge(x_normed, t + 1)

                def h_low(j):
                    dve.wait_ge(h_hi_ready, j + 1)
                    nc.vector.tensor_tensor(h_lo[:, ds(j, 1), :], xnT[:, ds(j, 1), :],
                                            h_hi[:, ds(j, 1), :].bitcast(F32), ALU.subtract).then_inc(h_ready, 1)

                XS = 6 + ADA_DVE - 1
                AS = ADA_DVE - 1
                own.enter()
                for slot in range(2):
                    x_step(slot, slot, 1, first=True)
                own.leave(2 * XS)
                with dve.Fori(0, 3) as g:
                    own.enter(2 * XS * g)
                    for slot in range(2):
                        x_step(2 * g + (slot + 2), slot, g + 2)
                own.leave(6 * XS, 3)
                for e in range(2):
                    split_lo(dve, e, e)

                def h_step(g, bank):
                    for slot in range(2):
                        j = 2 * g + (slot + 8)
                        ada_sum(slot, g + 5)
                        ada_take(j - 2, slot, bank)
                        h_low(2 * (2 * g + slot))
                        h_low(2 * (2 * g + slot) + 1)

                own.enter()
                h_step(0, projP)
                own.leave(2 * AS)
                with dve.Fori(0, 2) as g:
                    own.enter(2 * AS * g)
                    h_step(g + 1, sP)
                own.leave(4 * AS, 2)
                own.enter()
                for slot in range(2):
                    j = KD - 2 + slot
                    ada_sum(slot, KD // 2)
                    ada_take(j - 2, slot, sP)
                    h_low(KD - 4 + slot)
                own.leave(2 * AS)
                for j in range(KD - 2, KD):
                    ada_take(j, j % 2, sP)
                for j in range(KD - 2, KD):
                    h_low(j)

                def proj_step(b, first=False):
                    if not first:
                        split_lo(dve, 2 * b + 1, 1)
                    split_lo(dve, 2 * b + 2, 0)

                proj_step(0, first=True)
                with dve.Fori(B_SQ, B_FQ) as b:
                    proj_step(b)
                z, a, e, t, acc = [f[:] for f in fg]
                dve.wait_ge(fg_loaded, 32)
                dve.wait_ge(consts, 1)

                def gate_step(k):
                    proj_step(k + B_FQ)
                    dve.wait_ge(gate_loaded, 16 * (k + 1))
                    nc.vector.scalar_tensor_tensor(out=gate_acc[:], in0=gate_raw[:], scalar=c_sb[:, ds(k, 1)],
                                                   in1=gate_acc[:], op0=ALU.mult, op1=ALU.add).then_inc(gate_added, 1)
                    dve.wait_ge(gate_added, k + 2)

                own.enter()
                own(nc.vector.tensor_scalar(z, z, bf_c[:, 0:1], None, ALU.add))
                own(nc.vector.tensor_scalar(t, z, -1.0, None, ALU.mult))
                nc.vector.tensor_tensor(a, z, t, ALU.min).then_inc(fg_neg, 1)
                own(nc.vector.tensor_scalar(z, z, 0.0, None, ALU.min))
                own.leave(3)
                gate_step(0)
                own.enter()
                dve.wait_ge(fg_exp, 1)
                own(nc.vector.tensor_scalar(t, e, 2.0, None, ALU.add))
                own(nc.vector.reciprocal(t, t))
                own.leave(2)
                gate_step(1)
                own.enter()
                own(nc.vector.tensor_tensor(a, e, t, ALU.mult))
                own(nc.vector.tensor_tensor(t, a, a, ALU.mult))
                own(nc.vector.tensor_scalar(acc, t, 1.0 / 15.0, None, ALU.mult))
                own.leave(3)
                gate_step(2)

                def series(n):
                    own(nc.vector.scalar_tensor_tensor(out=acc, in0=acc, scalar=1.0 / (2 * n + 1), in1=t,
                                                       op0=ALU.add, op1=ALU.mult))

                for k in range(3):
                    own.enter()
                    series(6 - 2 * k)
                    series(5 - 2 * k)
                    own.leave(2)
                    gate_step(3 + k)
                own.enter()
                own(nc.vector.scalar_tensor_tensor(out=acc, in0=acc, scalar=1.0, in1=a, op0=ALU.add, op1=ALU.mult))
                own(nc.vector.scalar_tensor_tensor(out=a, in0=acc, scalar=-2.0, in1=z, op0=ALU.mult, op1=ALU.add))
                own(nc.vector.memset(t, 1.0))
                own.leave(3)
                gate_step(6)
                nc.vector.tensor_tensor_scan(acc, t, a, 0.0, ALU.mult, ALU.add).then_inc(cum_done, 1)
                with dve.Fori(7, KD) as k:
                    gate_step(k)
                dve.wait_ge(cum_done, 1)
                dve.wait_ge(cum_hi, 2)
                nc.vector.scalar_tensor_tensor(out=cum_k[32:32 + FOX_HEADS, :], in0=acc, scalar=-1.0,
                                               in1=cum_k[0:FOX_HEADS, :].bitcast(F32), op0=ALU.mult,
                                               op1=ALU.subtract).then_inc(cum_ready, 1)
                nc.vector.tensor_tensor(cum_q[96:96 + FOX_HEADS, :], cum_k[0:FOX_HEADS, :].bitcast(F32), acc,
                                        ALU.add).then_inc(cum_ready, 1)
                proj_step(B_FQ + KD)
                dve.wait_ge(gate_loaded, 16 * (KD + 1))
                dve.wait_ge(gate_summed, 1)
                for q in range(4):
                    last = nc.vector.tensor_tensor(gate_row[:, q * HALF:(q + 1) * HALF],
                                                   (sP if q < 2 else tP)[0:1, q % 2, :],
                                                   gate_row[:, q * HALF:(q + 1) * HALF], ALU.add)
                last.then_inc(gate_ready, 1)
                with dve.Fori(B_FQ + KD + 1, B_G) as b:
                    proj_step(b)

                dve.wait_ge(consts, 2)
                dve.wait_ge(small_loaded, 16)
                own.enter()
                own(nc.vector.tensor_scalar(neg_sinks[:], sinks[:], -1.0, None, ALU.mult))
                for e in range(2):
                    for i in range(4):
                        slope = 2.0 ** (-8.0 * (4 * e + i + 1) / SWA_HEADS)
                        own(nc.vector.tensor_scalar(s_bias[:, e, i], dist[:], -slope, None, ALU.mult))
                own.leave(9)
                def low_parts(slot, u):
                    dve.wait_ge(s_hi, u + 1)
                    top = slice(SWA_D, P)
                    nc.vector.scalar_tensor_tensor(out=sq[top], in0=sq_raw[top], scalar=SWA_D ** -0.5,
                                                   in1=sq[top].bitcast(F32), op0=ALU.mult, op1=ALU.subtract
                                                   ).then_inc(s_prep, 1)
                    low = slice(0, SWA_D)
                    nc.vector.tensor_tensor(sk_lo[:, slot], sk_raw[low], sk_hi[low, slot].bitcast(F32),
                                            ALU.subtract).then_inc(s_prep, 1)

                def unit(g, m, par, last=False):
                    u = 8 * g + 2 * m + par
                    b = u + B_G
                    dve.wait_ge(s_vt_hi, u + 1)
                    nc.vector.tensor_tensor(sv[:, par, :, 1, :], tP[:, 0, 0:P].rearrange("p (e d) -> p e d", e=2),
                                            sv[:, par, :, 0, :].bitcast(F32), ALU.subtract).then_inc(s_v, 1)
                    for e in range(2):
                        s = 2 * u + e
                        dve.wait_ge(s_qk, s + 2)
                        sc = sP[:].rearrange("p a (i k t) -> p (a i) k t", i=2, k=2)
                        for k in range(2):
                            now = k == par
                            if par == 0 and not now:
                                ins = nc.vector.scalar_tensor_tensor(
                                    out=sp_w[:, :, k, :], in0=sc[:, :, k, :], scalar=no_prev[:, ds(m, 1)],
                                    in1=s_bias[:, e, :, 0, :], op0=ALU.add, op1=ALU.add)
                            else:
                                ins = nc.vector.tensor_tensor(sp_w[:, :, k, :], sc[:, :, k, :],
                                                              s_bias[:, e, :, 1 if now else 0, :], ALU.add)
                        ins.then_inc(s_biased, 1)
                        dve.wait_ge(s_biased, s + 2)
                        own(nc.vector.tensor_reduce(neg_max[:], sp_w[:].rearrange("p i k t -> p i (k t)"),
                                                    AX.X, ALU.max, negate=True))
                        own(nc.vector.tensor_tensor(neg_max[:], neg_max[:],
                                                    neg_sinks[:, ds(8 * g + 4 * e, 4)], ALU.min))
                        nc.vector.tensor_tensor(sink_exp[:], neg_max[:], sinks[:, ds(8 * g + 4 * e, 4)],
                                                ALU.add).then_inc(s_max, 1)
                        split_lo(dve, 2 * b + (e + 1), 1 - e)
                        dve.wait_ge(s_exp, s + 1)
                        own(nc.vector.tensor_tensor(row_inv[:], row_sum[:], sink_exp[:], ALU.add))
                        nc.vector.reciprocal(row_inv[:], row_inv[:]).then_inc(s_inv, 1)
                        dve.wait_ge(s_inv, s + 1)
                        for i in range(2, 4):
                            w = sp_w[:, i].rearrange("p k t -> p (k t)")
                            ins = nc.vector.tensor_tensor(w, w, row_inv[:, i:i + 1].broadcast_to([P, 2 * P]),
                                                           ALU.mult)
                        ins.then_inc(s_norm, 1)
                        for k in range(2):
                            dve.wait_ge(s_pt_hi, 2 * s + (k + 1))
                            nc.vector.tensor_tensor(spT_lo[:, k, :], tP[:, k, :], spT_hi[:, k, :].bitcast(F32),
                                                    ALU.subtract).then_inc(s_pt, 1)
                    if not last:
                        low_parts(1 - par, u + 1)
                    for e in range(2):
                        dve.wait_ge(s_half, 2 * u + (e + 1))
                        nc.vector.tensor_tensor(so_st[:, e, :], (oP, adaP)[e][0:SWA_D, :], so_st[:, e, :], ALU.add
                                                ).then_inc(s_o, 1)

                low_parts(0, 0)
                for g in range(2):
                    with dve.Fori(0, 4 - g) as m:
                        own.enter(12 * m)
                        unit(g, m, 0)
                        unit(g, m, 1)
                    own.leave(48 - 12 * g, 4 - g)
                    if g == 0:
                        nc.vector.tensor_scalar(s_bias[:].rearrange("p e i k t -> p (e i k t)"),
                                                s_bias[:].rearrange("p e i k t -> p (e i k t)"), 1.0 / 16.0, None,
                                                ALU.mult).then_inc(s_scaled, 1)
                        dve.wait_ge(s_scaled, 1)
                own.enter()
                unit(1, 3, 0)
                unit(1, 3, 1, last=True)
                own.leave(12)

                with dve.Fori(0, FOX_HEADS) as h:
                    def q_low(i):
                        dve.wait_ge(f_q_hi, 8 * h + (i + 1))
                        nc.vector.scalar_tensor_tensor(out=fq_lo[:], in0=fq_raw[:, i % 2, :], scalar=float(P) ** -0.5,
                                                       in1=fq_hi[:].bitcast(F32), op0=ALU.mult, op1=ALU.subtract)
                        nc.vector.tensor_scalar(fcq[:], cum_q[:, i * P:(i + 1) * P].bitcast(F32),
                                                head_sel[:, ds(h, 1)], None, ALU.mult).then_inc(f_q, 1)

                    q_low(0)
                    dve.wait_ge(f_k_hi, h + 1)
                    nc.vector.tensor_tensor(fk_lo[:], fk_raw[:], fk_hi[:].bitcast(F32), ALU.subtract).then_inc(f_k, 1)
                    dve.wait_ge(f_vt_hi, h + 1)
                    for k in range(2):
                        last = nc.vector.tensor_tensor(
                            fv_lo[:, 4 * k:4 * k + 4, :].rearrange("p j t -> p (j t)"), tP[:, k, :],
                            fv_hi[:, 4 * k:4 * k + 4, :].bitcast(F32).rearrange("p j t -> p (j t)"), ALU.subtract)
                    last.then_inc(f_v, 1)
                    turned = 0
                    for i in range(8):
                        b = 4 * h + (B_M + i // 2)
                        e = i % 2
                        dve.wait_ge(f_qk, 8 * h + (i + 2))
                        nc.vector.tensor_reduce(neg_max[:, 0:1],
                                                sP[:, :, :].rearrange("p a t -> p (a t)")[:, 0:(i + 1) * P],
                                                AX.X, ALU.max, negate=True).then_inc(f_max, 1)
                        split_lo(dve, 2 * b + (e + 1), 1 - e)
                        dve.wait_ge(f_exp, 8 * h + (i + 2))
                        nc.vector.reciprocal(row_inv[:, 0:1], row_sum[:, 0:1]).then_inc(f_inv, 1)
                        for k in range(i // 4 + 1):
                            turned += 1
                            n = min(4, i + 1 - 4 * k)
                            dve.wait_ge(f_pt_hi, 12 * h + turned)
                            nc.vector.tensor_tensor(
                                fpT[:, 4 * k:4 * k + n, 1, :],
                                tP[:, k, 0:n * P].rearrange("p (j t) -> p j t", j=n),
                                fpT[:, 4 * k:4 * k + n, 0, :].bitcast(F32), ALU.subtract).then_inc(f_pt, 1)
                        if i < 7:
                            q_low(i + 1)
                        dve.wait_ge(f_half, 8 * h + (i + 1))
                        nc.vector.tensor_tensor(fo_st[:], oP[:, P:2 * P], fo_st[:], ALU.add).then_inc(f_o, 1)

            @block.tensor
            def _(pe):
                def turn(dst, src):
                    return nc.tensor.transpose(dst, src, ident[:])

                pe.wait_ge(ident_ready, 1)
                pe.wait_ge(c_loaded, 32)
                nc.tensor.transpose(projP[:, 0, 0:2 * KD], ada_rows[:], ident[0:2 * KD, 0:2 * KD]
                                    ).then_inc(ada_b_turned, 1)
                pe.wait_ge(c_one, 1)

                def ada_turn(j, slot):
                    pe.wait_ge(ada_row_ready, j + 1)
                    if isinstance(j, int) and j < 2:
                        pe.wait_ge(ada_b_ready, 1)
                    else:
                        pe.wait_ge(ada_read, j - 1)
                    late = isinstance(j, int) and j >= 8
                    if late:
                        pe.wait_ge(xt_copied, 32)
                    for s in range(2):
                        last = nc.tensor.matmul((sP if late else projP)[:, slot, s:s + 1],
                                                ada_row[:, slot, s * P:(s + 1) * P],
                                                c_sb[0:1, KD:KD + 1], start=True, stop=True)
                    last.then_inc(ada_turned, 1)

                def ada_chunk(j, slot, loads, first=False):
                    row = (adaP if slot else oP)[0:1, 0:2 * P]
                    w = ada_raw[:, slot].rearrange("p k s n -> p k (s n)")
                    pe.wait_ge(ada_loaded[2 * slot], 32 * loads)
                    if not first:
                        pe.wait_ge(ada_row_ready, j - 1)
                    for k in range(ADA_DVE, KD):
                        if k == 8:
                            last.then_inc(ada_half, 1)
                            pe.wait_ge(ada_loaded[2 * slot + 1], 32 * loads)
                        last = nc.tensor.matmul(row, c_sb[:, k:k + 1], w[:, k, :], start=(k == ADA_DVE), stop=False)
                    if not (isinstance(j, int) and j == 0):
                        ada_turn(j - 1, 1 - slot)
                    pe.wait_ge(ada_summed, j + 1)
                    nc.tensor.matmul(row, c_sb[:, KD:KD + 1], ada_acc[:, slot, :], start=False, stop=True
                                     ).then_inc(ada_done, 1)

                def x_turn(t, slot, first=False):
                    pe.wait_ge(x_normed, t + 1)
                    if not first:
                        pe.wait_ge(xt_copied, 4 * t)
                    for q in range(4):
                        for j in range(4):
                            last = turn((sP if q < 2 else tP)[:, q % 2, j * P:(j + 1) * P],
                                        x_t[:, slot, (4 * q + j) * P:(4 * q + j + 1) * P])
                        last.then_inc(x_turned, 1)

                for t in range(2):
                    ada_chunk(t, t, 1, first=True)
                    x_turn(t, t, first=(t == 0))
                with pe.Fori(1, 4) as g:
                    for slot in range(2):
                        ada_chunk(2 * g + slot, slot, g + 1)
                        x_turn(2 * g + slot, slot)

                def first_tile(k):
                    if k == 0:
                        pe.wait_ge(chunk_lo, 1)
                        pe.wait_ge(ada_read, 8)
                    pe.wait_ge(h_ready, k + 1)
                    for half in range(2):
                        for part, (w, hh) in enumerate(((w_hi, h_hi), (w_hi, h_lo), (w_lo, h_hi))):
                            last = nc.tensor.matmul(projP[:, half, :], w[:, 0, k * P:(k + 1) * P],
                                                    hh[:, k, half * HALF:(half + 1) * HALF],
                                                    start=(k == 0 and part == 0), stop=False)
                    return last

                for j in range(8, KD):
                    ada_chunk(j, j % 2, j // 2 + 1)
                    if j >= 10:
                        first_tile(j - 10)
                ada_turn(KD - 1, 1)
                first_tile(6)
                first_tile(7).then_inc(chunk_used, 1)

                def proj(b, e, lo=0, hi=MMS):
                    for n in range(lo, hi):
                        half, k, part = n // 24, n // 3 % 8, n % 3
                        if n == 0:
                            pe.wait_ge(chunk_lo, 2 * b + (e + 1))
                        if n % 24 == 0 and e == 0 and not isinstance(b, int):
                            pe.wait_ge(proj_copied, 2 * b + (half - 1))
                        if isinstance(b, int) and half == 0 and part == 0:
                            pe.wait_ge(h_ready, 8 * e + k + 1)
                        w, hh = ((w_hi, h_hi), (w_hi, h_lo), (w_lo, h_hi))[part]
                        last = nc.tensor.matmul(projP[:, half, :], w[:, e, k * P:(k + 1) * P],
                                                hh[:, 8 * e + k, half * HALF:(half + 1) * HALF],
                                                start=(e == 0 and n % 24 == 0), stop=(e == 1 and n % 24 == 23))
                        if e == 1 and n == 23:
                            last.then_inc(half0_done, 1)
                        if n == MMS - 1:
                            last.then_inc(chunk_used, 1)

                proj(0, 1)
                with pe.Fori(B_SQ, B_FQ + KD) as b:
                    proj(b, 0)
                    proj(b, 1)
                pe.wait_ge(consts, 1)
                pe.wait_ge(gate_added, KD + 1)
                for q in range(4):
                    last = nc.tensor.matmul((sP if q < 2 else tP)[0:1, q % 2, :], ones[:],
                                            gate_acc[:, q * HALF:(q + 1) * HALF], start=True, stop=True)
                last.then_inc(gate_summed, 1)
                with pe.Fori(B_FQ + KD, B_G) as b:
                    proj(b, 0)
                    proj(b, 1)

                with pe.Fori(0, 2) as g:
                    with pe.Fori(0, 4) as m:
                        for par in range(2):
                            u = 8 * g + 2 * m + par
                            b = u + B_G

                            def scores(e):
                                pe.wait_ge(s_prep, 2 * u + 3)
                                pe.wait_ge(gate_ready, 1)
                                pe.wait_ge(s_biased, 2 * u + e + 1)
                                for i in range(4):
                                    dst = sP[:, i // 2, 2 * P * (i % 2):2 * P * (i % 2 + 1)]
                                    nc.tensor.matmul(dst, sq[:, 4 * e + i, :], sk_hi[:, :, e, :],
                                                     start=True, stop=False)
                                    last = nc.tensor.matmul(dst, sq[0:SWA_D, 4 * e + i, :], sk_lo[:, :, e, :],
                                                            start=False, stop=True)
                                last.then_inc(s_qk, 1)

                            def turn_weights(e):
                                pe.wait_ge(s_norm, 4 * u + 2 * (e + 1))
                                if e == 0:
                                    pe.wait_ge(s_v, u + 1)
                                for k in range(2):
                                    for i in range(4):
                                        last = turn(tP[:, k, i * P:(i + 1) * P], sp_w[:, i, k, :])
                                    last.then_inc(s_turned, 1)

                            def weigh(e):
                                pe.wait_ge(s_pt, 4 * u + 2 * (e + 1) + 1)
                                if e == 0:
                                    pe.wait_ge(s_o, 2 * u + 1)
                                out_e = (oP, adaP)[e]
                                nc.tensor.matmul(out_e[:, :], sv[:, 0, e, :, :], spT_hi[:, 0, :],
                                                 start=True, stop=False)
                                for k in range(2):
                                    nc.tensor.matmul(out_e[0:SWA_D, :], sv[:, k, e, 0, :], spT_lo[:, k, :],
                                                     start=False, stop=False)
                                nc.tensor.matmul(out_e[:, :], sv[:, 1, e, :, :], spT_hi[:, 1, :],
                                                 start=False, stop=True).then_inc(s_pv, 1)

                            pe.wait_ge(s_loaded[par], 80 * (4 * g + m + 1))
                            pe.wait_ge(s_pt, 4 * u + 1)
                            turn(tP[:, 0, 0:P], sv_raw[:, par, :]).then_inc(s_vt, 1)
                            proj(b, 0, 0, 6)
                            scores(0)
                            proj(b, 0, 6, MMS)
                            proj(b, 1, 0, 3)
                            turn_weights(0)
                            scores(1)
                            proj(b, 1, 3, 15)
                            weigh(0)
                            proj(b, 1, 15, 38)
                            turn_weights(1)
                            proj(b, 1, 38, MMS)
                            weigh(1)

                with pe.Fori(0, FOX_HEADS) as h:
                    pe.wait_ge(f_kv_loaded, 32 * h + 32)
                    pe.wait_ge(s_pt, 64 + 1)
                    pe.wait_ge(f_pt, 12 * h + 1)
                    for j in range(8):
                        last = turn(tP[:, j // 4, (j % 4) * P:(j % 4 + 1) * P], fv_raw[:, j * P:(j + 1) * P])
                    last.then_inc(f_vt, 1)
                    turned = 0
                    for i in range(8):
                        b = 4 * h + (B_M + i // 2)
                        e = i % 2
                        first = 18 if i == 0 else 0
                        proj(b, e, 0, first)
                        pe.wait_ge(f_q, 8 * h + (i + 3))
                        if i == 0:
                            pe.wait_ge(f_k, h + 2)
                            pe.wait_ge(s_biased, 32 + 1)
                        pe.wait_ge(f_exp, 8 * h + i + 1)
                        for a in range(i // 4 + 1):
                            c0, c1 = a * HALF, min((a + 1) * HALF, (i + 1) * P)
                            dst = sP[:, a, 0:c1 - c0]
                            nc.tensor.matmul(dst, fcq[:], cum_k[:, c0:c1], start=True, stop=False)
                            if a == i // 4:
                                nc.tensor.matmul(sP[:, a, (i % 4) * P:(i % 4 + 1) * P], ident_r[:], mask_r[:],
                                                 start=False, stop=False)
                            for part, (q, k) in enumerate(((fq_hi, fk_hi), (fq_hi, fk_lo), (fq_lo, fk_hi))):
                                last = nc.tensor.matmul(dst, q[:], k[:, c0:c1], start=False, stop=(part == 2))
                        last.then_inc(f_qk, 1)
                        proj(b, e, first, 36)
                        pe.wait_ge(f_norm, 8 * h + (i + 1))
                        if i == 0:
                            pe.wait_ge(f_v, h + 1)
                        for j in range(i + 1):
                            last = turn(tP[:, j // 4, (j % 4) * P:(j % 4 + 1) * P], fp_w[:, j, :])
                            if j == 3 or j == i:
                                last.then_inc(f_turned, 1)
                        turned += i // 4 + 1
                        proj(b, e, 36, MMS)
                        pe.wait_ge(f_pt, 12 * h + turned + 1)
                        pe.wait_ge(f_o, 8 * h + i + 1)
                        for j in range(i + 1):
                            nc.tensor.matmul(oP[:, 0:2 * P], fv_hi[:, j, :], fpT[:, j, :, :],
                                             start=(j == 0), stop=False)
                            last = nc.tensor.matmul(oP[:, 0:P], fv_lo[:, j, :], fpT[:, j, 0, :],
                                                    start=False, stop=(j == i))
                        last.then_inc(f_pv, 1)

        with ExitStack() as last_part:
            def sb2(name, shape, dt=F32):
                return sb(name, shape, dt, last_part)

            yP = last_part.enter_context(nc.psum_tensor("yP", [P, 4, HALF], F32))
            zP = last_part.enter_context(nc.psum_tensor("zP", [P, 4, HALF], F32))
            with ExitStack() as late:
                lng_all = sb("lng_all", [P, D], F32, late)
                lnb_all = sb("lnb_all", [P, D], F32, late)
            og_hi = sb2("og_hi", [P, KD, HALF], F32R)
            og_lo = sb2("og_lo", [P, KD, HALF], F32R)
            mg_hi = sb2("mg_hi", [P, KD, HALF], F32R)
            mg_lo = sb2("mg_lo", [P, KD, HALF], F32R)
            z = sb2("z", [P, 4, D])
            aux = sb2("aux", [P, 2, HALF])
            sg = sb2("sg", [P, 2, HALF])
            z_tmp = sb2("z_tmp", [P, 4, HALF])
            ta, tb_ = z_tmp[:, 0, :], z_tmp[:, 1, :]
            gate_sl = sb2("gate_sl", [P, HALF])
            lng = sb2("lng", [P, HALF])
            lnb = sb2("lnb", [P, HALF])
            z_bn = sb2("z_bn", [P, 4, 4, 6])
            z_mv = sb2("z_mv", [P, 4, 2])
            z_sm = sb2("z_sm", [P, 6, 4])

            og_sig = sem("og_sig")
            og_t = sem("og_t")
            og_g = sem("og_g")
            og_hi_ready = sem("og_hi_ready")
            og_ready = sem("og_ready")
            aux_loaded = sem("aux_loaded")
            sg_ready = sem("sg_ready")
            y_read = sem("y_read")
            t_ready = sem("t_ready")
            mg_hi_ready = sem("mg_hi_ready")
            mg_ready = sem("mg_ready")
            gate_slice_loaded = sem("gate_slice_loaded")
            z_x_loaded = sem("z_x_loaded")
            z_product_done = sem("z_product_done")
            z_read = sem("z_read")
            z_added = sem("z_added")
            z_summed = sem("z_summed")
            z_var = sem("z_var")
            z_std = sem("z_std")
            ln_ready = sem("ln_ready")
            ln_loaded = sem("ln_loaded")
            ln_done = sem("ln_done")
            out_stored = sem("out_stored")
            dve_step_2 = sem("dve_step_2")
            pool_step_2 = sem("pool_step_2")
            ln_all_loaded = sem("ln_all_loaded")
            z_normed = sem("z_normed")
            ln_part = sem("ln_part")
            dve_out = sem("dve_out")
            pool_out = sem("pool_out")
            last_stored = sem("last_stored")

            block = last_part.enter_context(nc.Block())

            @block.sync
            def _(sp):
                def aux_in(nb, H):
                    for w in range(2):
                        sp.dma_start(aux[:, w, :], proj_d[ds(nb + (B_M + KD * w), 1), :, H * HALF:(H + 1) * HALF]
                                     .rearrange("a p t -> p (a t)")).then_inc(aux_loaded, 16)

                sp.wait_ge(f_stored, 1024 + 1)
                load_og(sp, 3)
                load_chunk(sp, TAIL + 2, 0, wbf_v[:, :, 0:P])
                load_og(sp, 4)
                for s in range(2):
                    sp.wait_ge(proj_stored[s], 16 * BLOCKS)
                aux_in(0, 0)
                load_chunk(sp, TAIL + 3, 1, wbf_v[:, :, P:2 * P])
                sp.wait_ge(sg_ready, 1)
                aux_in(1, 0)
                for H in range(2):
                    with sp.Fori(2 - 2 * H, KD) as nb:
                        load_chunk(sp, 2 * nb + (TAIL + 64 * H), 0, wbf_v[:, :, ds(nb * P, P)])
                        load_chunk(sp, 2 * nb + (TAIL + 64 * H + 1), 1, wbs_v[:, :, ds(nb * P, P)])
                        sp.wait_ge(sg_ready, nb + 2 * KD * H)
                        if H == 1:
                            sp.wait_ge(og_ready, 2 * KD)
                        aux_in(nb, H)
                    with sp.Fori(0, 4) as cg:
                        for kk in range(8):
                            load_chunk(sp, 8 * cg + (TAIL + 64 * H + 32 + kk), kk % 2,
                                       w_out_v[:, 2 * kk:2 * kk + 2, ds(cg * HALF, HALF)])
                            if kk == 1:
                                sp.wait_ge(*((og_ready, KD) if H == 0 else (out_stored, 64)))
                                cols = ds(cg * HALF, HALF)
                                sp.dma_start(z[:, :, cols], x2[:, 4 * H:4 * H + 4, cols]).then_inc(z_x_loaded, 16)
                            if kk == 5 and H == 1:
                                sp.wait_ge(chunk_used, TAIL + 96)
                                for src, dst in ((ln_g, lng_all), (ln_b, lnb_all)):
                                    sp.dma_start(dst[:, ds(cg * HALF, HALF)],
                                                 src[0:1, ds(cg * HALF, HALF)].broadcast_to([P, HALF])
                                                 ).then_inc(ln_all_loaded, 16)
                            if kk == 3:
                                sp.wait_ge(z_read, 4 * cg + (16 * H + 4))
                                sp.dma_start(gate_sl[:], gate_d[0:1, ds(cg * HALF, HALF)].broadcast_to([P, HALF])
                                             ).then_inc(gate_slice_loaded, 16)
                            if H == 0 and kk % 2 == 0:
                                k = 4 * cg + kk // 2
                                sp.wait_ge(sg_ready, KD)
                                sp.wait_ge(og_ready, k + KD)
                                for w, src, base in ((0, o_d, 0), (1, proj_d, B_G)):
                                    sp.dma_start(aux[:, w, :], src[ds(k + base, 1), :, HALF:SEQ]
                                                 .rearrange("a p t -> p (a t)")).then_inc(aux_loaded, 16)
                for tb in range(4):
                    for done, cols in ((dve_out, slice(0, DVE_COLS)), (pool_out, slice(DVE_COLS, D))):
                        sp.wait_ge(done, tb + 1)
                        sp.dma_start(out2[:, 4 + tb, cols], z[:, tb, cols]).then_inc(last_stored, 16)
                sp.wait_ge(last_stored, 128)

            @block.gpsimd
            def _(pool):
                for n in range(KD):
                    pool.wait_ge(og_sig, n + 1)
                    nc.gpsimd.tensor_tensor(go_in[:, n, 0, :], go_in[:, n, 0, :], z_tmp[:, n % 2, :], ALU.mult
                                            ).then_inc(og_g, 1)
                pool.wait_ge(ln_ready, 1)
                for cs in range(4):
                    cols = slice(cs * HALF, (cs + 1) * HALF)
                    if cs:
                        pool.wait_ge(ln_done, 4 * cs)
                    pool.dma_start(lng[:], ln_g[0:1, cols].broadcast_to([P, HALF])).then_inc(ln_loaded, 16)
                    pool.dma_start(lnb[:], ln_b[0:1, cols].broadcast_to([P, HALF])).then_inc(ln_loaded, 16)
                    for tb in range(4):
                        nc.gpsimd.tensor_scalar(z[:, tb, cols], z[:, tb, cols], z_mv[:, tb, 0:1],
                                                z_sm[:, 3, tb:tb + 1], ALU.subtract, ALU.mult
                                                ).then_inc(pool_step_2, 1)
                    pool.wait_ge(ln_loaded, 32 * cs + 32)
                    for tb in range(4):
                        pool.wait_ge(pool_step_2, 8 * cs + 1 + tb)
                        nc.gpsimd.tensor_tensor(z[:, tb, cols], z[:, tb, cols], lng[:], ALU.mult
                                                ).then_inc(pool_step_2, 1)
                    for tb in range(4):
                        pool.wait_ge(pool_step_2, 8 * cs + 5 + tb)
                        nc.gpsimd.tensor_tensor(z[:, tb, cols], z[:, tb, cols], lnb[:], ALU.add
                                                ).then_inc(ln_done, 1)
                    pool.wait_ge(ln_done, 4 * cs + 4)
                    pool.dma_start(out2[:, 0:4, cols], z[:, :, cols]).then_inc(out_stored, 16)
                pool.wait_ge(ln_all_loaded, 128)
                for tb in range(4):
                    cols = slice(DVE_COLS, D)
                    pool.wait_ge(z_normed, tb + 1)
                    nc.gpsimd.tensor_tensor(z[:, tb, cols], z[:, tb, cols], lng_all[:, cols], ALU.mult
                                            ).then_inc(pool_step_2, 1)
                    pool.wait_ge(pool_step_2, 33 + tb)
                    nc.gpsimd.tensor_tensor(z[:, tb, cols], z[:, tb, cols], lnb_all[:, cols], ALU.add
                                            ).then_inc(pool_out, 1)
                pool.wait_ge(out_stored, 64)

            @block.scalar
            def _(act):
                def root_and_back(H):
                    act.wait_ge(z_var, H + 1)
                    nc.scalar.activation(z_sm[:, 1, :], z_sm[:, 0, :], ACT.Sqrt).then_inc(z_std, 1)
                    if H == 0:
                        nc.scalar.activation(z_sm[:, 5, :], z_sm[:, 0, :], ACT.Sigmoid)

                def og_high(n):
                    k = OG_ORDER[n]
                    act.wait_ge(og_t, n + 1)
                    nc.scalar.copy(og_hi[:, k, :], go_in[:, n, 1, :]).then_inc(og_hi_ready, 1)

                def merge_gates(nb, H):
                    act.wait_ge(aux_loaded, 32 * nb + (1024 * H + 32))
                    nc.scalar.activation(sg[:], aux[:], ACT.Sigmoid).then_inc(sg_ready, 1)

                def merged_high(nb, H):
                    act.wait_ge(t_ready, nb + (KD * H + 1))
                    nc.scalar.copy(mg_hi[:, ds(nb, 1), :].rearrange("p a t -> p (a t)"), ta
                                   ).then_inc(mg_hi_ready, 1)

                for n in range(KD):
                    for q, (n0, _) in enumerate(OG_GROUPS):
                        if n == n0:
                            act.wait_ge(og_in[q], 32)
                    if n >= 2:
                        act.wait_ge(og_g, n - 1)
                    nc.scalar.activation(z_tmp[:, n % 2, :], go_in[:, n, 0, :], ACT.Sigmoid).then_inc(og_sig, 1)
                    if n == 3:
                        split_hi(act, TAIL + 1, 1, TAIL // 2 + 1)
                    elif n:
                        og_high(n - 1 if n < 3 else n - 2)
                    if n == 11:
                        split_hi(act, TAIL + 2, 0, TAIL // 2 + 2)
                    if n == 13:
                        split_hi(act, TAIL + 3, 1, TAIL // 2 + 2)
                    if n == 14:
                        merge_gates(0, 0)
                og_high(KD - 2)
                og_high(KD - 1)
                split_hi(act, TAIL + 4, 0, TAIL // 2 + 3)
                split_hi(act, TAIL + 5, 1, TAIL // 2 + 3)
                merged_high(0, 0)
                merge_gates(1, 0)
                merged_high(1, 0)

                for H in range(2):
                    def branch_step(nb):
                        c0 = 2 * nb + (TAIL + 64 * H)
                        if isinstance(nb, int) and nb == 1:
                            root_and_back(0)
                        merge_gates(nb, H)
                        for e in range(2):
                            split_hi(act, c0 + (2 + e), e, nb + (TAIL // 2 + 32 * H + 2))
                        merged_high(nb, H)

                    if H == 1:
                        branch_step(0)
                        branch_step(1)
                    with act.Fori(2, KD) as nb:
                        branch_step(nb)

                    def out_step(cg, last):
                        for kk in range(8):
                            c = 8 * cg + (TAIL + 64 * H + 32 + kk)
                            if H == 0 and kk % 2 == 0:
                                k = 4 * cg + kk // 2
                                act.wait_ge(aux_loaded, 32 * k + (32 * KD + 32))
                                nc.scalar.activation(sg[:, 0, :], aux[:, 1, :], ACT.Sigmoid).then_inc(sg_ready, 1)
                                act.wait_ge(og_t, k + (KD + 1))
                                nc.scalar.copy(og_hi[:, ds(k, 1), :].rearrange("p a t -> p (a t)"), aux[:, 0, :]
                                               ).then_inc(og_hi_ready, 1)
                            if not (last and kk >= 6):
                                split_hi(act, c + 2, kk % 2, 4 * cg + (TAIL // 2 + 32 * H + 18 + kk // 2))

                    with act.Fori(0, 4 - H) as cg:
                        out_step(cg, False)
                    if H == 1:
                        out_step(3, True)
                root_and_back(1)
                act.wait_ge(ln_ready, 2)
                for tb in range(4):
                    cols = slice(DVE_COLS, D)
                    nc.scalar.activation(z[:, tb, cols], z[:, tb, cols], ACT.Identity, bias=z_sm[:, 4, tb:tb + 1],
                                         scale=z_sm[:, 3, tb:tb + 1]).then_inc(z_normed, 1)

            @block.vector
            def _(dve):
                own = Steps(dve, dve_step_2)

                def og_low(n):
                    k = OG_ORDER[n]
                    dve.wait_ge(og_hi_ready, n + 1)
                    nc.vector.tensor_tensor(og_lo[:, k, :], go_in[:, n, 1, :], og_hi[:, k, :].bitcast(F32),
                                            ALU.subtract).then_inc(og_ready, 1)

                def y_weigh(nb, H, br, bank):
                    c0 = 2 * nb + (TAIL + 64 * H)
                    dve.wait_ge(sg_ready, nb + (2 * KD * H + 1))
                    if br == 0 and not (isinstance(nb, int) and nb == 0 and H == 0):
                        dve.wait_ge(mg_ready, nb + KD * H)
                    dve.wait_ge(chunk_used, c0 + (br + 1))
                    nc.vector.tensor_tensor((ta, tb_)[br], yP[:, 2 * bank + br, :], sg[:, br, :], ALU.mult
                                            ).then_inc(y_read, 1)

                def merge(nb, H):
                    dve.wait_ge(y_read, 2 * nb + (2 * KD * H + 2))
                    nc.vector.tensor_tensor(ta, ta, tb_, ALU.add).then_inc(t_ready, 1)
                    if not (isinstance(nb, int) and nb == 1 and H == 0):
                        split_lo(dve, 2 * nb + (TAIL + 64 * H + (5 if isinstance(nb, int) and H == 0 else 3)), 1)
                    dve.wait_ge(mg_hi_ready, nb + (KD * H + 1))
                    nc.vector.tensor_tensor(mg_lo[:, ds(nb, 1), :].rearrange("p a t -> p (a t)"), ta,
                                            mg_hi[:, ds(nb, 1), :].bitcast(F32).rearrange("p a t -> p (a t)"),
                                            ALU.subtract).then_inc(mg_ready, 1)

                for n in range(KD):
                    for q, (n0, _) in enumerate(OG_GROUPS):
                        if n == n0:
                            dve.wait_ge(og_in[q], 32)
                    dve.wait_ge(og_g, n + 1)
                    nc.vector.tensor_tensor(go_in[:, n, 1, :], go_in[:, n, 1, :], go_in[:, n, 0, :], ALU.mult
                                            ).then_inc(og_t, 1)
                    if n == 3:
                        split_lo(dve, TAIL + 1, 1)
                    elif n:
                        og_low(n - 1 if n < 3 else n - 2)
                    if n == 11:
                        split_lo(dve, TAIL + 2, 0)
                    if n == 13:
                        split_lo(dve, TAIL + 3, 1)
                og_low(KD - 2)
                og_low(KD - 1)
                split_lo(dve, TAIL + 4, 0)
                dve.wait_ge(chunk_used, TAIL + 4)
                y_weigh(0, 0, 0, 0)
                y_weigh(0, 0, 1, 0)
                merge(0, 0)
                y_weigh(1, 0, 0, 1)
                y_weigh(1, 0, 1, 1)
                merge(1, 0)

                def z_rest(cg, H):
                    for tb in range(4):
                        nc.vector.bn_stats(z_bn[:, tb, ds(cg, 1), :].rearrange("p a s -> p (a s)"),
                                           z[:, tb, ds(cg * HALF, HALF)]).then_inc(z_added, 1)

                def norm_scalars(H):
                    dve.wait_ge(z_added, 16 * (H + 1))
                    for tb in range(4):
                        last = nc.vector.bn_aggr(z_mv[:, tb, :], z_bn[:, tb, :, :].rearrange("p c s -> p (c s)"))
                    own(last)
                    nc.vector.tensor_scalar(z_sm[:, 0, :], z_mv[:, :, 1], LN_EPS, None, ALU.add).then_inc(z_var, 1)
                    dve.wait_ge(z_std, H + 1)
                    r, w = z_sm[:, 2, :], z_sm[:, 3, :]
                    own(nc.vector.reciprocal(r, z_sm[:, 1, :]))
                    own(nc.vector.tensor_tensor(w, r, r, ALU.mult))
                    own(nc.vector.tensor_tensor(w, w, z_sm[:, 0, :], ALU.mult))
                    own(nc.vector.tensor_scalar(w, w, -0.5, 1.5, ALU.mult, ALU.add))
                    own(nc.vector.tensor_tensor(w, w, r, ALU.mult))
                    nc.vector.scalar_tensor_tensor(out=z_sm[:, 4, :], in0=w, scalar=-1.0, in1=z_mv[:, :, 0],
                                                   op0=ALU.mult, op1=ALU.mult).then_inc(ln_ready, 1)

                for H in range(2):
                    def branch_step(nb, bank):
                        c0 = 2 * nb + (TAIL + 64 * H)
                        if isinstance(nb, int) and nb == 0:
                            z_rest(3, 0)
                        if isinstance(nb, int) and nb == 1:
                            own.enter()
                            norm_scalars(0)
                            own.leave(6)
                        y_weigh(nb, H, 0, bank)
                        split_lo(dve, c0 + 2, 0)
                        y_weigh(nb, H, 1, bank)
                        merge(nb, H)

                    if H == 1:
                        branch_step(0, 0)
                        branch_step(1, 1)
                    with dve.Fori(1, KD // 2) as pair:
                        for bank in range(2):
                            branch_step(2 * pair + bank, bank)

                    def out_step(cg, last=False):
                        for kk in range(8):
                            c = 8 * cg + (TAIL + 64 * H + 32 + kk)
                            if kk == 1 and not (isinstance(cg, int) and cg == 0):
                                z_rest(cg - 1, H)
                            if H == 0 and kk % 2 == 0:
                                k = 4 * cg + kk // 2
                                dve.wait_ge(sg_ready, k + (KD + 1))
                                nc.vector.tensor_tensor(tb_, aux[:, 1, :], sg[:, 0, :], ALU.mult).then_inc(og_g, 1)
                                dve.wait_ge(og_g, k + (KD + 1))
                                nc.vector.tensor_tensor(aux[:, 0, :], aux[:, 0, :], tb_, ALU.mult).then_inc(og_t, 1)
                                dve.wait_ge(og_hi_ready, k + (KD + 1))
                                nc.vector.tensor_tensor(
                                    og_lo[:, ds(k, 1), :].rearrange("p a t -> p (a t)"), aux[:, 0, :],
                                    og_hi[:, ds(k, 1), :].bitcast(F32).rearrange("p a t -> p (a t)"),
                                    ALU.subtract).then_inc(og_ready, 1)
                            if kk < 6 or (kk == 6 and not last):
                                split_lo(dve, c + 2, kk % 2)
                        cols = ds(cg * HALF, HALF)
                        dve.wait_ge(gate_slice_loaded, 16 * cg + (64 * H + 16))
                        dve.wait_ge(z_x_loaded, 16 * cg + (64 * H + 16))
                        for tb in range(4):
                            if tb < 3:
                                dve.wait_ge(z_product_done, 3 * cg + (12 * H + tb + 1))
                            else:
                                dve.wait_ge(chunk_used, 8 * cg + (TAIL + 64 * H + 40))
                            nc.vector.tensor_tensor(z_tmp[:, tb, :], zP[:, tb, :], gate_sl[:], ALU.mult
                                                    ).then_inc(z_read, 1)
                            dve.wait_ge(z_read, 4 * cg + (16 * H + 5 + tb))
                            nc.vector.scalar_tensor_tensor(out=z[:, tb, cols], in0=z[:, tb, cols], scalar=ALPHA,
                                                           in1=z_tmp[:, tb, :], op0=ALU.mult, op1=ALU.add
                                                           ).then_inc(z_summed, 1)
                        dve.wait_ge(z_summed, 4 * cg + (16 * H + 4))
                        if not last:
                            split_lo(dve, 8 * cg + (TAIL + 64 * H + 41), 1)

                    out_step(0)
                    with dve.Fori(1, 4 - H) as cg:
                        out_step(cg)
                    if H == 1:
                        out_step(3, last=True)
                own.enter()
                z_rest(3, 1)
                norm_scalars(1)
                own.leave(6)
                dve.wait_ge(ln_ready, 2)
                dve.wait_ge(ln_all_loaded, 128)
                cols = slice(0, DVE_COLS)
                for tb in range(4):
                    nc.vector.scalar_tensor_tensor(out=z[:, tb, cols], in0=z[:, tb, cols], scalar=z_mv[:, tb, 0:1],
                                                   in1=lng_all[:, cols], op0=ALU.subtract, op1=ALU.mult
                                                   ).then_inc(ln_part, 1)
                    dve.wait_ge(ln_part, tb + 1)
                    nc.vector.scalar_tensor_tensor(out=z[:, tb, cols], in0=z[:, tb, cols],
                                                   scalar=z_sm[:, 3, tb:tb + 1], in1=lnb_all[:, cols],
                                                   op0=ALU.mult, op1=ALU.add).then_inc(dve_out, 1)

            @block.tensor
            def _(pe):
                pe.sem_inc(z_read, 4)

                def y_product(br, bank, slot, k):
                    for part, (w, o) in enumerate(((w_hi, og_hi), (w_hi, og_lo), (w_lo, og_hi))):
                        last = nc.tensor.matmul(yP[:, 2 * bank + br, :], w[:, slot, k * P:(k + 1) * P],
                                                o[:, 8 * br + k, :],
                                                start=(k == 0 and part == 0), stop=(k == 7 and part == 2))
                    return last

                for turn_of, br in enumerate((1, 0)):
                    for n in range(12):
                        for nb in range(2):
                            k = n - 4 * nb
                            if 0 <= k < 8:
                                if k == 0:
                                    pe.wait_ge(chunk_lo, TAIL + 1 + 2 * turn_of + nb)
                                if nb == 0:
                                    pe.wait_ge(og_ready, 8 * turn_of + k + 1)
                                last = y_product(br, nb, nb, k)
                                if k == 7:
                                    last.then_inc(chunk_used, 1)

                def branch(H, nb, bank):
                    for br in range(2):
                        pe.wait_ge(chunk_lo, 2 * nb + (TAIL + 64 * H + 1 + br))
                        pe.wait_ge(y_read, 2 * nb + (2 * KD * H - 3 + br))
                        for k in range(8):
                            last = y_product(br, bank, br, k)
                        last.then_inc(chunk_used, 1)

                for H in range(2):
                    if H == 1:
                        pe.wait_ge(og_ready, 2 * KD)
                    with pe.Fori(1 - H, KD // 2) as pair:
                        for bank in range(2):
                            branch(H, 2 * pair + bank, bank)
                    with pe.Fori(0, 4) as cg:
                        for kk in range(8):
                            c = 8 * cg + (TAIL + 64 * H + 32 + kk)
                            pe.wait_ge(mg_ready, KD * H + 2 * kk + 2)
                            pe.wait_ge(chunk_lo, c + 1)
                            for tb in range(4):
                                if kk == 0:
                                    pe.wait_ge(z_read, 4 * cg + (16 * H + tb + 1))
                                for k2 in range(2):
                                    for part, (m, w) in enumerate(((mg_hi, w_hi), (mg_hi, w_lo), (mg_lo, w_hi))):
                                        last = nc.tensor.matmul(
                                            zP[:, tb, :], m[:, 2 * kk + k2, tb * P:(tb + 1) * P],
                                            w[:, kk % 2, k2 * HALF:(k2 + 1) * HALF],
                                            start=(kk == 0 and k2 == 0 and part == 0),
                                            stop=(kk == 7 and k2 == 1 and part == 2))
                                if kk == 7 and tb < 3:
                                    last.then_inc(z_product_done, 1)
                            last.then_inc(chunk_used, 1)


_INS = ['x', 'c', 'w_ada', 'b_ada', 'w_in', 'b_f', 'attn_sinks', 'w_br_fox', 'w_br_swa', 'w_out', 'ln_g', 'ln_b']


def kernel(**inputs):
    import numpy as _np
    import concourse.bacc as _bacc
    from concourse import mybir as _mybir
    from concourse.bass_utils import run_bass_kernel_spmd as _run

    nc = _bacc.Bacc("TRN2", target_bir_lowering=False, num_devices=1)
    arrays, args = {}, []
    for name in _INS:
        a = _np.ascontiguousarray(inputs[name])
        arrays[f"in_{name}_dram"] = a
        args.append(nc.dram_tensor(f"in_{name}_dram", a.shape, _mybir.dt.from_np(a.dtype), kind="ExternalInput").ap())
    out = nc.dram_tensor("out_dram", inputs["x"].shape, F32, kind="ExternalOutput").ap()
    build(nc, *args, out)
    r = _run(nc, [arrays], core_ids=[0])
    return r.results[0]["out_dram"]
```
